# Optimizing a Trainium2 kernel written in Bass

```python
import jax, jax.numpy as jnp
from jax import lax
import numpy as np

D_MODEL = 1024
BATCH = 1
SEQ = 128
DEPTH = 2
DEC_BATCH = 1
DEC_SEQ = 128
PAST_LEN = 128

GRID_W = 64
N_HEADS = 4
QK_NOPE = 128
QK_ROPE = 64
V_DIM = 128
Q_LORA = 384
KV_LORA = 256
POOL_W = 512
POOL_GROUPS = 4
POOL_WINDOWS = (2, 4, 8, 16)
POOL_CH = POOL_W // POOL_GROUPS
D_MIX = N_HEADS * V_DIM + POOL_W
D_IN = Q_LORA + KV_LORA + QK_ROPE + POOL_W
D_FF = 2816
N_EXPERTS = 8
TOP_K = 2
D_FF_EXPERT = 3584
N_DENSE = (DEPTH + 1) // 2
N_MOE = DEPTH // 2
ROPE_BASE = 10000.0
EPS = 1e-6
Q_BLOCK = 128

kernel_name = "hymba_mla_pool_prefix_dit_step"

def rmsnorm(x, g):
    xf = x.astype(jnp.float32)
    y = xf * lax.rsqrt(jnp.mean(xf * xf, axis=-1, keepdims=True) + EPS)
    return (y * g.astype(jnp.float32)).astype(x.dtype)

def ada_params(cond, w_ada, b_ada):
    m = jax.nn.silu(cond) @ w_ada + b_ada
    return jnp.split(m[..., None, :], 6, axis=-1)

def modulate(h, shift, scale):
    return h * (1.0 + scale) + shift

def rope_2d_tables(n_tok):
    t = jnp.arange(n_tok)
    rows = (t // GRID_W).astype(jnp.float32)
    cols = (t % GRID_W).astype(jnp.float32)
    half = QK_ROPE // 2
    freqs = ROPE_BASE ** (-jnp.arange(0, half, 2, dtype=jnp.float32) / half)
    ang_r = rows[:, None] * freqs
    ang_c = cols[:, None] * freqs
    ang = jnp.concatenate([ang_r, ang_r, ang_c, ang_c], axis=-1)
    return jnp.cos(ang), jnp.sin(ang)

def rotate_half_axial(x):
    xr = x.reshape(x.shape[:-1] + (2, 2, QK_ROPE // 4))
    return jnp.concatenate([-xr[..., 1:, :], xr[..., :1, :]], axis=-2).reshape(x.shape)

def apply_rope(x, cos, sin):
    xf = x.astype(jnp.float32)
    return (xf * cos + rotate_half_axial(xf) * sin).astype(x.dtype)

def mixer_inputs(h, w_in, q_norm_g, kv_norm_g, w_uq):
    b, s, _ = h.shape
    proj = h @ w_in
    cq, ckv_raw, kpe, u = jnp.split(proj, [Q_LORA, Q_LORA + KV_LORA, Q_LORA + KV_LORA + QK_ROPE], axis=-1)
    q = (rmsnorm(cq, q_norm_g) @ w_uq).reshape(b, s, N_HEADS, QK_NOPE + QK_ROPE)
    ckv = rmsnorm(ckv_raw, kv_norm_g)
    return q[..., :QK_NOPE], q[..., QK_NOPE:], ckv, kpe, u

def expand_kv(ckv, w_ukv):
    b, s, _ = ckv.shape
    kv = (ckv @ w_ukv).reshape(b, s, N_HEADS, QK_NOPE + V_DIM)
    return kv[..., :QK_NOPE], kv[..., QK_NOPE:]

def mla_attend(q_nope, q_pe, k_nope, k_pe, v):
    b, sq = q_nope.shape[:2]
    nb = sq // Q_BLOCK
    scale = (QK_NOPE + QK_ROPE) ** -0.5

    def block(qs):
        qn, qp = qs
        s = (jnp.einsum('bqhd,bkhd->bhqk', qn, k_nope, preferred_element_type=jnp.float32)
             + jnp.einsum('bqhr,bkr->bhqk', qp, k_pe, preferred_element_type=jnp.float32))
        p = jax.nn.softmax(s * scale, axis=-1).astype(v.dtype)
        return jnp.einsum('bhqk,bkhd->bqhd', p, v)

    def to_blocks(t):
        return t.reshape((b, nb, Q_BLOCK) + t.shape[2:]).swapaxes(0, 1)

    o = lax.map(block, (to_blocks(q_nope), to_blocks(q_pe)))
    return o.swapaxes(0, 1).reshape(b, sq, N_HEADS * V_DIM)

def multiscale_pool(u):
    b, s, _ = u.shape
    ug = u.reshape(b, s, POOL_GROUPS, POOL_CH).astype(jnp.float32)
    cs = jnp.concatenate([jnp.zeros((b, 1, POOL_GROUPS, POOL_CH), jnp.float32), jnp.cumsum(ug, axis=1)], axis=1)
    t = jnp.arange(s)
    outs = []
    for g, w in enumerate(POOL_WINDOWS):
        lo = jnp.maximum(t - w // 2, 0)
        hi = jnp.minimum(t + w // 2, s)
        cnt = (hi - lo).astype(jnp.float32)[None, :, None]
        outs.append((cs[:, hi, g] - cs[:, lo, g]) / cnt - ug[:, :, g])
    return jnp.stack(outs, axis=2).astype(u.dtype)

def mixer_output(attn, u, w_pool, pool_scale, w_out):
    b, s = attn.shape[:2]
    pooled = jnp.einsum('bsgc,gcd->bsgd', multiscale_pool(u), w_pool).reshape(b, s, POOL_W) * pool_scale
    return jnp.concatenate([attn, pooled], axis=-1) @ w_out

def swiglu(h, w_gate, w_up, w_down):
    return (jax.nn.silu(h @ w_gate) * (h @ w_up)) @ w_down

def moe_swiglu(h, w_router, we_gate, we_up, we_down):
    b, s, d = h.shape
    x = h.reshape(b * s, d)
    logits = (x @ w_router).astype(jnp.float32)
    top_v, top_i = lax.top_k(logits, TOP_K)
    top_w = jax.nn.softmax(top_v, axis=-1)
    gates = jnp.sum(jax.nn.one_hot(top_i, N_EXPERTS, dtype=jnp.float32) * top_w[..., None], axis=1).astype(h.dtype)
    y = jnp.zeros_like(x)
    for e in range(N_EXPERTS):
        y = y + gates[:, e:e + 1] * swiglu(x, we_gate[e], we_up[e], we_down[e])
    return y.reshape(b, s, d)

def channel_mixer(l, h, ffn_w_gate, ffn_w_up, ffn_w_down, moe_w_router, moe_w_gate, moe_w_up, moe_w_down):
    j = l // 2
    if l % 2 == 0:
        return swiglu(h, ffn_w_gate[j], ffn_w_up[j], ffn_w_down[j])
    return moe_swiglu(h, moe_w_router[j], moe_w_gate[j], moe_w_up[j], moe_w_down[j])

def setup_inputs(seed: int = 0) -> dict:
    key = jax.random.key(seed)
    ks = iter(jax.random.split(key, 32))
    f32 = jnp.float32

    def nrm(shape, fan_in, mult=1.0):
        return jax.random.normal(next(ks), shape, f32) * (mult * fan_in ** -0.5)

    def gain(shape):
        return 1.0 + 0.02 * jax.random.normal(next(ks), shape, f32)

    return {
        "x_prompt": jax.random.normal(next(ks), (BATCH, SEQ, D_MODEL), f32),
        "x_sample": jax.random.normal(next(ks), (DEC_BATCH, DEC_SEQ, D_MODEL), f32),
        "c": jax.random.normal(next(ks), (DEC_BATCH, D_MODEL), f32),
        "cache_ckv": jax.random.normal(next(ks), (DEC_BATCH, DEPTH, PAST_LEN, KV_LORA), f32),
        "cache_kpe": jax.random.normal(next(ks), (DEC_BATCH, DEPTH, PAST_LEN, QK_ROPE), f32),
        "c_ctx": jax.random.normal(next(ks), (D_MODEL,), f32),
        "norm1_g": gain((DEPTH, D_MODEL)),
        "norm2_g": gain((DEPTH, D_MODEL)),
        "w_ada": nrm((DEPTH, D_MODEL, 6 * D_MODEL), D_MODEL, 0.5),
        "b_ada": 0.02 * jax.random.normal(next(ks), (DEPTH, 6 * D_MODEL), f32),
        "w_in": nrm((DEPTH, D_MODEL, D_IN), D_MODEL),
        "q_norm_g": gain((DEPTH, Q_LORA)),
        "kv_norm_g": gain((DEPTH, KV_LORA)),
        "w_uq": nrm((DEPTH, Q_LORA, N_HEADS * (QK_NOPE + QK_ROPE)), Q_LORA),
        "w_ukv": nrm((DEPTH, KV_LORA, N_HEADS * (QK_NOPE + V_DIM)), KV_LORA),
        "w_pool": nrm((DEPTH, POOL_GROUPS, POOL_CH, POOL_CH), POOL_CH),
        "pool_scale": gain((DEPTH, POOL_W)),
        "w_out": nrm((DEPTH, D_MIX, D_MODEL), D_MIX),
        "ffn_w_gate": nrm((N_DENSE, D_MODEL, D_FF), D_MODEL),
        "ffn_w_up": nrm((N_DENSE, D_MODEL, D_FF), D_MODEL),
        "ffn_w_down": nrm((N_DENSE, D_FF, D_MODEL), D_FF),
        "moe_w_router": nrm((N_MOE, D_MODEL, N_EXPERTS), D_MODEL),
        "moe_w_gate": nrm((N_MOE, N_EXPERTS, D_MODEL, D_FF_EXPERT), D_MODEL),
        "moe_w_up": nrm((N_MOE, N_EXPERTS, D_MODEL, D_FF_EXPERT), D_MODEL),
        "moe_w_down": nrm((N_MOE, N_EXPERTS, D_FF_EXPERT, D_MODEL), D_FF_EXPERT),
        "final_norm_g": gain((D_MODEL,)),
    }

def reference(x_prompt, x_sample, c, cache_ckv, cache_kpe, c_ctx,
              norm1_g, norm2_g, w_ada, b_ada, w_in, q_norm_g, kv_norm_g, w_uq, w_ukv,
              w_pool, pool_scale, w_out, ffn_w_gate, ffn_w_up, ffn_w_down,
              moe_w_router, moe_w_gate, moe_w_up, moe_w_down, final_norm_g):
    n_lat = x_sample.shape[1]
    cos, sin = rope_2d_tables(n_lat)
    xc, xl = x_prompt, x_sample
    new_ckv, new_kpe = [], []
    for l in range(DEPTH):
        sh1, sc1, g1, sh2, sc2, g2 = ada_params(c_ctx, w_ada[l], b_ada[l])
        h = modulate(rmsnorm(xc, norm1_g[l]), sh1, sc1)
        q_nope, q_pe, ckv, kpe, u = mixer_inputs(h, w_in[l], q_norm_g[l], kv_norm_g[l], w_uq[l])
        k_nope, v = expand_kv(ckv, w_ukv[l])
        attn = mla_attend(q_nope, q_pe, k_nope, kpe, v)
        xc = xc + g1 * mixer_output(attn, u, w_pool[l], pool_scale[l], w_out[l])
        h = modulate(rmsnorm(xc, norm2_g[l]), sh2, sc2)
        xc = xc + g2 * channel_mixer(l, h, ffn_w_gate, ffn_w_up, ffn_w_down,
                                     moe_w_router, moe_w_gate, moe_w_up, moe_w_down)
        new_ckv.append(ckv)
        new_kpe.append(kpe)

        sh1, sc1, g1, sh2, sc2, g2 = ada_params(c, w_ada[l], b_ada[l])
        h = modulate(rmsnorm(xl, norm1_g[l]), sh1, sc1)
        q_nope, q_pe, ckv_lat, kpe_lat, u = mixer_inputs(h, w_in[l], q_norm_g[l], kv_norm_g[l], w_uq[l])
        q_pe = apply_rope(q_pe, cos[:, None, :], sin[:, None, :])
        kpe_lat = apply_rope(kpe_lat, cos, sin)
        ckv_all = jnp.concatenate([ckv_lat, cache_ckv[:, l].astype(ckv_lat.dtype)], axis=1)
        kpe_all = jnp.concatenate([kpe_lat, cache_kpe[:, l].astype(kpe_lat.dtype)], axis=1)
        k_nope, v = expand_kv(ckv_all, w_ukv[l])
        attn = mla_attend(q_nope, q_pe, k_nope, kpe_all, v)
        xl = xl + g1 * mixer_output(attn, u, w_pool[l], pool_scale[l], w_out[l])
        h = modulate(rmsnorm(xl, norm2_g[l]), sh2, sc2)
        xl = xl + g2 * channel_mixer(l, h, ffn_w_gate, ffn_w_up, ffn_w_down,
                                     moe_w_router, moe_w_gate, moe_w_up, moe_w_down)

    y_prompt = rmsnorm(xc, final_norm_g)
    y_sample = rmsnorm(xl, final_norm_g)
    new_ckv_arr = jnp.stack(new_ckv, axis=1)
    new_kpe_arr = jnp.stack(new_kpe, axis=1)
    return (y_prompt, y_sample, new_ckv_arr, new_kpe_arr)


_drawn_inputs = setup_inputs


def setup_inputs(seed=0):
    import zlib

    import numpy as np

    out = dict(_drawn_inputs(seed))
    spreads = {}
    factors = {'cache_kpe': 3.466,
     'norm1_g': 2.874,
     'norm2_g': 3.145,
     'q_norm_g': 7.433,
     'kv_norm_g': 2.89,
     'pool_scale': 5.742,
     'final_norm_g': 2.796}
    for name, (base, spread) in spreads.items():
        noise = np.random.default_rng([zlib.crc32(name.encode()), seed]).standard_normal(out[name].shape)
        drawn = base * np.exp(spread * noise) if base else spread * noise
        out[name] = __import__('jax').numpy.asarray(drawn.astype(out[name].dtype))
    for name, factor in factors.items():
        out[name] = (out[name] * factor).astype(out[name].dtype)
    return out
```

```python
import numpy as np
import concourse.bass as bass
from concourse import mybir
from contextlib import ExitStack

D = 1024
T = 128
DEPTH = 2
PAST = 128
GRID_W = 64
NH = 4
NOPE = 128
ROPE = 64
VD = 128
QL = 384
KL = 256
POOL_WINDOWS = (2, 4, 8, 16)
NG = len(POOL_WINDOWS)
POOL_W = 512
FF = 2816
NE = 8
FE = 3584
EPS = 1e-6
ROPE_BASE = 10000.0

KD = D // 128
KQ = QL // 128
KK = KL // 128
N2 = 2 * T
ADA = 6 * D
ADA_COLS = 512
ADA_ITEMS = ADA // ADA_COLS
FC = 256
FSTEPS = FF // FC
EC = 512
ESTEPS = FE // EC
SLOTS = 7
SLOT = 4096
E_ITEMS = 3 * ESTEPS
assert E_ITEMS % SLOTS == 0
PAD = 8
TP = T + 2 * PAD

C_ID, C_ROT, C_COS, C_SIN, C_TRI, C_IOTA, C_CNT = (128 * i for i in range(7))
C_COLS = C_CNT + NG * 128

V_BADA, V_N1, V_N2 = 0, 96, 112
V_FIN, V_PS, V_QG, V_KG, V_CC, V_C = (128 + i for i in (0, 8, 16, 22, 26, 34))
V_B_ROWS = 42


def constants():
    out = np.zeros((128, C_COLS), np.float32)
    out[:, C_ID:C_ID + 128] = np.eye(128)
    rot = np.zeros((128, 128), np.float32)
    q = ROPE // 4
    for base in range(0, 128, 2 * q):
        for i in range(q):
            rot[base + i, base + q + i] = -1.0
            rot[base + q + i, base + i] = 1.0
    out[:, C_ROT:C_ROT + 128] = rot.T
    t = np.arange(T)
    half = ROPE // 2
    freqs = (ROPE_BASE ** (-np.arange(0, half, 2, dtype=np.float32) / half)).astype(np.float32)
    ar = (t // GRID_W).astype(np.float32)[:, None] * freqs
    ac = (t % GRID_W).astype(np.float32)[:, None] * freqs
    ang = np.concatenate([ar, ar, ac, ac], axis=-1).T
    out[:, C_COS:C_COS + 128] = np.tile(np.cos(ang), (2, 1))
    out[:, C_SIN:C_SIN + 128] = np.tile(np.sin(ang), (2, 1))
    out[:, C_TRI:C_TRI + 128] = np.triu(np.ones((128, 128)), 1)
    out[:, C_IOTA:C_IOTA + 128] = np.arange(128)
    for g, w in enumerate(POOL_WINDOWS):
        cnt = np.minimum(t + w // 2, T) - np.maximum(t - w // 2, 0)
        out[:, C_CNT + g * 128:C_CNT + (g + 1) * 128] = (1.0 / cnt).astype(np.float32)
    return out


STREAM = []
for _l in range(DEPTH):
    STREAM += [("ada", _l, j) for j in range(ADA_ITEMS)]
for _l in range(DEPTH):
    STREAM += [("in", _l, j) for j in range(3)] + [("uq", _l, 0), ("ukv", _l, 0)]
    STREAM += [("out", _l, j) for j in range(2)]
    if _l == 0:
        for _c in range(FSTEPS):
            STREAM += [("gu", _l, _c)]
            if _c:
                STREAM += [("down", _l, _c - 1)]
        STREAM += [("down", _l, FSTEPS - 1)]
    while len(STREAM) % SLOTS and _l == DEPTH - 1:
        STREAM += [("none", _l, 0)]
ITEM = {x: n for n, x in enumerate(STREAM)}
MOE0 = len(STREAM)
IN_COLS = ((0, QL), (QL, QL + KL + ROPE), (QL + KL + ROPE, QL + KL + ROPE + POOL_W))

_count = [0] * SLOTS
ARRIVED = []
for _n, _x in enumerate(STREAM):
    _count[_n % SLOTS] += {"gu": 32, "none": 0}.get(_x[0], 16)
    ARRIVED.append(_count[_n % SLOTS])
MOE_ARRIVED = list(_count)


def item_g(c):
    return 0 if c == 0 else 3 * c - 1


def item_u(c):
    return item_g(c) + 1


def item_d(c):
    return 3 * c + 4 if c < ESTEPS - 1 else E_ITEMS - 1


def program(nc, ins, consts, y_prompt, y_sample, new_ckv, new_kpe):
    f32 = mybir.dt.float32
    i32 = mybir.dt.int32
    u32 = mybir.dt.uint32
    ALU = mybir.AluOpType
    ACT = mybir.ActivationFunctionType
    AX = mybir.AxisListType
    SCALE = float(NOPE + ROPE) ** -0.5

    ctx = ExitStack()
    with ctx:
        def sb(name, *shape, dt=f32):
            return ctx.enter_context(nc.sbuf_tensor(name, list(shape), dt))

        def sem(name):
            return ctx.enter_context(nc.semaphore(name))

        ring = sb("ring", 128, SLOTS, SLOT)
        cst = sb("cst", 128, C_COLS)
        xT = sb("xT", 128, KD, N2)
        hT = sb("hT", 128, KD, N2)
        sq = sb("sq", 128, KD, N2)
        ones = sb("ones", 128, 128)
        vecT = sb("vecT", 128, 128 + V_B_ROWS)
        silu_c = sb("silu_c", 128, KD, 2)
        mod = sb("mod", 128, DEPTH, 48, 2)
        amod = sb("amod", 128, DEPTH, 2, KD, 2)
        rs = sb("rs", 128, N2)
        wpool = sb("wpool", 128, DEPTH * NG, 128)
        wr = sb("wr", 128, KD, NE)
        kv_out = sb("kv_out", 128, DEPTH, KL + ROPE)
        hid = sb("hid", 128, 3, 2, 512)
        sg, hm = hid[:, 0], hid[:, 1]
        hTm = hid[:, 2].rearrange("p a (r t) -> p a r t", r=4)
        mrow = hid[0:2, 2]
        cache = sb("cache", 128, DEPTH, KL + 2 * ROPE)
        stat = sb("stat", 128, 64)
        rt8 = sb("rt8", 128, 2, 8)
        rti = sb("rti", 128, 2, 8, dt=u32)
        oh = sb("oh", 128, 4, 2, NE)
        over = sb("over", 128, 1, dt=i32)

        arena_words = 9344
        arena = sb("arena", 128, arena_words)
        at = [0]

        def cut(*shape):
            n = int(np.prod(shape))
            a = arena[:, at[0]:at[0] + n]
            at[0] += n
            assert at[0] <= arena_words, at[0]
            if len(shape) == 1:
                return a
            names = "abcd"[:len(shape)]
            return a.rearrange(f"p ({' '.join(names)}) -> p {' '.join(names)}", **dict(zip(names, shape)))

        cqT = cut(KQ, N2)
        ckvT = cut(KK, T + T + PAST)
        kpe_raw = cut(N2)
        kpeT = cut(T + T + PAST)
        sqqk = cut(KQ + KK, N2)
        rqk = cut(2, N2)
        qT = cut(NH, N2)
        qpe = cut(2, N2)
        qq = arena[:, at[0] - (NH + 2) * N2:at[0]]
        rope_t = cut(2, T)
        hidden = hid[:, :, :, :].rearrange("p a b n -> p (a b n)")
        kT = hidden[:, 0:NH * 3 * 128].rearrange("p (h t) -> p h t", h=NH)
        v = hidden[:, NH * 3 * 128:2 * NH * 3 * 128].rearrange("p (i n) -> p i n", i=3)
        p = qq.rearrange("p (h t) -> p h t", h=NH)
        pT = kT
        up = cut(NG, 2, TP)
        win = cut(2, NG * 2 * TP)
        mixT = hT
        poolT = sq[:, 0:NG, :]
        at[0] = 0
        h2 = cut(2, D)
        P = cut(NE + 1, 2, 128)
        PgT = cut(NE + 1, 2, 128)
        acc = sq
        Y = cut(D)
        xg = cut(KD, 128)
        Pg = cut(2, 128)
        xin = ring[:, SLOTS - 1, 0:2 * D].rearrange("p (b d) -> p b d", b=2)
        vrow = ring[:, SLOTS - 1, 2 * D:2 * D + 256].rearrange("p (a d) -> p a d", a=2)

        ps = ctx.enter_context(nc.psum_tensor("ps", [128, 8, 512], f32))

        in_slot = [sem(f"in_slot{i}") for i in range(SLOTS)]
        items_used = sem("items_used")
        small_in = sem("small_in")
        x_in = sem("x_in")
        cache_in = sem("cache_in")
        ones_set = sem("ones_set")
        pads_set = sem("pads_set")
        vecT_done, vecT_ready = sem("vecT_done"), sem("vecT_ready")
        xT_done, x_ready = sem("xT_done"), sem("x_ready")
        silu_ready = sem("silu_ready")
        ada_done, mrow_ready, modT_done, mod_ready = (sem(x) for x in ("ada_done", "mrow_ready", "modT_done", "mod_ready"))
        amod_ready = sem("amod_ready")
        sq_ready, ss_done, ms_ready, rt_ready, h_ready = (sem(x) for x in ("sq_ready", "ss_done", "ms_ready", "rt_ready", "h_ready"))
        cacheT_done, cacheT_ready = sem("cacheT_done"), sem("cacheT_ready")
        u_ready, sqqk_ready, ssqk_done, kpe_rot_done = (sem(x) for x in ("u_ready", "sqqk_ready", "ssqk_done", "kpe_rot_done"))
        msqk_ready, rtqk_ready, qkvn_ready, kpe_ready = (sem(x) for x in ("msqk_ready", "rtqk_ready", "qkvn_ready", "kpe_ready"))
        qraw_ready, qpe_rot_done, qpe_ready = (sem(x) for x in ("qraw_ready", "qpe_rot_done", "qpe_ready"))
        k_ready, v_ready, s_done, nmx_ready, p_ready, pn_ready = (sem(x) for x in ("k_ready", "v_ready", "s_done", "nmx_ready", "p_ready", "pn_ready"))
        pT_done, pT_low_ready, pT_high_ready, o_done, o_ready = (sem(x) for x in ("pT_done", "pT_low_ready", "pT_high_ready", "o_done", "o_ready"))
        pool_ready, pooled_done, pooled_ready = (sem(x) for x in ("pool_ready", "pooled_done", "pooled_ready"))
        kv_outT_done, kv_out_ready, stored = (sem(x) for x in ("kv_outT_done", "kv_out_ready", "stored"))
        fsg_ready, fh_ready = sem("fsg_ready"), sem("fh_ready")
        h2T_done, h2_ready, logits_done, sel_ready, rank_done, P_ready = (sem(x) for x in ("h2T_done", "h2_ready", "logits_done", "sel_ready", "rank_done", "P_ready"))
        e1_ready, top2_ready = sem("e1_ready"), sem("top2_ready")
        Pg_ready, PgT_done, PgT_ready = sem("Pg_ready"), sem("PgT_done"), sem("PgT_ready")
        moe_zero = sem("moe_zero")
        over_ready, shift_ready = sem("over_ready"), sem("shift_ready")
        esg_ready, eh_ready, ehT_done, ehT_ready = (sem(x) for x in ("esg_ready", "eh_ready", "ehT_done", "ehT_ready"))
        Y_ready, cmb_done, acc_ready = sem("Y_ready"), sem("cmb_done"), sem("acc_ready")
        gat_done, xg_ready = sem("gat_done"), sem("xg_ready")
        outT_done, y_ready = sem("outT_done"), sem("y_ready")
        dve_step, act_step, pool_step = sem("dve_step"), sem("act_step"), sem("pool_step")

        ident = cst[:, C_ID:C_ID + 128]

        class Steps:

            def __init__(self, eng, semaphore):
                self.eng, self.sem, self.n, self.base = eng, semaphore, 0, 0

            def __call__(self, instruction):
                self.n += 1
                instruction.then_inc(self.sem, 1)
                self.eng.wait_ge(self.sem, self.base + self.n)

        block = ctx.enter_context(nc.Block())

        @block.sync
        def _(sp):
            w_ada = ins["w_ada"].rearrange("l (k p) n -> l p k n", p=128)
            w_in = ins["w_in"].rearrange("l (k p) n -> l p k n", p=128)
            w_uq = ins["w_uq"].rearrange("l (k p) n -> l p k n", p=128)
            w_ukv = ins["w_ukv"].rearrange("l (k p) n -> l p k n", p=128)
            w_out = ins["w_out"].rearrange("l (k p) n -> l p k n", p=128)
            f_gate = ins["ffn_w_gate"].rearrange("l (k p) n -> l p k n", p=128)
            f_up = ins["ffn_w_up"].rearrange("l (k p) n -> l p k n", p=128)
            f_down = ins["ffn_w_down"].rearrange("l (k p) n -> l p k n", p=128)
            e_gate = ins["moe_w_gate"].rearrange("l e (k p) n -> (l e) p k n", p=128)
            e_up = ins["moe_w_up"].rearrange("l e (k p) n -> (l e) p k n", p=128)
            e_down = ins["moe_w_down"].rearrange("l e (c p r) n -> (l e) c p r n", p=128, r=EC // 128)

            def slot(n, k, width):
                return ring[:, n % SLOTS, 0:k * width].rearrange("p (k n) -> p k n", k=k)

            sp.dma_start(cst[:, :], consts).then_inc(small_in, 16)
            for n, (kind, l, j) in enumerate(STREAM):
                if kind == "none":
                    continue
                if n >= SLOTS:
                    sp.wait_ge(items_used, n - SLOTS + 1)
                elif n == SLOTS - 1:
                    sp.wait_ge(xT_done, 1)
                    sp.wait_ge(vecT_done, 1)
                s = in_slot[n % SLOTS]
                if kind == "ada":
                    sp.dma_start(slot(n, KD, ADA_COLS), w_ada[l, :, :, j * ADA_COLS:(j + 1) * ADA_COLS]).then_inc(s, 16)
                elif kind == "in":
                    a, b = IN_COLS[j]
                    sp.dma_start(slot(n, KD, b - a), w_in[l, :, :, a:b]).then_inc(s, 16)
                elif kind == "uq":
                    sp.dma_start(slot(n, KQ, NH * (NOPE + ROPE)), w_uq[l]).then_inc(s, 16)
                elif kind == "ukv":
                    sp.dma_start(slot(n, KK, NH * (NOPE + VD)), w_ukv[l]).then_inc(s, 16)
                elif kind == "out":
                    sp.dma_start(slot(n, KD, 512), w_out[l, :, :, j * 512:(j + 1) * 512]).then_inc(s, 16)
                elif kind == "gu":
                    gu = ring[:, n % SLOTS, :].rearrange("p (w k n) -> p w k n", w=2, k=KD)
                    for w, src in enumerate((f_gate, f_up)):
                        sp.dma_start(gu[:, w], src[l // 2, :, :, j * FC:(j + 1) * FC]).then_inc(s, 16)
                else:
                    k = FC // 128
                    sp.dma_start(slot(n, k, D), f_down[l // 2, :, j * k:(j + 1) * k, :]).then_inc(s, 16)

            def experts(rnd):
                with sp.Fori(0, NE) as e:
                    k = e + NE * rnd
                    for c in range(ESTEPS):
                        todo = [(item_g(c), e_gate, "g"), (item_u(c), e_up, "u")]
                        if c:
                            todo += [(item_d(c - 1), e_down, "d")]
                        if c == ESTEPS - 1:
                            todo += [(item_d(c), e_down, "d")]
                        for i, src, what in todo:
                            sp.wait_ge(items_used, k * E_ITEMS + (MOE0 + i - SLOTS + 1))
                            if what == "d":
                                cc = c - 1 if i == item_d(c - 1) else c
                                sp.dma_start(slot(i, EC // 128, D), src[bass.ds(e, 1), cc].rearrange("o p r n -> (o p) r n")).then_inc(in_slot[i % SLOTS], 16)
                            else:
                                sp.dma_start(slot(i, KD, EC), src[bass.ds(e, 1), :, :, c * EC:(c + 1) * EC].rearrange("o p k n -> (o p) k n")).then_inc(in_slot[i % SLOTS], 16)

            experts(0)
            sp.wait_ge(over_ready, 1)
            more = sp.value_load(over[0:1, 0:1])
            with sp.If(more > 0):
                experts(1)
            sp.wait_ge(y_ready, 4)
            ysb = sq[:, :, :].rearrange("p k t -> p (k t)")
            sp.dma_start(y_prompt, ysb[:, 0:D]).then_inc(stored, 16)
            sp.dma_start(y_sample, ysb[:, D:2 * D]).then_inc(stored, 16)
            sp.wait_ge(stored, 16 * (2 + 2 * DEPTH))

        @block.gpsimd
        def _(pool):
            step = Steps(pool, pool_step)
            nc.gpsimd.memset(ones[:, :], 1.0).then_inc(ones_set, 1)
            nc.gpsimd.memset(up, 0.0).then_inc(pads_set, 1)
            wa = win[:, 0, :].rearrange("p (g b t) -> p g b t", g=NG, b=2)
            wb = win[:, 1, :].rearrange("p (g b t) -> p g b t", g=NG, b=2)
            for l in range(DEPTH):
                pool.wait_ge(u_ready, l + 1)
                src = up
                for g, w in enumerate(POOL_WINDOWS):
                    dst = (wa, wb)[g % 2]
                    n = TP - w + 1
                    for gg in range(g, NG):
                        last = nc.gpsimd.tensor_tensor(dst[:, gg, :, 0:n], src[:, gg, :, 0:n], src[:, gg, :, w // 2:w // 2 + n], ALU.add)
                    step(last)
                    cnt = cst[:, C_CNT + g * 128:C_CNT + (g + 1) * 128]
                    for b in range(2):
                        last = nc.gpsimd.tensor_tensor(poolT[:, g, b * T:(b + 1) * T], dst[:, g, b, PAD - w // 2:PAD - w // 2 + T], cnt, ALU.mult)
                    step(last)
                    for b in range(2):
                        last = nc.gpsimd.tensor_tensor(poolT[:, g, b * T:(b + 1) * T], poolT[:, g, b * T:(b + 1) * T], up[:, g, b, PAD:PAD + T], ALU.subtract)
                    if g == NG - 1:
                        last.then_inc(pool_ready, 1)
                    else:
                        step(last)
                    src = dst

        @block.scalar
        def _(act):
            step = Steps(act, act_step)
            A = nc.scalar.activation
            act.dma_start(xin[:, 0, :], ins["x_prompt"].rearrange("b t d -> (b t) d")).then_inc(x_in, 16)
            act.dma_start(xin[:, 1, :], ins["x_sample"].rearrange("b t d -> (b t) d")).then_inc(x_in, 16)

            def rows(r, a):
                src = a.rearrange("(r p) -> r p", p=128) if len(a.shape) == 1 else a.rearrange("l (r p) -> (l r) p", p=128)
                act.dma_start(vrow[r % 128:r % 128 + src.shape[0], r // 128, :], src).then_inc(small_in, 16)

            for r, name in ((V_BADA, "b_ada"), (V_N1, "norm1_g"), (V_N2, "norm2_g"), (V_FIN, "final_norm_g"),
                            (V_PS, "pool_scale"), (V_QG, "q_norm_g"), (V_KG, "kv_norm_g"), (V_CC, "c_ctx"), (V_C, "c")):
                rows(r, ins[name])
            for l in range(DEPTH):
                act.dma_start(cache[:, l, 0:KL], ins["cache_ckv"][0, l]).then_inc(cache_in, 16)
                for i in range(2):
                    act.dma_start(cache[:, l, KL + i * ROPE:KL + (i + 1) * ROPE], ins["cache_kpe"][0, l]).then_inc(cache_in, 16)
            act.dma_start(wpool[:, :, :], ins["w_pool"].rearrange("l g c d -> c (l g) d")).then_inc(cache_in, 16)
            act.dma_start(wr[:, :, :], ins["moe_w_router"].rearrange("l (k p) n -> p (l k) n", p=128)).then_inc(cache_in, 16)

            act.wait_ge(vecT_ready, 1)
            A(silu_c[:, :, :].rearrange("p k c -> p c k"), vecT[:, V_CC:V_CC + 2 * KD].rearrange("p (c k) -> p c k", c=2), ACT.Silu).then_inc(silu_ready, 1)
            for l in range(DEPTH):
                for j in range(ADA_ITEMS):
                    n = l * ADA_ITEMS + j
                    act.wait_ge(items_used, ITEM["ada", l, j] + 1)
                    if n >= 2:
                        act.wait_ge(modT_done, n - 1)
                    A(mrow[:, n % 2, :], ps[0:2, 6 + n % 2, :], ACT.Copy).then_inc(mrow_ready, 1)

            def norm(t):
                act.wait_ge(x_ready, t + 1)
                if t:
                    act.wait_ge(ss_done, t)
                if t % 2 == 0 and t:
                    pass
                A(sq[:, :, :], xT[:, :, :], ACT.Square).then_inc(sq_ready, 1)
                act.wait_ge(ms_ready, t + 1)
                A(rs[:, :], rs[:, :], ACT.Sqrt).then_inc(rt_ready, 1)

            def mixer(l):
                norm(2 * l)
                act.wait_ge(items_used, ITEM["in", l, 1] + 1)
                A(cqT[:, 0:2, :], ps[:, 1, :], ACT.Copy)
                A(cqT[:, 2, :], ps[:, 2, 0:N2], ACT.Copy)
                A(kpe_raw, ps[:, 2, N2:2 * N2], ACT.Copy)
                last = A(rqk, ps[:, 3, :], ACT.Copy)
                step(last)
                A(sqqk[:, 0:KQ, :], cqT, ACT.Square)
                A(sqqk[:, KQ:, :], rqk, ACT.Square).then_inc(sqqk_ready, 1)
                act.wait_ge(msqk_ready, l + 1)
                A(sqqk[:, 0:2, :], sqqk[:, 2:4, :], ACT.Sqrt).then_inc(rtqk_ready, 1)
                act.wait_ge(items_used, ITEM["uq", l, 0] + 1)
                A(qT[:, 0:2, :], ps[:, 4, :], ACT.Copy)
                A(qT[:, 2:4, :], ps[:, 5, :], ACT.Copy)
                A(qpe, ps[:, 3, :], ACT.Copy).then_inc(qraw_ready, 1)
                act.wait_ge(items_used, ITEM["ukv", l, 0] + 1)
                for h, b in enumerate((4, 5, 3, 1)):
                    last = A(kT[:, h, :], ps[:, b, 0:3 * 128], ACT.Copy)
                last.then_inc(k_ready, 1)
                act.wait_ge(nmx_ready, l + 1)
                for h in range(NH):
                    for b, (a, z) in enumerate(((0, T), (T, 3 * T))):
                        last = A(p[:, h, a:z], ps[:, 4 + h, a:z], ACT.Exp, bias=stat[:, 8 + 2 * h + b:9 + 2 * h + b],
                                 scale=SCALE, accum_out=stat[:, 16 + 2 * h + b:17 + 2 * h + b])
                last.then_inc(p_ready, 1)
                act.wait_ge(pT_done, l + 1)
                A(pT[:, 0, :], ps[:, 1, 0:3 * 128], ACT.Copy)
                A(pT[:, 1, :], ps[:, 2, 0:3 * 128], ACT.Copy).then_inc(pT_low_ready, 1)
                act.wait_ge(o_done, l + 1)
                A(mixT[:, 0:2, :], ps[:, 4, :], ACT.Copy)
                A(mixT[:, 2:4, :], ps[:, 5, :], ACT.Copy).then_inc(o_ready, 1)
                act.wait_ge(kv_outT_done, l + 1)
                A(kv_out[:, l, :], ps[:, 4, 0:KL + ROPE], ACT.Copy).then_inc(kv_out_ready, 1)
                act.wait_ge(kv_out_ready, l + 1)
                act.dma_start(new_ckv[0, l], kv_out[:, l, 0:KL]).then_inc(stored, 16)
                act.dma_start(new_kpe[0, l], kv_out[:, l, KL:KL + ROPE]).then_inc(stored, 16)
                norm(2 * l + 1)

            mixer(0)
            for c in range(FSTEPS):
                act.wait_ge(items_used, ITEM["gu", 0, c] + 1)
                if c >= 2:
                    act.wait_ge(fh_ready, c - 1)
                A(sg[:, c % 2, :], ps[:, 0, :], ACT.Silu).then_inc(fsg_ready, 1)
            mixer(1)

            act.wait_ge(h2T_done, 1)
            A(h2[:, 0, 0:512], ps[:, 0, :], ACT.Copy)
            A(h2[:, 0, 512:1024], ps[:, 1, :], ACT.Copy)
            A(h2[:, 1, 0:512], ps[:, 2, :], ACT.Copy)
            A(h2[:, 1, 512:1024], ps[:, 3, :], ACT.Copy).then_inc(h2_ready, 1)
            act.wait_ge(top2_ready, 1)
            A(stat[:, 26:28], stat[:, 24:26], ACT.Exp).then_inc(e1_ready, 1)
            act.wait_ge(e1_ready, 1)
            A(stat[:, 28:29], stat[:, 0:1], ACT.Copy).then_inc(esg_ready, 1)
            A(stat[:, 29:30], stat[:, 0:1], ACT.Copy).then_inc(ehT_ready, 1)
            A(stat[:, 30:31], stat[:, 0:1], ACT.Copy).then_inc(Y_ready, 1)

            def experts(rnd):
                with act.Fori(0, NE) as e:
                    k = e + NE * rnd
                    for c in range(ESTEPS + 1):
                        if c < ESTEPS:
                            act.wait_ge(items_used, k * E_ITEMS + (MOE0 + item_g(c) + 1))
                            act.wait_ge(eh_ready, k * ESTEPS + (c + 1))
                            A(sg[:, c % 2, :], ps[:, 0, :], ACT.Silu).then_inc(esg_ready, 1)
                        if c:
                            act.wait_ge(ehT_done, k * ESTEPS + c)
                            A(hTm[:, (c - 1) % 2, :, :], ps[:, 2, :], ACT.Copy).then_inc(ehT_ready, 1)
                    act.wait_ge(items_used, k * E_ITEMS + (MOE0 + E_ITEMS))
                    act.wait_ge(cmb_done, k * 4 + (4 + 4 * rnd))
                    A(Y[:, 0:512], ps[:, 4, :], ACT.Copy)
                    A(Y[:, 512:1024], ps[:, 5, :], ACT.Copy).then_inc(Y_ready, 1)

            experts(0)
            act.wait_ge(over_ready, 1)
            more = act.value_load(over[0:1, 0:1])
            with act.If(more > 0):
                experts(1)
            norm(2 * DEPTH)
            ysb = sq[:, :, :].rearrange("p k t -> p (k t)")
            act.wait_ge(outT_done, 1)
            for b in range(4):
                last = A(ysb[:, b * 512:(b + 1) * 512], ps[:, 1 + b, :], ACT.Copy)
                last.then_inc(y_ready, 1)

        @block.vector
        def _(dve):
            step = Steps(dve, dve_step)
            V = nc.vector
            dve.wait_ge(vecT_done, 1)
            V.tensor_copy(vecT[:, :], ps[:, 0, 0:128 + V_B_ROWS]).then_inc(vecT_ready, 1)
            dve.wait_ge(xT_done, 1)
            for b in range(2):
                for q in range(2):
                    last = V.tensor_copy(xT[:, 4 * q:4 * q + 4, b * T:(b + 1) * T], ps[:, 1 + 2 * b + q, :].rearrange("p (k t) -> p k t", k=4))
            last.then_inc(x_ready, 1)
            dve.wait_ge(vecT_ready, 1)
            for l in range(DEPTH):
                for j in range(ADA_ITEMS):
                    dve.wait_ge(modT_done, l * ADA_ITEMS + j + 1)
                    bias = vecT[:, V_BADA + 48 * l + 4 * j:V_BADA + 48 * l + 4 * j + 4].rearrange("p (m o) -> p m o", o=1).to_broadcast([128, 4, 2])
                    V.tensor_tensor(mod[:, l, 4 * j:4 * j + 4, :], ps[:, 5, 0:8].rearrange("p (m c) -> p m c", c=2), bias, ALU.add).then_inc(mod_ready, 1)
                dve.wait_ge(mod_ready, (l + 1) * ADA_ITEMS)
                for i, (sc, vg) in enumerate(((8, V_N1), (32, V_N2))):
                    g = vecT[:, vg + KD * l:vg + KD * (l + 1)].rearrange("p (m o) -> p m o", o=1).to_broadcast([128, KD, 2])
                    last = V.scalar_tensor_tensor(amod[:, l, i, :, :], mod[:, l, sc:sc + KD, :], 1.0, g, ALU.add, ALU.mult)
                last.then_inc(amod_ready, 1)

            def norm(t):
                dve.wait_ge(ss_done, t + 1)
                V.tensor_scalar(rs[:, :], ps[:, 0, 0:N2], 1.0 / D, EPS, ALU.mult, ALU.add).then_inc(ms_ready, 1)
                dve.wait_ge(rt_ready, t + 1)
                step(V.reciprocal(rs[:, :], rs[:, :]))
                if t == 2 * DEPTH:
                    for k in range(KD):
                        last = V.scalar_tensor_tensor(hT[:, k, :], xT[:, k, :], vecT[:, V_FIN + k:V_FIN + k + 1], rs[:, :], ALU.mult, ALU.mult)
                    last.then_inc(h_ready, 1)
                    return
                l, i = divmod(t, 2)
                step(V.tensor_tensor(hT[:, :, :], xT[:, :, :], rs[:, :].rearrange("p (o t) -> p o t", o=1).to_broadcast([128, KD, N2]), ALU.mult))
                dve.wait_ge(amod_ready, l + 1)
                for k in range(KD):
                    for b in range(2):
                        x = hT[:, k, b * T:(b + 1) * T]
                        last = V.tensor_scalar(x, x, amod[:, l, i, k, b:b + 1], mod[:, l, 24 * i + k, b:b + 1], ALU.mult, ALU.add)
                last.then_inc(h_ready, 1)

            def residual(l, i, src):
                for k in range(KD):
                    for b in range(2):
                        x = xT[:, k, b * T:(b + 1) * T]
                        last = V.scalar_tensor_tensor(x, src(k, b), mod[:, l, 24 * i + 16 + k, b:b + 1], x, ALU.mult, ALU.add)
                last.then_inc(x_ready, 1)
                dve.wait_ge(x_ready, 2 * l + i + 2)

            def mixer(l):
                dve.wait_ge(cacheT_done, l + 1)
                V.tensor_copy(ckvT[:, :, 2 * T:], ps[:, 3, 0:2 * PAST].rearrange("p (k t) -> p k t", k=KK))
                V.tensor_copy(kpeT[:, 2 * T:], ps[:, 3, 2 * PAST:3 * PAST]).then_inc(cacheT_ready, 1)
                norm(2 * l)
                dve.wait_ge(items_used, ITEM["in", l, 2] + 1)
                dve.wait_ge(pads_set, 1)
                if l:
                    dve.wait_ge(pool_ready, l)
                for i in range(2):
                    last = V.tensor_copy(up[:, 2 * i:2 * i + 2, :, PAD:PAD + T], ps[:, 4 + i, :].rearrange("p (g b t) -> p g b t", g=2, b=2))
                last.then_inc(u_ready, 1)
                dve.wait_ge(ssqk_done, l + 1)
                V.tensor_scalar(sqqk[:, 2, :], ps[:, 1, 0:N2], 1.0 / QL, EPS, ALU.mult, ALU.add)
                V.tensor_scalar(sqqk[:, 3, :], ps[:, 1, N2:2 * N2], 1.0 / KL, EPS, ALU.mult, ALU.add).then_inc(msqk_ready, 1)
                dve.wait_ge(kpe_rot_done, l + 1)
                V.tensor_copy(kpeT[:, 0:T], kpe_raw[:, 0:T])
                V.tensor_tensor(kpeT[:, T:2 * T], kpe_raw[:, T:2 * T], cst[:, C_COS:C_COS + T], ALU.mult)
                step(V.tensor_tensor(rope_t[:, 0, :], ps[:, 2, 0:T], cst[:, C_SIN:C_SIN + T], ALU.mult))
                V.tensor_tensor(kpeT[:, T:2 * T], kpeT[:, T:2 * T], rope_t[:, 0, :], ALU.add).then_inc(kpe_ready, 1)
                dve.wait_ge(rtqk_ready, l + 1)
                step(V.reciprocal(sqqk[:, 0:2, :], sqqk[:, 0:2, :]))
                for m in range(KQ):
                    V.scalar_tensor_tensor(cqT[:, m, :], cqT[:, m, :], vecT[:, V_QG + KQ * l + m:V_QG + KQ * l + m + 1], sqqk[:, 0, :], ALU.mult, ALU.mult)
                for m in range(KK):
                    last = V.scalar_tensor_tensor(ckvT[:, m, 0:N2], rqk[:, m, :], vecT[:, V_KG + KK * l + m:V_KG + KK * l + m + 1], sqqk[:, 1, :], ALU.mult, ALU.mult)
                last.then_inc(qkvn_ready, 1)
                dve.wait_ge(qpe_rot_done, l + 1)
                cos, sin = (cst[:, a:a + T].rearrange("p (o t) -> p o t", o=1).to_broadcast([128, 2, T]) for a in (C_COS, C_SIN))
                V.tensor_tensor(qpe[:, :, T:], qpe[:, :, T:], cos, ALU.mult)
                step(V.tensor_tensor(rope_t, ps[:, 2, 0:N2].rearrange("p (j t) -> p j t", j=2), sin, ALU.mult))
                V.tensor_tensor(qpe[:, :, T:], qpe[:, :, T:], rope_t, ALU.add).then_inc(qpe_ready, 1)
                dve.wait_ge(items_used, ITEM["ukv", l, 0] + 1)
                for i, b in enumerate((0, 6, 7)):
                    last = V.tensor_copy(v[:, i, :], ps[:, b, :])
                last.then_inc(v_ready, 1)
                dve.wait_ge(s_done, l + 1)
                mx = stat[:, 0:8].rearrange("p (h b) -> p h b", b=2)
                V.reduce_max(mx[:, :, 0], ps[:, 4:8, 0:T], AX.X)
                step(V.reduce_max(mx[:, :, 1], ps[:, 4:8, T:3 * T], AX.X))
                V.tensor_scalar(stat[:, 8:16], stat[:, 0:8], -SCALE, None, ALU.mult).then_inc(nmx_ready, 1)
                dve.wait_ge(p_ready, l + 1)
                step(V.reciprocal(stat[:, 16:24], stat[:, 16:24]))
                ri = stat[:, 16:24].rearrange("p (h b) -> p h b", b=2)
                V.tensor_tensor(p[:, :, 0:T], p[:, :, 0:T], ri[:, :, 0:1].to_broadcast([128, NH, T]), ALU.mult)
                V.tensor_tensor(p[:, :, T:], p[:, :, T:], ri[:, :, 1:2].to_broadcast([128, NH, 2 * T]), ALU.mult).then_inc(pn_ready, 1)
                dve.wait_ge(pT_done, l + 1)
                V.tensor_copy(pT[:, 2, :], ps[:, 3, 0:3 * 128])
                V.tensor_copy(pT[:, 3, :], ps[:, 0, 0:3 * 128]).then_inc(pT_high_ready, 1)
                dve.wait_ge(pooled_done, l + 1)
                for g in range(NG):
                    last = V.tensor_scalar(mixT[:, NH + g, :], ps[:, 6 + g // 2, (g % 2) * N2:(g % 2 + 1) * N2], vecT[:, V_PS + NG * l + g:V_PS + NG * l + g + 1], None, ALU.mult)
                last.then_inc(pooled_ready, 1)
                dve.wait_ge(items_used, ITEM["out", l, 1] + 1)
                residual(l, 0, lambda k, b: ps[:, k // 2, (k % 2) * N2 + b * T:(k % 2) * N2 + (b + 1) * T])
                norm(2 * l + 1)

            mixer(0)
            for c in range(FSTEPS):
                dve.wait_ge(fsg_ready, c + 1)
                if c >= 2:
                    dve.wait_ge(items_used, ITEM["down", 0, c - 2] + 1)
                V.tensor_tensor(hm[:, c % 2, :], sg[:, c % 2, :], ps[:, 1, :], ALU.mult).then_inc(fh_ready, 1)
            dve.wait_ge(items_used, ITEM["down", 0, FSTEPS - 1] + 1)
            residual(0, 1, lambda k, b: ps[:, 2 + k // 2, (k % 2) * N2 + b * T:(k % 2) * N2 + (b + 1) * T])
            mixer(1)

            dve.wait_ge(logits_done, 1)
            lg = stat[:, 32:48].rearrange("p (b e) -> p b e", b=2)
            step(V.tensor_copy(lg, ps[:, 4, 0:16].rearrange("p (b e) -> p b e", b=2)))
            for b in range(2):
                last = V.max(rt8[:, b, :], lg[:, b, :])
            step(last)
            for b in range(2):
                V.max_index(rti[:, b, :], rt8[:, b, :], lg[:, b, :])
            last = V.tensor_tensor(stat[:, 24:26], rt8[:, :, 1], rt8[:, :, 0], ALU.subtract)
            last.then_inc(top2_ready, 1)
            dve.wait_ge(top2_ready, 1)
            step(V.tensor_copy(stat[:, 48:52].rearrange("p (b j) -> p b j", b=2), rti[:, :, 0:2]))
            iota8 = cst[:, C_IOTA:C_IOTA + NE]
            for b in range(2):
                for j in range(2):
                    last = V.tensor_scalar(oh[:, j, b, :], iota8, stat[:, 48 + 2 * b + j:49 + 2 * b + j], None, ALU.is_equal)
            step(last)
            V.tensor_tensor(oh[:, 2, :, :], oh[:, 0, :, :], oh[:, 1, :, :], ALU.add).then_inc(sel_ready, 1)
            dve.wait_ge(e1_ready, 1)
            step(V.tensor_scalar(stat[:, 52:54], stat[:, 26:28], 1.0, None, ALU.add))
            step(V.reciprocal(stat[:, 52:54], stat[:, 52:54]))
            step(V.tensor_tensor(stat[:, 54:56], stat[:, 52:54], stat[:, 26:28], ALU.mult))
            for b in range(2):
                last = V.tensor_scalar(oh[:, 0, b, :], oh[:, 0, b, :], stat[:, 52 + b:53 + b], None, ALU.mult)
            step(last)
            for b in range(2):
                last = V.scalar_tensor_tensor(oh[:, 3, b, :], oh[:, 1, b, :], stat[:, 54 + b:55 + b], oh[:, 0, b, :], ALU.mult, ALU.add)
            step(last)
            dve.wait_ge(rank_done, 1)
            step(V.scalar_tensor_tensor(oh[:, 0, :, :], ps[:, 5, 0:16].rearrange("p (b e) -> p b e", b=2), 1.0, oh[:, 2, :, :], ALU.add, ALU.mult))
            step(V.tensor_scalar(oh[:, 0, :, :], oh[:, 0, :, :], -1.0, None, ALU.add))
            step(V.reduce_max(stat[:, 56:57], ps[:, 5, 16:16 + NE], AX.X))
            step(V.tensor_scalar(stat[:, 57:58], stat[:, 56:57], OVER_LIMIT, None, ALU.is_gt))
            V.tensor_copy(over[:, :], stat[:, 57:58]).then_inc(over_ready, 1)
            V.memset(P[:, NE, :, :], 0.0)
            V.memset(PgT[:, 0, :, :], 0.0)
            V.memset(Y, 0.0)
            V.memset(stat[:, 58:59], 0.0).then_inc(eh_ready, 1)
            V.memset(stat[:, 59:60], 0.0).then_inc(eh_ready, 1)
            V.memset(stat[:, 60:61], 0.0).then_inc(acc_ready, 1)
            V.memset(stat[:, 61:62], 0.0).then_inc(acc_ready, 1)
            V.memset(acc[:, :, :], 0.0).then_inc(moe_zero, 1)
            dve.wait_ge(moe_zero, 1)

            def place(rnd):
                if rnd:
                    V.tensor_scalar(oh[:, 0, :, :], oh[:, 0, :, :], -128.0, None, ALU.add).then_inc(shift_ready, 1)
                    dve.wait_ge(shift_ready, rnd)
                iota = cst[:, C_IOTA:C_IOTA + 128]
                for e in range(NE):
                    for b in range(2):
                        last = V.tensor_scalar(P[:, e, b, :], iota, oh[:, 0, b, e:e + 1], None, ALU.is_equal)
                    last.then_inc(P_ready, 1)
                    if e or rnd:
                        dve.wait_ge(PgT_done, e + NE * rnd)
                        V.tensor_copy(PgT[:, e if e else NE, :, :], ps[:, 6, 0:N2].rearrange("p (b t) -> p b t", b=2)) if e else None
                    for b in range(2):
                        last = V.tensor_scalar(Pg[:, b, :], iota, oh[:, 0, b, e:e + 1], oh[:, 3, b, e:e + 1], ALU.is_equal, ALU.mult)
                    last.then_inc(Pg_ready, 1)
                dve.wait_ge(PgT_done, NE * (rnd + 1))
                V.tensor_copy(PgT[:, NE, :, :], ps[:, 6, 0:N2].rearrange("p (b t) -> p b t", b=2)).then_inc(PgT_ready, 1)

            def take_xg():
                for q in range(2):
                    last = V.tensor_copy(xg[:, 4 * q:4 * q + 4, :], ps[:, 6 + q, :].rearrange("p (k t) -> p k t", k=4))
                last.then_inc(xg_ready, 1)

            def add_up(done):
                for r in range(4):
                    dve.wait_ge(cmb_done, done + (r + 1))
                    a = acc[:, 2 * r:2 * r + 2, :]
                    V.tensor_tensor(a, a, ps[:, 6 + r % 2, :].rearrange("p (k t) -> p k t", k=2), ALU.add).then_inc(acc_ready, 1)

            def experts(rnd):
                place(rnd)
                dve.wait_ge(gat_done, 9 * rnd + 1)
                take_xg()
                with dve.Fori(0, NE) as e:
                    k = e + NE * rnd
                    for c in range(ESTEPS):
                        dve.wait_ge(items_used, k * E_ITEMS + (MOE0 + item_u(c) + 1))
                        dve.wait_ge(esg_ready, k * ESTEPS + (c + 2))
                        V.tensor_tensor(hm[:, c % 2, :], sg[:, c % 2, :], ps[:, 1, :], ALU.mult).then_inc(eh_ready, 1)
                        if c == 0:
                            add_up(k * 4 + 4 * rnd)
                    dve.wait_ge(gat_done, k + (rnd + 2))
                    take_xg()
                add_up(36 * rnd + 32)
                dve.wait_ge(acc_ready, 36 * (rnd + 1) + 2)

            experts(0)
            more = dve.value_load(over[0:1, 0:1])
            with dve.If(more > 0):
                experts(1)
            residual(1, 1, lambda k, b: acc[:, k, b * T:(b + 1) * T])
            norm(2 * DEPTH)

        @block.tensor
        def _(pe):
            mm = nc.tensor.matmul

            def slot(n, k, width):
                return ring[:, n % SLOTS, 0:k * width].rearrange("p (k n) -> p k n", k=k)

            def arrived(kind, l, j):
                n = ITEM[kind, l, j]
                pe.wait_ge(in_slot[n % SLOTS], ARRIVED[n])
                return n

            pe.wait_ge(small_in, 16 * 10)
            for a, r in ((0, 128), (1, V_B_ROWS)):
                last = nc.tensor.transpose(ps[:, 0, 128 * a:128 * a + r], vrow[0:r, a, :], ident[0:r, 0:r])
            last.then_inc(vecT_done, 1)
            pe.wait_ge(x_in, 32)
            for b in range(2):
                for k in range(KD):
                    last = nc.tensor.transpose(ps[:, 1 + 2 * b + k // 4, (k % 4) * 128:(k % 4 + 1) * 128], xin[:, b, k * 128:(k + 1) * 128], ident)
            last.then_inc(xT_done, 1)

            pe.wait_ge(silu_ready, 1)
            done = [0]

            def turn_mod(n):
                pe.wait_ge(mrow_ready, n + 1)
                if n:
                    pe.wait_ge(mod_ready, n)
                for q in range(4):
                    last = mm(ps[:, 5, 2 * q:2 * q + 2], mrow[:, n % 2, q * 128:(q + 1) * 128], ident[0:2, 0:2], start=True, stop=True)
                last.then_inc(modT_done, 1)

            for l in range(DEPTH):
                for j in range(ADA_ITEMS):
                    n = l * ADA_ITEMS + j
                    w = slot(arrived("ada", l, j), KD, ADA_COLS)
                    if n >= 2:
                        pe.wait_ge(mrow_ready, n - 1)
                    for k in range(KD):
                        last = mm(ps[0:2, 6 + n % 2, :], silu_c[:, k, :], w[:, k, :], start=k == 0, stop=k == KD - 1)
                    last.then_inc(items_used, 1)
                    if n:
                        turn_mod(n - 1)
            turn_mod(DEPTH * ADA_ITEMS - 1)
            pe.wait_ge(ones_set, 1)
            pe.wait_ge(cache_in, 16 * (3 * DEPTH + 2))

            def norm(t):
                pe.wait_ge(sq_ready, t + 1)
                for k in range(KD):
                    last = mm(ps[:, 0, 0:N2], ones[:, :], sq[:, k, :], start=k == 0, stop=k == KD - 1)
                last.then_inc(ss_done, 1)

            def project(bank, half, w, cols, x, kk):
                for k in range(kk):
                    last = mm(ps[:, bank, half * N2:(half + 1) * N2], w[:, k, cols], x[:, k, 0:N2], start=k == 0, stop=k == kk - 1)
                return last

            def mixer(l):
                for m in range(KK):
                    nc.tensor.transpose(ps[:, 3, m * 128:(m + 1) * 128], cache[:, l, m * 128:(m + 1) * 128], ident)
                nc.tensor.transpose(ps[:, 3, 256:384], cache[:, l, KL:KL + 128], ident).then_inc(cacheT_done, 1)
                norm(2 * l)
                pe.wait_ge(h_ready, 2 * l + 1)
                w = slot(arrived("in", l, 0), KD, QL)
                for m in range(KQ):
                    last = project(1 + m // 2, m % 2, w, slice(m * 128, (m + 1) * 128), hT, KD)
                last.then_inc(items_used, 1)
                w = slot(arrived("in", l, 1), KD, KL + ROPE)
                pe.wait_ge(cacheT_ready, l + 1)
                for m in range(KK):
                    project(3, m, w, slice(m * 128, (m + 1) * 128), hT, KD)
                for i in range(2):
                    for k in range(KD):
                        last = mm(ps[64 * i:64 * i + 64, 2, N2:2 * N2], w[:, k, KL:KL + ROPE], hT[:, k, :], start=k == 0, stop=k == KD - 1)
                last.then_inc(items_used, 1)
                w = slot(arrived("in", l, 2), KD, POOL_W)
                for g in range(NG):
                    last = project(4 + g // 2, g % 2, w, slice(g * 128, (g + 1) * 128), hT, KD)
                last.then_inc(items_used, 1)
                pe.wait_ge(sqqk_ready, l + 1)
                for m in range(KQ):
                    mm(ps[:, 1, 0:N2], ones[:, :], sqqk[:, m, :], start=m == 0, stop=m == KQ - 1)
                for m in range(KK):
                    last = mm(ps[:, 1, N2:2 * N2], ones[:, :], sqqk[:, KQ + m, :], start=m == 0, stop=m == KK - 1)
                last.then_inc(ssqk_done, 1)
                rot = cst[:, C_ROT:C_ROT + 128]
                mm(ps[:, 2, 0:T], rot, kpe_raw[:, T:], start=True, stop=True).then_inc(kpe_rot_done, 1)
                pe.wait_ge(qkvn_ready, l + 1)
                pe.wait_ge(u_ready, l + 1)
                w = slot(arrived("uq", l, 0), KQ, NH * (NOPE + ROPE))
                for h in range(NH):
                    a = h * (NOPE + ROPE)
                    project(4 + h // 2, h % 2, w, slice(a, a + NOPE), cqT, KQ)
                for h in range(NH):
                    a, pp = h * (NOPE + ROPE) + NOPE, slice(64 * (h % 2), 64 * (h % 2) + 64)
                    for k in range(KQ):
                        last = mm(ps[pp, 3, h // 2 * N2:(h // 2 + 1) * N2], w[:, k, a:a + ROPE], cqT[:, k, :], start=k == 0, stop=k == KQ - 1)
                last.then_inc(items_used, 1)
                pe.wait_ge(qraw_ready, l + 1)
                pe.wait_ge(kpe_ready, l + 1)
                mm(ps[:, 2, 0:N2], rot, qpe[:, :, T:], start=True, stop=True).then_inc(qpe_rot_done, 1)
                w = slot(arrived("ukv", l, 0), KK, NH * (NOPE + VD))
                for h, b in enumerate((4, 5, 3, 1)):
                    for k in range(KK):
                        mm(ps[:, b, 0:3 * 128], w[:, k, h * 256:h * 256 + NOPE], ckvT[:, k, :], start=k == 0, stop=k == KK - 1)
                wv = w.rearrange("p k (h n) -> p k h n", h=NH)
                for i, b in enumerate((0, 6, 7)):
                    for k in range(KK):
                        last = mm(ps[:, b, :], ckvT[:, k, i * 128:(i + 1) * 128], wv[:, k, :, NOPE:], start=k == 0, stop=k == KK - 1)
                last.then_inc(items_used, 1)
                pe.wait_ge(k_ready, l + 1)
                pe.wait_ge(v_ready, l + 1)
                pe.wait_ge(qpe_ready, l + 1)
                for h in range(NH):
                    pp = slice(64 * (h % 2), 64 * (h % 2) + 64)
                    for b, (a, z) in enumerate(((0, T), (T, 3 * T))):
                        mm(ps[:, 4 + h, a:z], qT[:, h, b * T:(b + 1) * T], kT[:, h, a:z], start=True, stop=False)
                        last = mm(ps[:, 4 + h, a:z], qpe[pp, h // 2, b * T:(b + 1) * T], kpeT[pp, a:z], start=False, stop=True)
                last.then_inc(s_done, 1)
                pe.wait_ge(pn_ready, l + 1)
                for h, b in enumerate((1, 2, 3, 0)):
                    for i in range(3):
                        last = nc.tensor.transpose(ps[:, b, i * 128:(i + 1) * 128], p[:, h, i * 128:(i + 1) * 128], ident)
                last.then_inc(pT_done, 1)
                pe.wait_ge(pool_ready, l + 1)
                for g in range(NG):
                    last = mm(ps[:, 6 + g // 2, (g % 2) * N2:(g % 2 + 1) * N2], wpool[:, l * NG + g, :], poolT[:, g, :], start=True, stop=True)
                last.then_inc(pooled_done, 1)
                pe.wait_ge(pT_low_ready, l + 1)
                pe.wait_ge(pT_high_ready, l + 1)
                for h in range(NH):
                    o = ps[:, 4 + h // 2, (h % 2) * N2:(h % 2 + 1) * N2]
                    vh = slice(h * VD, (h + 1) * VD)
                    mm(o[:, 0:T], v[:, 0, vh], pT[:, h, 0:128], start=True, stop=True)
                    mm(o[:, T:], v[:, 1, vh], pT[:, h, 128:256], start=True, stop=False)
                    last = mm(o[:, T:], v[:, 2, vh], pT[:, h, 256:384], start=False, stop=True)
                last.then_inc(o_done, 1)
                pe.wait_ge(o_ready, l + 1)
                pe.wait_ge(pooled_ready, l + 1)
                for j in range(2):
                    w = slot(arrived("out", l, j), KD, 512)
                    for m in range(4):
                        last = project((4 * j + m) // 2, m % 2, w, slice(m * 128, (m + 1) * 128), mixT, KD)
                    last.then_inc(items_used, 1)
                for m in range(KK):
                    nc.tensor.transpose(ps[:, 4, m * 128:(m + 1) * 128], ckvT[:, m, 0:T], ident)
                nc.tensor.transpose(ps[:, 4, KL:KL + ROPE], kpe_raw[0:ROPE, 0:T], ident[0:ROPE, 0:ROPE]).then_inc(kv_outT_done, 1)
                pe.wait_ge(x_ready, 2 * l + 2)
                norm(2 * l + 1)
                pe.wait_ge(h_ready, 2 * l + 2)

            mixer(0)
            pe.wait_ge(kv_out_ready, 1)

            def ffn_down(c):
                w = slot(arrived("down", 0, c), FC // 128, D)
                pe.wait_ge(fh_ready, c + 1)
                for k in range(FC // 128):
                    for m in range(KD):
                        last = mm(ps[:, 2 + m // 2, (m % 2) * N2:(m % 2 + 1) * N2], w[:, k, m * 128:(m + 1) * 128], hm[:, c % 2, k * N2:(k + 1) * N2],
                                  start=c == 0 and k == 0 and m % 2 == 0, stop=c == FSTEPS - 1 and k == FC // 128 - 1, skip_group_check=True)
                last.then_inc(items_used, 1)

            for c in range(FSTEPS):
                n = arrived("gu", 0, c)
                gu = ring[:, n % SLOTS, :].rearrange("p (w k n) -> p w k n", w=2, k=KD)
                for w in range(2):
                    if c:
                        pe.wait_ge((fsg_ready, fh_ready)[w], c)
                    for m in range(2):
                        last = project(w, m, gu[:, w], slice(m * 128, (m + 1) * 128), hT, KD)
                last.then_inc(items_used, 1)
                if c:
                    ffn_down(c - 1)
            ffn_down(FSTEPS - 1)
            pe.wait_ge(x_ready, 3)
            mixer(1)
            for n in range(MOE0):
                if STREAM[n][0] == "none":
                    pe.sem_inc(items_used, 1)

            for b in range(2):
                for k in range(KD):
                    last = nc.tensor.transpose(ps[:, 2 * b + k // 4, (k % 4) * 128:(k % 4 + 1) * 128], hT[:, k, b * T:(b + 1) * T], ident)
            last.then_inc(h2T_done, 1)
            pe.wait_ge(kv_out_ready, 2)
            for b in range(2):
                for k in range(KD):
                    last = mm(ps[:, 4, b * NE:(b + 1) * NE], hT[:, k, b * T:(b + 1) * T], wr[:, k, :], start=k == 0, stop=k == KD - 1)
            last.then_inc(logits_done, 1)
            pe.wait_ge(sel_ready, 1)
            tri = cst[:, C_TRI:C_TRI + 128]
            mm(ps[:, 5, 0:NE], tri, oh[:, 2, 0, :], start=True, stop=True)
            mm(ps[:, 5, NE:2 * NE], tri, oh[:, 2, 1, :], start=True, stop=False)
            mm(ps[:, 5, NE:2 * NE], ones[:, :], oh[:, 2, 0, :], start=False, stop=True)
            for b in range(2):
                last = mm(ps[:, 5, 2 * NE:3 * NE], ones[:, :], oh[:, 2, b, :], start=b == 0, stop=b == 1)
            last.then_inc(rank_done, 1)

            def gather(e):
                for m in range(KD):
                    for b in range(2):
                        rhs = P[:, e, b, :] if isinstance(e, int) else P[:, bass.ds(e, 1), b, :].rearrange("p o t -> p (o t)")
                        last = mm(ps[:, 6 + m // 4, (m % 4) * 128:(m % 4 + 1) * 128], h2[:, b, m * 128:(m + 1) * 128], rhs, start=b == 0, stop=b == 1)
                last.then_inc(gat_done, 1)

            def combine(e, k4):
                for r in range(4):
                    pe.wait_ge(acc_ready, k4 + (r + 1))
                    for q in range(2):
                        m = 2 * r + q
                        rhs = PgT[:, e, :, :] if isinstance(e, int) else PgT[:, bass.ds(e, 1), :, :].rearrange("p o b t -> p (o b) t")
                        last = mm(ps[:, 6 + r % 2, q * N2:(q + 1) * N2], Y[:, m * 128:(m + 1) * 128], rhs, start=True, stop=True)
                    last.then_inc(cmb_done, 1)

            def experts(rnd):
                for e in range(NE):
                    pe.wait_ge(Pg_ready, e + 1 + NE * rnd)
                    if e:
                        pass
                    for b in range(2):
                        last = nc.tensor.transpose(ps[:, 6, b * 128:(b + 1) * 128], Pg[:, b, :], ident)
                    last.then_inc(PgT_done, 1)
                pe.wait_ge(PgT_ready, rnd + 1)
                pe.wait_ge(h2_ready, 1)
                pe.wait_ge(moe_zero, 1)
                gather(0)
                with pe.Fori(0, NE) as e:
                    k = e + NE * rnd
                    per = E_ITEMS // SLOTS * 16

                    def weights(i, kk, width):
                        pe.wait_ge(in_slot[i % SLOTS], k * per + (MOE_ARRIVED[i % SLOTS] + 16 * (i // SLOTS + 1)))
                        return slot(i, kk, width)

                    def into_hidden(bank, i):
                        w = weights(i, KD, EC)
                        for kk in range(KD):
                            last = mm(ps[:, bank, :], xg[:, kk, :], w[:, kk, :], start=kk == 0, stop=kk == KD - 1)
                        last.then_inc(items_used, 1)

                    def turn(c):
                        pe.wait_ge(eh_ready, k * ESTEPS + (c + 3))
                        pe.wait_ge(ehT_ready, k * ESTEPS + (c + 1))
                        for r in range(EC // 128):
                            last = nc.tensor.transpose(ps[:, 2, r * 128:(r + 1) * 128], hm[:, c % 2, r:EC:EC // 128], ident)
                        last.then_inc(ehT_done, 1)

                    def down(c):
                        w = weights(item_d(c), EC // 128, D)
                        pe.wait_ge(ehT_ready, k * ESTEPS + (c + 2))
                        if c == 0:
                            pe.wait_ge(Y_ready, k + 1)
                        for half in range(2):
                            for r in range(EC // 128):
                                last = mm(ps[:, 4 + half, :], hTm[:, c % 2, r, :], w[:, r, half * 512:(half + 1) * 512],
                                          start=c == 0 and r == 0, stop=c == ESTEPS - 1 and r == EC // 128 - 1)
                        last.then_inc(items_used, 1)

                    pe.wait_ge(xg_ready, k + (rnd + 1))
                    for c in range(ESTEPS):
                        pe.wait_ge(esg_ready, k * ESTEPS + (c + 1))
                        into_hidden(0, item_g(c))
                        if c:
                            turn(c - 1)
                        pe.wait_ge(eh_ready, k * ESTEPS + (c + 2))
                        into_hidden(1, item_u(c))
                        if c:
                            down(c - 1)
                        else:
                            pe.wait_ge(Y_ready, k + 1)
                            combine(e, k * 4 + 4 * rnd)
                    pe.wait_ge(acc_ready, k * 4 + (4 * rnd + 6))
                    gather(e + 1)
                    turn(ESTEPS - 1)
                    down(ESTEPS - 1)
                pe.wait_ge(Y_ready, NE * (rnd + 1) + 1)
                pe.wait_ge(xg_ready, 9 * (rnd + 1))
                combine(NE, 36 * rnd + 32)

            experts(0)
            pe.wait_ge(over_ready, 1)
            more = pe.value_load(over[0:1, 0:1])
            with pe.If(more > 0):
                experts(1)
            norm(2 * DEPTH)
            pe.wait_ge(h_ready, 2 * DEPTH + 1)
            for b in range(2):
                for k in range(KD):
                    last = nc.tensor.transpose(ps[:, 1 + 2 * b + k // 4, (k % 4) * 128:(k % 4 + 1) * 128], hT[:, k, b * T:(b + 1) * T], ident)
            last.then_inc(outT_done, 1)


OVER_LIMIT = 128.0
_INS = ["x_prompt", "x_sample", "c", "cache_ckv", "cache_kpe", "c_ctx", "norm1_g", "norm2_g", "w_ada", "b_ada", "w_in",
        "q_norm_g", "kv_norm_g", "w_uq", "w_ukv", "w_pool", "pool_scale", "w_out", "ffn_w_gate", "ffn_w_up", "ffn_w_down",
        "moe_w_router", "moe_w_gate", "moe_w_up", "moe_w_down", "final_norm_g"]
_OUTS = [(1, T, D), (1, T, D), (1, DEPTH, T, KL), (1, DEPTH, T, ROPE)]


def kernel(**inputs):
    import concourse.bacc as _bacc
    from concourse.bass_utils import run_bass_kernel_spmd as _run

    nc = _bacc.Bacc("TRN2", target_bir_lowering=False, num_devices=1)
    f32 = mybir.dt.float32
    arrays, aps = {}, {}
    for name in _INS:
        a = np.ascontiguousarray(inputs[name])
        arrays[f"in_{name}"] = a
        aps[name] = nc.dram_tensor(f"in_{name}", a.shape, f32, kind="ExternalInput").ap()
    arrays["in_constants"] = constants()
    consts = nc.dram_tensor("in_constants", (128, C_COLS), f32, kind="ExternalInput").ap()
    outs = [nc.dram_tensor(f"out_{i}", s, f32, kind="ExternalOutput").ap() for i, s in enumerate(_OUTS)]
    program(nc, aps, consts, outs[0].rearrange("b t d -> (b t) d"), outs[1].rearrange("b t d -> (b t) d"), outs[2], outs[3])
    r = _run(nc, [arrays], core_ids=[0])
    return tuple(r.results[0][f"out_{i}"] for i in range(len(_OUTS)))
```

```python
import numpy as np
import concourse.bass as bass
from concourse import mybir
from contextlib import ExitStack

D = 1024
T = 128
DEPTH = 2
PAST = 128
GRID_W = 64
NH = 4
NOPE = 128
ROPE = 64
VD = 128
QL = 384
KL = 256
POOL_WINDOWS = (2, 4, 8, 16)
NG = len(POOL_WINDOWS)
POOL_W = 512
FF = 2816
NE = 8
FE = 3584
EPS = 1e-6
ROPE_BASE = 10000.0

KD = D // 128
KQ = QL // 128
KK = KL // 128
N2 = 2 * T
ADA = 6 * D
ADA_COLS = 512
ADA_ITEMS = ADA // ADA_COLS
FC = 256
FSTEPS = FF // FC
EC = 512
ESTEPS = FE // EC
SLOTS = 7
SLOT = 2048
PIECE = 1024
PIECES = 7
E_ITEMS = 6 * ESTEPS
E_PIECES = 2 * E_ITEMS
assert E_PIECES % PIECES == 0
COMBINE_BANKS = (6, 7, 3, 2)
PAD = 8
TP = T + 2 * PAD

C_ID, C_ROT, C_COS, C_SIN, C_TRI, C_IOTA, C_CNT = (128 * i for i in range(7))
C_SEL = C_CNT + NG * 128
C_COLS = C_SEL + 2

V_BADA, V_N1, V_N2 = 0, 96, 112
V_FIN, V_PS, V_QG, V_KG, V_CC, V_C = (128 + i for i in (0, 8, 16, 22, 26, 34))
V_B_ROWS = 42


def constants():
    out = np.zeros((128, C_COLS), np.float32)
    out[:, C_ID:C_ID + 128] = np.eye(128)
    rot = np.zeros((128, 128), np.float32)
    q = ROPE // 4
    for base in range(0, 128, 2 * q):
        for i in range(q):
            rot[base + i, base + q + i] = -1.0
            rot[base + q + i, base + i] = 1.0
    out[:, C_ROT:C_ROT + 128] = rot.T
    t = np.arange(T)
    half = ROPE // 2
    freqs = (ROPE_BASE ** (-np.arange(0, half, 2, dtype=np.float32) / half)).astype(np.float32)
    ar = (t // GRID_W).astype(np.float32)[:, None] * freqs
    ac = (t % GRID_W).astype(np.float32)[:, None] * freqs
    ang = np.concatenate([ar, ar, ac, ac], axis=-1).T
    out[:, C_COS:C_COS + 128] = np.tile(np.cos(ang), (2, 1))
    out[:, C_SIN:C_SIN + 128] = np.tile(np.sin(ang), (2, 1))
    out[:, C_TRI:C_TRI + 128] = np.triu(np.ones((128, 128)), 1)
    out[:, C_IOTA:C_IOTA + 128] = np.arange(128)
    for g, w in enumerate(POOL_WINDOWS):
        cnt = np.minimum(t + w // 2, T) - np.maximum(t - w // 2, 0)
        out[:, C_CNT + g * 128:C_CNT + (g + 1) * 128] = (1.0 / cnt).astype(np.float32)
    out[0:4, C_SEL:C_SEL + 2] = np.tile(np.eye(2), (2, 1))
    return out


DIRECT = ("cache", "uq", "ukv", "pool")
IN_COLS = ((0, 256), (256, 512), (512, QL + KL + ROPE), (704, 960), (960, 1216))
ADA_AFTER = {c: c for c in range(FSTEPS)}


def stream():
    def ada(l, j):
        return [("ada", l, 2 * j), ("ada", l, 2 * j + 1)]

    out = [x for j in range(ADA_ITEMS) for x in ada(0, j)]
    for l in range(DEPTH):
        out += [("cache", l, 0)] + [("in", l, j) for j in range(5)]
        out += [("uq", l, 0), ("uq", l, 1), ("ukv", l, 0), ("pool", l, 0)] + [("out", l, j) for j in range(4)]
        if l == 0:
            for c in range(FSTEPS):
                out += [("gate", l, c), ("up", l, c)]
                if c:
                    out += [("down", l, c - 1)]
                out += ada(1, c)
            out += [("down", l, FSTEPS - 1)] + ada(1, FSTEPS)
    return out


STREAM = stream()
ITEM = {x: n for n, x in enumerate(STREAM)}
N0 = len(STREAM)
MOE0 = -(-N0 // SLOTS) * SLOTS
PIECE0 = [2 * sum(x[0] not in DIRECT for x in STREAM[:n]) for n in range(N0 + 1)]
MP0 = PIECE0[N0]


def first(kind, l, j):
    return PIECE0[ITEM[kind, l, j]]


def end(kind, l, j):
    return PIECE0[ITEM[kind, l, j] + 1]


TRANSFERS = {"cache": 3}
_count = [0] * SLOTS
ARRIVED = []
for _n, _x in enumerate(STREAM):
    _count[_n % SLOTS] += 16 * TRANSFERS.get(_x[0], 1)
    ARRIVED.append(_count[_n % SLOTS])
MOE_ARRIVED = list(_count)
PER_EXPERT = [len(range(s, E_ITEMS, SLOTS)) for s in range(SLOTS)]
DIRECT_USED = {("cache", 0): 1, ("uq", 0): 2, ("uq", 1): 2, ("ukv", 0): 3, ("pool", 0): 4}


def piece_g(c):
    return 0 if c == 0 else 12 * c - 4


def piece_u(c):
    return piece_g(c) + 4


def piece_d(c):
    return 12 * c + 16 if c < ESTEPS - 1 else E_PIECES - 4


def expert_item(i):
    for c in range(ESTEPS):
        for what, at in (("g", piece_g(c)), ("u", piece_u(c)), ("d", piece_d(c))):
            if 0 <= 2 * i - at < 4:
                return what, c, (2 * i - at) // 2


def program(nc, ins, consts, y_prompt, y_sample, new_ckv, new_kpe):
    f32 = mybir.dt.float32
    f32r = mybir.dt.float32r
    i32 = mybir.dt.int32
    u32 = mybir.dt.uint32
    ALU = mybir.AluOpType
    ACT = mybir.ActivationFunctionType
    AX = mybir.AxisListType
    SCALE = float(NOPE + ROPE) ** -0.5

    ctx = ExitStack()
    with ctx:
        place_at = [-(-nc.sbuf_base // 32) * 32]

        def sb(name, *shape, dt=f32):
            t = nc.alloc_sbuf_tensor_at(name, list(shape), dt, offset=place_at[0])
            place_at[0] += -(-4 * int(np.prod(shape[1:])) // 32) * 32
            return t

        def sem(name):
            return ctx.enter_context(nc.semaphore(name))

        ring = sb("ring", 128, SLOTS, SLOT)
        high = sb("high", 128, PIECES, PIECE, dt=f32r)
        low = sb("low", 128, PIECES, PIECE, dt=f32r)
        cst = sb("cst", 128, C_COLS)
        xT = sb("xT", 128, KD, N2)
        sq = sb("sq", 128, KD, N2)
        ones = sb("ones", 128, 128)
        vecT = sb("vecT", 128, 128 + V_B_ROWS)
        silu_f = sb("silu_f", 128, KD, 2)
        silu_c = sb("silu_c", 128, KD, 4, dt=f32r)
        mod = sb("mod", 128, DEPTH, 48, 2)
        amod = sb("amod", 128, DEPTH, 2, KD, 2)
        mrow = sb("mrow", 4, ADA_COLS)
        rs = sb("rs", 128, N2)
        wr = sb("wr", 128, KD, NE)
        kv_out = sb("kv_out", 128, DEPTH, KL + ROPE)
        stat = sb("stat", 128, 64)
        rt8 = sb("rt8", 128, 2, 8)
        rti = sb("rti", 128, 2, 8, dt=u32)
        oh = sb("oh", 128, 4, 2, NE)
        over = sb("over", 128, 1, dt=i32)
        shared = place_at[0]
        hT = sq

        def words(*shape):
            return int(np.prod(shape))

        def view(t, at, *shape):
            a = t[:, at:at + words(*shape)]
            if len(shape) == 1:
                return a
            names = "abcd"[:len(shape)]
            return a.rearrange(f"p ({' '.join(names)}) -> p {' '.join(names)}", **dict(zip(names, shape)))

        hx = sb("hx", 128, KD, 2, N2, dt=f32r)
        hid = sb("hid", 128, 2 * NH * 3 * 128)
        arena_at = place_at[0]
        arena = sb("arena", 128, 9344)
        assert place_at[0] <= nc.sbuf_usable_end, (place_at[0], nc.sbuf_usable_end)
        at = [0]

        def cut(*shape):
            at[0] += words(*shape)
            assert at[0] <= 9344, at[0]
            return view(arena, at[0] - words(*shape), *shape)

        xin = view(arena, 0, 2, D)
        vrow = view(arena, 2 * D, 2, 128)
        cqT = cut(KQ, N2)
        ckvT = cut(KK, T + T + PAST)
        kpe_raw = cut(N2)
        kpeT = cut(T + T + PAST)
        sqqk = cut(KQ + KK, N2)
        rqk = cut(2, N2)
        qT = cut(NH, N2)
        qpe = cut(2, N2)
        qq = arena[:, at[0] - (NH + 2) * N2:at[0]]
        rope_t = cut(2, T)
        kT = view(hid, 0, NH, 3 * 128)
        v = view(hid, NH * 3 * 128, 3, NH * VD)
        p = qq.rearrange("p (h t) -> p h t", h=NH)
        pT = kT
        up = cut(NG, 2, TP)
        win = cut(2, NG * 2 * TP)
        poolT = sq[:, 0:NG, :]
        fsg, fh = view(hid, 0, 2, FC * 2), view(hid, 2 * FC * 2, 2, FC * 2)
        place_at[0] = arena_at
        fx = sb("fx", 128, 2, FC // 128, 2, N2, dt=f32r)
        place_at[0] = shared
        hTm = sb("hTm", 128, 2, EC // 128, 128, dt=f32r)
        xg = sb("xg", 128, 2, KD, 128, dt=f32r)
        ehid = sb("ehid", 128, 2, 2, EC)
        sg, hm = ehid[:, 0], ehid[:, 1]
        h2 = sb("h2", 128, 2, D)
        P = sb("P", 128, NE + 1, 2, 128)
        PgT = sb("PgT", 128, NE + 1, 2, 128)
        Y = sb("Y", 128, D)
        Pg = sb("Pg", 128, 2, 128)
        yout = h2[:, :, :].rearrange("p b d -> p (b d)")
        acc = sq

        ps = ctx.enter_context(nc.psum_tensor("ps", [128, 8, 512], f32))

        in_slot = [sem(f"in_slot{i}") for i in range(SLOTS)]
        high_ready, low_ready, pieces_used, direct_used = (sem(x) for x in ("high_ready", "low_ready", "pieces_used", "direct_used"))
        small_in, x_in, router_in = sem("small_in"), sem("x_in"), sem("router_in")
        ones_set, pads_set = sem("ones_set"), sem("pads_set")
        vecT_done, vecT_ready = sem("vecT_done"), sem("vecT_ready")
        xT_done, x_ready = sem("xT_done"), sem("x_ready")
        silu_ready, siluh_ready, silul_ready = sem("silu_ready"), sem("siluh_ready"), sem("silul_ready")
        mrow_ready, modT_done, mod_ready, amod_ready = (sem(x) for x in ("mrow_ready", "modT_done", "mod_ready", "amod_ready"))
        sq_ready, ss_done, ms_ready, rt_ready, h_ready = (sem(x) for x in ("sq_ready", "ss_done", "ms_ready", "rt_ready", "h_ready"))
        hxh_ready, hx_ready = sem("hxh_ready"), sem("hx_ready")
        cacheT_ready = sem("cacheT_ready")
        u_ready, sqqk_ready, ssqk_done, kpe_rot_done = (sem(x) for x in ("u_ready", "sqqk_ready", "ssqk_done", "kpe_rot_done"))
        msqk_ready, rtqk_ready, qkvn_ready, kpe_ready = (sem(x) for x in ("msqk_ready", "rtqk_ready", "qkvn_ready", "kpe_ready"))
        qraw_ready, qpe_rot_done, qpe_ready = (sem(x) for x in ("qraw_ready", "qpe_rot_done", "qpe_ready"))
        k_ready, v_ready, s_done, nmx_ready, p_ready, pn_ready = (sem(x) for x in ("k_ready", "v_ready", "s_done", "nmx_ready", "p_ready", "pn_ready"))
        pT_done, pT_low_ready, pT_high_ready, o_done, oh_ready, ol_ready = (sem(x) for x in ("pT_done", "pT_low_ready", "pT_high_ready", "o_done", "oh_ready", "ol_ready"))
        pool_ready, pooledh_ready, pooledl_ready = (sem(x) for x in ("pool_ready", "pooledh_ready", "pooledl_ready"))
        kv_outT_done, kv_out_ready, stored = (sem(x) for x in ("kv_outT_done", "kv_out_ready", "stored"))
        fsg_ready, fh_ready, fxh_ready, fx_ready = (sem(x) for x in ("fsg_ready", "fh_ready", "fxh_ready", "fx_ready"))
        h2T_done, h2_ready, logits_done, sel_ready, rank_done = (sem(x) for x in ("h2T_done", "h2_ready", "logits_done", "sel_ready", "rank_done"))
        e1_ready, top2_ready = sem("e1_ready"), sem("top2_ready")
        Pg_ready, PgT_done, PgT_ready = sem("Pg_ready"), sem("PgT_done"), sem("PgT_ready")
        moe_zero, over_ready, shift_ready = sem("moe_zero"), sem("over_ready"), sem("shift_ready")
        esg_ready, eh_ready, ehT_done, ehTh_ready, ehT_ready = (sem(x) for x in ("esg_ready", "eh_ready", "ehT_done", "ehTh_ready", "ehT_ready"))
        Y_ready, cmb_done, acc_ready = sem("Y_ready"), sem("cmb_done"), sem("acc_ready")
        gat_done, xgh_ready, xg_ready = sem("gat_done"), sem("xgh_ready"), sem("xg_ready")
        outT_done, y_ready = sem("outT_done"), sem("y_ready")
        dve_step, act_step, pool_step = sem("dve_step"), sem("act_step"), sem("pool_step")

        ident = cst[:, C_ID:C_ID + 128]

        class Steps:

            def __init__(self, eng, semaphore):
                self.eng, self.sem, self.n = eng, semaphore, 0

            def __call__(self, instruction):
                self.n += 1
                instruction.then_inc(self.sem, 1)
                self.eng.wait_ge(self.sem, self.n)

        def slot(n, k, width):
            return ring[:, n % SLOTS, 0:k * width].rearrange("p (k n) -> p k n", k=k)

        def shape_of(kind, j):
            if kind == "in":
                return KD, IN_COLS[j][1] - IN_COLS[j][0]
            return {"ada": (KD // 2, ADA_COLS), "out": (KD, 256), "gate": (KD, FC), "up": (KD, FC), "down": (FC // 128, D)}[kind]

        def raw_piece(n, half):
            kind, _, j = STREAM[n]
            k, width = shape_of(kind, j)
            a = slot(n, k, width)
            if kind in ("ada", "down"):
                return a[:, half * k // 2:(half + 1) * k // 2, :]
            if kind == "in" and j == 2 and half:
                return a[:, :, 128:].rearrange("p k (o n) -> p k o n", o=1).to_broadcast([128, KD, 2, ROPE])
            return a[:, :, half * 128:(half + 1) * 128]

        def halves(q, like):
            for t in (high, low):
                a = t[:, q % PIECES, :]
                if len(like.shape) == 4:
                    yield a.rearrange("p (k o n) -> p k o n", k=KD, o=2)
                else:
                    yield a.rearrange("p (k n) -> p k n", k=like.shape[1])

        def free(eng, n):
            kind, l, j = STREAM[n]
            if kind in DIRECT:
                eng.wait_ge(direct_used, 4 * l + DIRECT_USED[kind, j])
            else:
                eng.wait_ge(low_ready, PIECE0[n + 1])

        def rows_bank(l, j):
            return 6 + j % 2 if l == 0 else 6

        def turned_bank(l):
            return 5 if l == 0 else 7

        block = ctx.enter_context(nc.Block())

        @block.sync
        def _(sp):
            def by_rows(name):
                return ins[name].rearrange("l (k p) n -> l p k n", p=128)

            w = {x: by_rows(y) for x, y in (("ada", "w_ada"), ("in", "w_in"), ("uq", "w_uq"), ("ukv", "w_ukv"), ("out", "w_out"),
                                            ("gate", "ffn_w_gate"), ("up", "ffn_w_up"), ("down", "ffn_w_down"))}
            e_gate = ins["moe_w_gate"].rearrange("l e (k p) n -> (l e) p k n", p=128)
            e_up = ins["moe_w_up"].rearrange("l e (k p) n -> (l e) p k n", p=128)
            e_down = ins["moe_w_down"].rearrange("l e (c p r) n -> (l e) c p r n", p=128, r=EC // 128)

            def rows(r, a):
                src = a.rearrange("(r p) -> r p", p=128) if len(a.shape) == 1 else a.rearrange("l (r p) -> (l r) p", p=128)
                sp.dma_start(vrow[r % 128:r % 128 + src.shape[0], r // 128, :], src).then_inc(small_in, 16)

            sp.dma_start(cst[:, :], consts).then_inc(small_in, 16)
            for r, name in ((V_CC, "c_ctx"), (V_C, "c"), (V_BADA, "b_ada"), (V_N1, "norm1_g"), (V_N2, "norm2_g"),
                            (V_FIN, "final_norm_g"), (V_PS, "pool_scale"), (V_QG, "q_norm_g"), (V_KG, "kv_norm_g")):
                rows(r, ins[name])

            for n, (kind, l, j) in enumerate(STREAM):
                if n >= SLOTS:
                    free(sp, n - SLOTS)
                s = in_slot[n % SLOTS]
                if kind == "cache":
                    sp.dma_start(ring[:, n % SLOTS, 0:KL], ins["cache_ckv"][0, l]).then_inc(s, 16)
                    for i in range(2):
                        sp.dma_start(ring[:, n % SLOTS, KL + i * ROPE:KL + (i + 1) * ROPE], ins["cache_kpe"][0, l]).then_inc(s, 16)
                elif kind == "pool":
                    sp.dma_start(slot(n, NG, 128), ins["w_pool"][l].rearrange("g c d -> c g d")).then_inc(s, 16)
                elif kind == "uq":
                    a, b = ((0, 2), (2, KQ))[j]
                    sp.dma_start(slot(n, b - a, NH * (NOPE + ROPE)), w["uq"][l][:, a:b, :]).then_inc(s, 16)
                elif kind == "ukv":
                    sp.dma_start(slot(n, KK, NH * (NOPE + VD)), w["ukv"][l]).then_inc(s, 16)
                elif kind == "ada":
                    b, half = divmod(j, 2)
                    sp.dma_start(slot(n, KD // 2, ADA_COLS), w["ada"][l][:, half * (KD // 2):(half + 1) * (KD // 2), b * ADA_COLS:(b + 1) * ADA_COLS]).then_inc(s, 16)
                elif kind == "down":
                    k = FC // 128
                    sp.dma_start(slot(n, k, D), w["down"][l // 2][:, j * k:(j + 1) * k, :]).then_inc(s, 16)
                else:
                    a, b = IN_COLS[j] if kind == "in" else (j * 256, (j + 1) * 256)
                    sp.dma_start(slot(n, KD, b - a), w[kind][l if kind in ("in", "out") else l // 2][:, :, a:b]).then_inc(s, 16)

            def load(e, i):
                what, c, half = expert_item(i)
                s = in_slot[i % SLOTS]
                one = slice(e, e + 1) if isinstance(e, int) else bass.ds(e, 1)
                if what == "d":
                    r = EC // 128 // 2
                    src = e_down[one, c, :, half * r:(half + 1) * r, :].rearrange("o p r n -> (o p) r n")
                    sp.dma_start(slot(i, r, D), src).then_inc(s, 16)
                else:
                    k = KD // 2
                    src = (e_gate if what == "g" else e_up)[one, :, half * k:(half + 1) * k, c * EC:(c + 1) * EC].rearrange("o p k n -> (o p) k n")
                    sp.dma_start(slot(i, k, EC), src).then_inc(s, 16)

            def rest(e, rnd):
                for i in range(SLOTS, E_ITEMS):
                    if i != SLOTS + 1:
                        sp.wait_ge(low_ready, (e + NE * rnd) * E_PIECES + (MP0 + 2 * (max(i, SLOTS + 1) - SLOTS + 1)))
                    load(e, i)

            def first_of_next(e, k):
                for i in range(SLOTS):
                    before = i + SLOTS * (PER_EXPERT[i] - 1)
                    sp.wait_ge(low_ready, k * E_PIECES + (MP0 + 2 * (before + 1)))
                    load(e, i)

            def experts(rnd):
                with sp.Fori(0, NE - 1) as e:
                    rest(e, rnd)
                    first_of_next(e + 1, e + NE * rnd)
                rest(NE - 1, rnd)

            for i in range(SLOTS):
                n = MOE0 + i - SLOTS
                if n >= N0:
                    n -= SLOTS
                free(sp, n)
                load(0, i)
            experts(0)
            sp.wait_ge(over_ready, 1)
            more = sp.value_load(over[0:1, 0:1])
            with sp.If(more > 0):
                first_of_next(0, NE - 1)
                experts(1)
            sp.wait_ge(y_ready, 2)
            sp.dma_start(y_prompt, yout[:, 0:D]).then_inc(stored, 16)
            sp.wait_ge(y_ready, 4)
            sp.dma_start(y_sample, yout[:, D:2 * D]).then_inc(stored, 16)
            sp.wait_ge(stored, 16 * (2 + 2 * DEPTH))

        @block.gpsimd
        def _(pool):
            step = Steps(pool, pool_step)
            nc.gpsimd.memset(ones[:, :], 1.0).then_inc(ones_set, 1)
            pool.wait_ge(xT_done, 1)
            nc.gpsimd.memset(up, 0.0).then_inc(pads_set, 1)
            wa = win[:, 0, :].rearrange("p (g b t) -> p g b t", g=NG, b=2)
            wb = win[:, 1, :].rearrange("p (g b t) -> p g b t", g=NG, b=2)
            for l in range(DEPTH):
                pool.wait_ge(u_ready, l + 1)
                src = up
                for g, w in enumerate(POOL_WINDOWS):
                    dst = (wa, wb)[g % 2]
                    n = TP - w + 1
                    for gg in range(g, NG):
                        last = nc.gpsimd.tensor_tensor(dst[:, gg, :, 0:n], src[:, gg, :, 0:n], src[:, gg, :, w // 2:w // 2 + n], ALU.add)
                    step(last)
                    cnt = cst[:, C_CNT + g * 128:C_CNT + (g + 1) * 128]
                    for b in range(2):
                        last = nc.gpsimd.tensor_tensor(poolT[:, g, b * T:(b + 1) * T], dst[:, g, b, PAD - w // 2:PAD - w // 2 + T], cnt, ALU.mult)
                    step(last)
                    for b in range(2):
                        last = nc.gpsimd.tensor_tensor(poolT[:, g, b * T:(b + 1) * T], poolT[:, g, b * T:(b + 1) * T], up[:, g, b, PAD:PAD + T], ALU.subtract)
                    if g == NG - 1:
                        last.then_inc(pool_ready, 1)
                    else:
                        step(last)
                    src = dst

        @block.scalar
        def _(act):
            step = Steps(act, act_step)
            A = nc.scalar.activation
            act.dma_start(xin[:, 0, :], ins["x_prompt"].rearrange("b t d -> (b t) d")).then_inc(x_in, 16)
            act.dma_start(xin[:, 1, :], ins["x_sample"].rearrange("b t d -> (b t) d")).then_inc(x_in, 16)
            act.dma_start(wr[:, :, :], ins["moe_w_router"].rearrange("l (k p) n -> p (l k) n", p=128)).then_inc(router_in, 16)

            split = [0]

            def upto(q_end):
                for q in range(split[0], min(q_end, MP0)):
                    n = next(n for n in range(N0) if PIECE0[n + 1] > q)
                    half = q - PIECE0[n]
                    if half == 0:
                        act.wait_ge(in_slot[n % SLOTS], ARRIVED[n])
                    if q >= PIECES:
                        act.wait_ge(pieces_used, q - PIECES + 1)
                    raw = raw_piece(n, half)
                    A(next(halves(q, raw)), raw, ACT.Copy).then_inc(high_ready, 1)
                    split[0] = q + 1

            AHEAD = PIECES - 1

            act.wait_ge(vecT_ready, 1)
            A(silu_f[:, :, :].rearrange("p k c -> p c k"), vecT[:, V_CC:V_CC + 2 * KD].rearrange("p (c k) -> p c k", c=2), ACT.Silu).then_inc(silu_ready, 1)
            act.wait_ge(silu_ready, 1)
            A(silu_c[:, :, 0:2], silu_f[:, :, :], ACT.Copy).then_inc(siluh_ready, 1)

            def norm_a(t):
                act.wait_ge(x_ready, t + 1)
                A(sq[:, :, :], xT[:, :, :], ACT.Square).then_inc(sq_ready, 1)
                act.wait_ge(ms_ready, t + 1)
                A(rs[:, :], rs[:, :], ACT.Sqrt).then_inc(rt_ready, 1)

            def norm_b(t):
                for q in range(2):
                    act.wait_ge(h_ready, 2 * t + q + 1)
                    A(hx[:, 4 * q:4 * q + 4, 0, :], hT[:, 4 * q:4 * q + 4, :], ACT.Copy).then_inc(hxh_ready, 1)

            def take_rows(l, j):
                m = l * ADA_ITEMS + j
                act.wait_ge(pieces_used, end("ada", l, 2 * j + 1))
                if m:
                    act.wait_ge(modT_done, m)
                A(mrow[:, :], ps[0:4, rows_bank(l, j), :], ACT.Copy).then_inc(mrow_ready, 1)

            norm_a(0)
            for j in range(ADA_ITEMS):
                upto(end("ada", 0, 2 * j + 1) + AHEAD)
                take_rows(0, j)

            def mixer(l):
                if l:
                    upto(first("in", l, 0) + AHEAD)
                    norm_a(2 * l)
                norm_b(2 * l)
                upto(end("in", l, 2) + AHEAD)
                act.wait_ge(pieces_used, end("in", l, 2))
                A(cqT[:, 0:2, :], ps[:, 1, :], ACT.Copy)
                A(cqT[:, 2, :], ps[:, 2, 0:N2], ACT.Copy)
                A(kpe_raw, ps[:, 2, N2:2 * N2], ACT.Copy)
                step(A(rqk, ps[:, 3, :], ACT.Copy))
                A(sqqk[:, 0:KQ, :], cqT, ACT.Square)
                A(sqqk[:, KQ:, :], rqk, ACT.Square).then_inc(sqqk_ready, 1)
                upto(end("in", l, 4) + AHEAD)
                act.wait_ge(msqk_ready, l + 1)
                A(sqqk[:, 0:2, :], sqqk[:, 2:4, :], ACT.Sqrt).then_inc(rtqk_ready, 1)
                upto(end("in", l, 4) + PIECES)
                act.wait_ge(direct_used, 4 * l + DIRECT_USED["uq", 0])
                A(qT[:, 0:2, :], ps[:, 4, :], ACT.Copy)
                A(qT[:, 2:4, :], ps[:, 5, :], ACT.Copy)
                A(qpe, ps[:, 3, :], ACT.Copy).then_inc(qraw_ready, 1)
                act.wait_ge(direct_used, 4 * l + DIRECT_USED["ukv", 0])
                for h, b in enumerate((4, 5, 3, 1)):
                    last = A(kT[:, h, :], ps[:, b, 0:3 * 128], ACT.Copy)
                last.then_inc(k_ready, 1)
                act.wait_ge(nmx_ready, l + 1)
                for h in range(NH):
                    for b, (a, z) in enumerate(((0, T), (T, 3 * T))):
                        last = A(p[:, h, a:z], ps[:, 4 + h, a:z], ACT.Exp, bias=stat[:, 8 + 2 * h + b:9 + 2 * h + b],
                                 scale=SCALE, accum_out=stat[:, 16 + 2 * h + b:17 + 2 * h + b])
                last.then_inc(p_ready, 1)
                act.wait_ge(pT_done, l + 1)
                A(pT[:, 0, :], ps[:, 1, 0:3 * 128], ACT.Copy)
                A(pT[:, 1, :], ps[:, 2, 0:3 * 128], ACT.Copy).then_inc(pT_low_ready, 1)
                act.wait_ge(direct_used, 4 * l + DIRECT_USED["pool", 0])
                for g in range(NG):
                    last = A(hx[:, NH + g, 0, :], ps[:, 6 + g // 2, (g % 2) * N2:(g % 2 + 1) * N2], ACT.Copy, scale=vecT[:, V_PS + NG * l + g:V_PS + NG * l + g + 1])
                last.then_inc(pooledh_ready, 1)
                act.wait_ge(o_done, l + 1)
                A(hx[:, 0:2, 0, :], ps[:, 4, :].rearrange("p (h t) -> p h t", h=2), ACT.Copy)
                A(hx[:, 2:4, 0, :], ps[:, 5, :].rearrange("p (h t) -> p h t", h=2), ACT.Copy).then_inc(oh_ready, 1)
                upto(end("out", l, 3) + AHEAD)
                act.wait_ge(kv_outT_done, l + 1)
                A(kv_out[:, l, :], ps[:, 4, 0:KL + ROPE], ACT.Copy).then_inc(kv_out_ready, 1)
                act.wait_ge(kv_out_ready, l + 1)
                act.dma_start(new_ckv[0, l], kv_out[:, l, 0:KL]).then_inc(stored, 16)
                act.dma_start(new_kpe[0, l], kv_out[:, l, KL:KL + ROPE]).then_inc(stored, 16)
                upto(end("out", l, 3) + PIECES)
                norm_a(2 * l + 1)
                if l == 0:
                    norm_b(1)

            mixer(0)
            for c in range(FSTEPS):
                upto(end("gate", 0, c) + AHEAD)
                act.wait_ge(pieces_used, end("gate", 0, c))
                if c >= 2:
                    act.wait_ge(fh_ready, c - 1)
                A(fsg[:, c % 2, :], ps[:, 0, :], ACT.Silu).then_inc(fsg_ready, 1)
                upto(end("up", 0, c) + AHEAD)
                act.wait_ge(fh_ready, c + 1)
                if c >= 2:
                    act.wait_ge(pieces_used, end("down", 0, c - 2))
                A(fx[:, c % 2, :, 0, :], fh[:, c % 2, :].rearrange("p (k t) -> p k t", t=N2), ACT.Copy).then_inc(fxh_ready, 1)
                upto(end("ada", 1, 2 * c + 1) + AHEAD)
                take_rows(1, c)
            upto(end("ada", 1, 2 * FSTEPS + 1) + AHEAD)
            take_rows(1, FSTEPS)
            mixer(1)

            act.wait_ge(h2T_done, 1)
            A(h2[:, 0, 0:512], ps[:, 0, :], ACT.Copy)
            A(h2[:, 0, 512:1024], ps[:, 1, :], ACT.Copy)
            A(h2[:, 1, 0:512], ps[:, 2, :], ACT.Copy)
            A(h2[:, 1, 512:1024], ps[:, 3, :], ACT.Copy).then_inc(h2_ready, 1)
            act.wait_ge(top2_ready, 1)
            A(stat[:, 26:28], stat[:, 24:26], ACT.Exp).then_inc(e1_ready, 1)
            act.wait_ge(e1_ready, 1)
            A(stat[:, 28:29], stat[:, 0:1], ACT.Copy).then_inc(esg_ready, 1)

            def take_xg(n):
                act.wait_ge(gat_done, n)
                for q in range(2):
                    last = A(xg[:, 0, 4 * q:4 * q + 4, :], ps[:, 6 + q, :].rearrange("p (k t) -> p k t", k=4), ACT.Copy)
                last.then_inc(xgh_ready, 1)

            def take_Y():
                A(Y[:, 0:512], ps[:, 4, :], ACT.Copy)
                A(Y[:, 512:1024], ps[:, 5, :], ACT.Copy).then_inc(Y_ready, 1)

            def experts(rnd):
                take_xg(9 * rnd + 1)
                with act.Fori(0, NE) as e:
                    k = e + NE * rnd
                    done = [0]

                    def upto_e(z):
                        for i in range(done[0], min(z, E_PIECES)):
                            n, half = divmod(i, 2)
                            s = n % SLOTS
                            if half == 0:
                                act.wait_ge(in_slot[s], k * (16 * PER_EXPERT[s]) + (MOE_ARRIVED[s] + 16 * (n // SLOTS + 1)))
                            act.wait_ge(pieces_used, k * E_PIECES + (MP0 + i - PIECES + 1))
                            A(high[:, (MP0 + i) % PIECES, :], ring[:, s, half * PIECE:(half + 1) * PIECE], ACT.Copy).then_inc(high_ready, 1)
                            done[0] = i + 1

                    upto_e(AHEAD)
                    act.wait_ge(pieces_used, k * E_PIECES + MP0)
                    take_Y()
                    for c in range(ESTEPS + 1):
                        upto_e((piece_g(c) if c < ESTEPS else piece_d(c - 2)) + 4 + AHEAD)
                        if c:
                            act.wait_ge(ehT_done, k * ESTEPS + c)
                            A(hTm[:, 0, :, :], ps[:, 2, :].rearrange("p (r t) -> p r t", t=128), ACT.Copy).then_inc(ehTh_ready, 1)
                        if c < ESTEPS:
                            act.wait_ge(pieces_used, k * E_PIECES + (MP0 + piece_g(c) + 4))
                            act.wait_ge(eh_ready, k * ESTEPS + (c + 1))
                            A(sg[:, c % 2, :], ps[:, 0, :], ACT.Silu).then_inc(esg_ready, 1)
                    upto_e(E_PIECES)
                    take_xg(k + (rnd + 2))
                act.wait_ge(pieces_used, NE * (rnd + 1) * E_PIECES + MP0)
                take_Y()

            experts(0)
            act.wait_ge(over_ready, 1)
            more = act.value_load(over[0:1, 0:1])
            with act.If(more > 0):
                experts(1)
            norm_a(2 * DEPTH)
            act.wait_ge(outT_done, 1)
            for b in range(4):
                A(yout[:, b * 512:(b + 1) * 512], ps[:, 1 + b, :], ACT.Copy).then_inc(y_ready, 1)

        @block.vector
        def _(dve):
            step = Steps(dve, dve_step)
            V = nc.vector
            split = [0]
            AHEAD = PIECES - 1

            def upto(q_end):
                for q in range(split[0], min(q_end, MP0)):
                    n = next(n for n in range(N0) if PIECE0[n + 1] > q)
                    raw = raw_piece(n, q - PIECE0[n])
                    hi, lo = halves(q, raw)
                    dve.wait_ge(high_ready, q + 1)
                    V.tensor_tensor(lo, raw, hi, ALU.subtract).then_inc(low_ready, 1)
                    split[0] = q + 1

            dve.wait_ge(vecT_done, 1)
            V.tensor_copy(vecT[:, :], ps[:, 0, 0:128 + V_B_ROWS]).then_inc(vecT_ready, 1)
            dve.wait_ge(xT_done, 1)
            for b in range(2):
                for q in range(2):
                    last = V.tensor_copy(xT[:, 4 * q:4 * q + 4, b * T:(b + 1) * T], ps[:, 1 + 2 * b + q, :].rearrange("p (k t) -> p k t", k=4))
            last.then_inc(x_ready, 1)
            dve.wait_ge(siluh_ready, 1)
            V.tensor_tensor(silu_c[:, :, 2:4], silu_f[:, :, :], silu_c[:, :, 0:2], ALU.subtract).then_inc(silul_ready, 1)
            dve.wait_ge(vecT_ready, 1)

            def norm_a(t):
                dve.wait_ge(ss_done, t + 1)
                V.tensor_scalar(rs[:, :], ps[:, 0, 0:N2], 1.0 / D, EPS, ALU.mult, ALU.add).then_inc(ms_ready, 1)
                dve.wait_ge(rt_ready, t + 1)
                step(V.reciprocal(rs[:, :], rs[:, :]))
                if t == 2 * DEPTH:
                    for k in range(KD):
                        last = V.scalar_tensor_tensor(hT[:, k, :], xT[:, k, :], vecT[:, V_FIN + k:V_FIN + k + 1], rs[:, :], ALU.mult, ALU.mult)
                    last.then_inc(h_ready, 1)
                else:
                    step(V.tensor_tensor(hT[:, :, :], xT[:, :, :], rs[:, :].rearrange("p (o t) -> p o t", o=1).to_broadcast([128, KD, N2]), ALU.mult))

            def norm_b(t, halves_too=True):
                l, i = divmod(t, 2)
                for q in range(2):
                    for k in range(4 * q, 4 * q + 4):
                        for b in range(2):
                            x = hT[:, k, b * T:(b + 1) * T]
                            last = V.tensor_scalar(x, x, amod[:, l, i, k, b:b + 1], mod[:, l, 24 * i + k, b:b + 1], ALU.mult, ALU.add)
                    last.then_inc(h_ready, 1)
                if halves_too:
                    for q in range(2):
                        dve.wait_ge(hxh_ready, 2 * t + q + 1)
                        x = slice(4 * q, 4 * q + 4)
                        V.tensor_tensor(hx[:, x, 1, :], hT[:, x, :], hx[:, x, 0, :], ALU.subtract).then_inc(hx_ready, 1)

            def take_mod(l, j):
                dve.wait_ge(modT_done, l * ADA_ITEMS + j + 1)
                bias = vecT[:, V_BADA + 48 * l + 4 * j:V_BADA + 48 * l + 4 * j + 4].rearrange("p (m o) -> p m o", o=1).to_broadcast([128, 4, 2])
                V.tensor_tensor(mod[:, l, 4 * j:4 * j + 4, :], ps[:, turned_bank(l), 0:8].rearrange("p (m c) -> p m c", c=2), bias, ALU.add).then_inc(mod_ready, 1)

            def take_amod(l):
                dve.wait_ge(mod_ready, (l + 1) * ADA_ITEMS)
                for i, (sc, vg) in enumerate(((8, V_N1), (32, V_N2))):
                    g = vecT[:, vg + KD * l:vg + KD * (l + 1)].rearrange("p (m o) -> p m o", o=1).to_broadcast([128, KD, 2])
                    last = V.scalar_tensor_tensor(amod[:, l, i, :, :], mod[:, l, sc:sc + KD, :], 1.0, g, ALU.add, ALU.mult)
                last.then_inc(amod_ready, 1)
                dve.wait_ge(amod_ready, l + 1)

            norm_a(0)
            for j in range(ADA_ITEMS):
                upto(end("ada", 0, 2 * j + 1) + AHEAD)
                if j:
                    take_mod(0, j - 1)
            take_mod(0, ADA_ITEMS - 1)
            take_amod(0)

            def residual(l, i, k, src):
                for b in range(2):
                    x = xT[:, k, b * T:(b + 1) * T]
                    last = V.scalar_tensor_tensor(x, src(k, b), mod[:, l, 24 * i + 16 + k, b:b + 1], x, ALU.mult, ALU.add)
                if k == KD - 1:
                    last.then_inc(x_ready, 1)
                    dve.wait_ge(x_ready, 2 * l + i + 2)

            def mixer(l):
                dve.wait_ge(direct_used, 4 * l + DIRECT_USED["cache", 0])
                if l:
                    dve.wait_ge(pieces_used, end("down", 0, FSTEPS - 1))
                V.tensor_copy(ckvT[:, :, 2 * T:], ps[:, 3, 0:2 * PAST].rearrange("p (k t) -> p k t", k=KK))
                V.tensor_copy(kpeT[:, 2 * T:], ps[:, 3, 2 * PAST:3 * PAST]).then_inc(cacheT_ready, 1)
                if l:
                    upto(first("in", l, 0) + AHEAD)
                    norm_a(2 * l)
                norm_b(2 * l)
                upto(end("in", l, 4) + AHEAD)
                dve.wait_ge(pieces_used, end("in", l, 4))
                dve.wait_ge(pads_set, 1)
                if l:
                    dve.wait_ge(pool_ready, l)
                for i in range(2):
                    last = V.tensor_copy(up[:, 2 * i:2 * i + 2, :, PAD:PAD + T], ps[:, 4 + i, :].rearrange("p (g b t) -> p g b t", g=2, b=2))
                last.then_inc(u_ready, 1)
                dve.wait_ge(ssqk_done, l + 1)
                V.tensor_scalar(sqqk[:, 2, :], ps[:, 1, 0:N2], 1.0 / QL, EPS, ALU.mult, ALU.add)
                V.tensor_scalar(sqqk[:, 3, :], ps[:, 1, N2:2 * N2], 1.0 / KL, EPS, ALU.mult, ALU.add).then_inc(msqk_ready, 1)
                dve.wait_ge(kpe_rot_done, l + 1)
                V.tensor_copy(kpeT[:, 0:T], kpe_raw[:, 0:T])
                V.tensor_tensor(kpeT[:, T:2 * T], kpe_raw[:, T:2 * T], cst[:, C_COS:C_COS + T], ALU.mult)
                step(V.tensor_tensor(rope_t[:, 0, :], ps[:, 2, 0:T], cst[:, C_SIN:C_SIN + T], ALU.mult))
                V.tensor_tensor(kpeT[:, T:2 * T], kpeT[:, T:2 * T], rope_t[:, 0, :], ALU.add).then_inc(kpe_ready, 1)
                dve.wait_ge(rtqk_ready, l + 1)
                step(V.reciprocal(sqqk[:, 0:2, :], sqqk[:, 0:2, :]))
                for m in range(KQ):
                    V.scalar_tensor_tensor(cqT[:, m, :], cqT[:, m, :], vecT[:, V_QG + KQ * l + m:V_QG + KQ * l + m + 1], sqqk[:, 0, :], ALU.mult, ALU.mult)
                for m in range(KK):
                    last = V.scalar_tensor_tensor(ckvT[:, m, 0:N2], rqk[:, m, :], vecT[:, V_KG + KK * l + m:V_KG + KK * l + m + 1], sqqk[:, 1, :], ALU.mult, ALU.mult)
                last.then_inc(qkvn_ready, 1)
                upto(end("in", l, 4) + PIECES)
                dve.wait_ge(qpe_rot_done, l + 1)
                cos, sin = (cst[:, a:a + T].rearrange("p (o t) -> p o t", o=1).to_broadcast([128, 2, T]) for a in (C_COS, C_SIN))
                q2 = qpe
                V.tensor_tensor(q2[:, :, T:], q2[:, :, T:], cos, ALU.mult)
                step(V.tensor_tensor(rope_t, ps[:, 2, 0:N2].rearrange("p (j t) -> p j t", j=2), sin, ALU.mult))
                V.tensor_tensor(q2[:, :, T:], q2[:, :, T:], rope_t, ALU.add).then_inc(qpe_ready, 1)
                dve.wait_ge(direct_used, 4 * l + DIRECT_USED["ukv", 0])
                for i, b in enumerate((0, 6, 7)):
                    last = V.tensor_copy(v[:, i, :], ps[:, b, :])
                last.then_inc(v_ready, 1)
                dve.wait_ge(s_done, l + 1)
                mx = stat[:, 0:8].rearrange("p (h b) -> p h b", b=2)
                V.reduce_max(mx[:, :, 0], ps[:, 4:8, 0:T], AX.X)
                step(V.reduce_max(mx[:, :, 1], ps[:, 4:8, T:3 * T], AX.X))
                V.tensor_scalar(stat[:, 8:16], stat[:, 0:8], -SCALE, None, ALU.mult).then_inc(nmx_ready, 1)
                dve.wait_ge(p_ready, l + 1)
                step(V.reciprocal(stat[:, 16:24], stat[:, 16:24]))
                ri = stat[:, 16:24].rearrange("p (h b) -> p h b", b=2)
                V.tensor_tensor(p[:, :, 0:T], p[:, :, 0:T], ri[:, :, 0:1].to_broadcast([128, NH, T]), ALU.mult)
                V.tensor_tensor(p[:, :, T:], p[:, :, T:], ri[:, :, 1:2].to_broadcast([128, NH, 2 * T]), ALU.mult).then_inc(pn_ready, 1)
                dve.wait_ge(pT_done, l + 1)
                V.tensor_copy(pT[:, 2, :], ps[:, 3, 0:3 * 128])
                V.tensor_copy(pT[:, 3, :], ps[:, 0, 0:3 * 128]).then_inc(pT_high_ready, 1)
                dve.wait_ge(pooledh_ready, l + 1)
                for g in range(NG):
                    last = V.scalar_tensor_tensor(hx[:, NH + g, 1, :], ps[:, 6 + g // 2, (g % 2) * N2:(g % 2 + 1) * N2],
                                                  vecT[:, V_PS + NG * l + g:V_PS + NG * l + g + 1], hx[:, NH + g, 0, :], ALU.mult, ALU.subtract)
                last.then_inc(pooledl_ready, 1)
                dve.wait_ge(oh_ready, l + 1)
                for i in range(2):
                    last = V.tensor_tensor(hx[:, 2 * i:2 * i + 2, 1, :], ps[:, 4 + i, :].rearrange("p (h t) -> p h t", h=2), hx[:, 2 * i:2 * i + 2, 0, :], ALU.subtract)
                last.then_inc(ol_ready, 1)
                for j in range(4):
                    upto(end("out", l, j) + AHEAD)
                    dve.wait_ge(pieces_used, end("out", l, j))
                    for m in (2 * j, 2 * j + 1):
                        residual(l, 0, m, lambda k, b: ps[:, k // 2, (k % 2) * N2 + b * T:(k % 2) * N2 + (b + 1) * T])
                upto(end("out", l, 3) + PIECES)
                norm_a(2 * l + 1)
                norm_b(2 * l + 1, l == 0)

            mixer(0)
            for c in range(FSTEPS):
                upto(end("up", 0, c) + AHEAD)
                dve.wait_ge(pieces_used, end("up", 0, c))
                dve.wait_ge(fsg_ready, c + 1)
                V.tensor_tensor(fh[:, c % 2, :], fsg[:, c % 2, :], ps[:, 1, :], ALU.mult).then_inc(fh_ready, 1)
                dve.wait_ge(fxh_ready, c + 1)
                dve.wait_ge(fh_ready, c + 1)
                V.tensor_tensor(fx[:, c % 2, :, 1, :], fh[:, c % 2, :].rearrange("p (k t) -> p k t", t=N2), fx[:, c % 2, :, 0, :], ALU.subtract).then_inc(fx_ready, 1)
                if c:
                    upto(end("down", 0, c - 1) + AHEAD)
                    take_mod(1, c - 1)
                upto(end("ada", 1, 2 * c + 1) + AHEAD)
            upto(end("down", 0, FSTEPS - 1) + AHEAD)
            dve.wait_ge(pieces_used, end("down", 0, FSTEPS - 1))
            for k in range(KD):
                residual(0, 1, k, lambda k, b: ps[:, 2 + k // 2, (k % 2) * N2 + b * T:(k % 2) * N2 + (b + 1) * T])
            take_mod(1, FSTEPS - 1)
            upto(end("ada", 1, 2 * FSTEPS + 1) + AHEAD)
            take_mod(1, FSTEPS)
            take_amod(1)
            mixer(1)

            dve.wait_ge(logits_done, 1)
            lg = stat[:, 32:48].rearrange("p (b e) -> p b e", b=2)
            step(V.tensor_copy(lg, ps[:, 4, 0:16].rearrange("p (b e) -> p b e", b=2)))
            for b in range(2):
                last = V.max(rt8[:, b, :], lg[:, b, :])
            step(last)
            for b in range(2):
                V.max_index(rti[:, b, :], rt8[:, b, :], lg[:, b, :])
            last = V.tensor_tensor(stat[:, 24:26], rt8[:, :, 1], rt8[:, :, 0], ALU.subtract)
            last.then_inc(top2_ready, 1)
            dve.wait_ge(top2_ready, 1)
            step(V.tensor_copy(stat[:, 48:52].rearrange("p (b j) -> p b j", b=2), rti[:, :, 0:2]))
            iota8 = cst[:, C_IOTA:C_IOTA + NE]
            for b in range(2):
                for j in range(2):
                    last = V.tensor_scalar(oh[:, j, b, :], iota8, stat[:, 48 + 2 * b + j:49 + 2 * b + j], None, ALU.is_equal)
            step(last)
            V.tensor_tensor(oh[:, 2, :, :], oh[:, 0, :, :], oh[:, 1, :, :], ALU.add).then_inc(sel_ready, 1)
            dve.wait_ge(e1_ready, 1)
            step(V.tensor_scalar(stat[:, 52:54], stat[:, 26:28], 1.0, None, ALU.add))
            step(V.reciprocal(stat[:, 52:54], stat[:, 52:54]))
            step(V.tensor_tensor(stat[:, 54:56], stat[:, 52:54], stat[:, 26:28], ALU.mult))
            for b in range(2):
                last = V.tensor_scalar(oh[:, 0, b, :], oh[:, 0, b, :], stat[:, 52 + b:53 + b], None, ALU.mult)
            step(last)
            for b in range(2):
                last = V.scalar_tensor_tensor(oh[:, 3, b, :], oh[:, 1, b, :], stat[:, 54 + b:55 + b], oh[:, 0, b, :], ALU.mult, ALU.add)
            step(last)
            dve.wait_ge(rank_done, 1)
            step(V.scalar_tensor_tensor(oh[:, 0, :, :], ps[:, 5, 0:16].rearrange("p (b e) -> p b e", b=2), 1.0, oh[:, 2, :, :], ALU.add, ALU.mult))
            step(V.tensor_scalar(oh[:, 0, :, :], oh[:, 0, :, :], -1.0, None, ALU.add))
            step(V.reduce_max(stat[:, 56:57], ps[:, 5, 16:16 + NE], AX.X))
            step(V.tensor_scalar(stat[:, 57:58], stat[:, 56:57], OVER_LIMIT, None, ALU.is_gt))
            V.tensor_copy(over[:, :], stat[:, 57:58]).then_inc(over_ready, 1)
            V.memset(P[:, NE, :, :], 0.0)
            V.memset(PgT[:, 0, :, :], 0.0)
            V.memset(stat[:, 58:59], 0.0).then_inc(eh_ready, 1)
            V.memset(stat[:, 59:60], 0.0).then_inc(eh_ready, 1)
            V.memset(stat[:, 62:63], 0.0).then_inc(ehT_ready, 1)
            V.memset(acc[:, :, :], 0.0).then_inc(moe_zero, 1)
            dve.wait_ge(moe_zero, 1)

            def place(rnd):
                if rnd:
                    V.tensor_scalar(oh[:, 0, :, :], oh[:, 0, :, :], -128.0, None, ALU.add).then_inc(shift_ready, 1)
                    dve.wait_ge(shift_ready, rnd)
                iota = cst[:, C_IOTA:C_IOTA + 128]
                for e in range(NE):
                    for b in range(2):
                        V.tensor_scalar(P[:, e, b, :], iota, oh[:, 0, b, e:e + 1], None, ALU.is_equal)
                    if e or rnd:
                        dve.wait_ge(PgT_done, e + NE * rnd)
                        if e:
                            V.tensor_copy(PgT[:, e, :, :], ps[:, 6, 0:N2].rearrange("p (b t) -> p b t", b=2))
                    for b in range(2):
                        last = V.tensor_scalar(Pg[:, b, :], iota, oh[:, 0, b, e:e + 1], oh[:, 3, b, e:e + 1], ALU.is_equal, ALU.mult)
                    last.then_inc(Pg_ready, 1)
                dve.wait_ge(PgT_done, NE * (rnd + 1))
                V.tensor_copy(PgT[:, NE, :, :], ps[:, 6, 0:N2].rearrange("p (b t) -> p b t", b=2)).then_inc(PgT_ready, 1)

            def take_xg(n):
                dve.wait_ge(xgh_ready, n)
                for q in range(2):
                    x = slice(4 * q, 4 * q + 4)
                    last = V.tensor_tensor(xg[:, 1, x, :], ps[:, 6 + q, :].rearrange("p (k t) -> p k t", k=4), xg[:, 0, x, :], ALU.subtract)
                last.then_inc(xg_ready, 1)

            def add_up(done):
                for r, bank in enumerate(COMBINE_BANKS):
                    dve.wait_ge(cmb_done, done + (r + 1))
                    a = acc[:, 2 * r:2 * r + 2, :]
                    V.tensor_tensor(a, a, ps[:, bank, :].rearrange("p (k t) -> p k t", k=2), ALU.add).then_inc(acc_ready, 1)

            def experts(rnd):
                place(rnd)
                take_xg(9 * rnd + 1)
                with dve.Fori(0, NE) as e:
                    k = e + NE * rnd
                    done = [0]

                    def upto_e(z):
                        for i in range(done[0], min(z, E_PIECES)):
                            n, half = divmod(i, 2)
                            q = (MP0 + i) % PIECES
                            dve.wait_ge(high_ready, k * E_PIECES + (MP0 + i + 1))
                            V.tensor_tensor(low[:, q, :], ring[:, n % SLOTS, half * PIECE:(half + 1) * PIECE], high[:, q, :], ALU.subtract).then_inc(low_ready, 1)
                            done[0] = i + 1

                    def take_hT(c):
                        dve.wait_ge(ehTh_ready, k * ESTEPS + (c + 1))
                        V.tensor_tensor(hTm[:, 1, :, :], ps[:, 2, :].rearrange("p (r t) -> p r t", t=128), hTm[:, 0, :, :], ALU.subtract).then_inc(ehT_ready, 1)

                    for c in range(ESTEPS):
                        if c:
                            upto_e(piece_g(c) + 4 + AHEAD)
                            take_hT(c - 1)
                        upto_e(piece_u(c) + 4 + AHEAD)
                        dve.wait_ge(pieces_used, k * E_PIECES + (MP0 + piece_u(c) + 4))
                        dve.wait_ge(esg_ready, k * ESTEPS + (c + 2))
                        V.tensor_tensor(hm[:, c % 2, :], sg[:, c % 2, :], ps[:, 1, :], ALU.mult).then_inc(eh_ready, 1)
                        if c == 0:
                            add_up(k * 4 + 4 * rnd)
                    upto_e(piece_d(ESTEPS - 2) + 4 + AHEAD)
                    take_hT(ESTEPS - 1)
                    upto_e(E_PIECES)
                    take_xg(k + (rnd + 2))
                add_up(36 * rnd + 32)
                dve.wait_ge(acc_ready, 36 * (rnd + 1))

            experts(0)
            more = dve.value_load(over[0:1, 0:1])
            with dve.If(more > 0):
                experts(1)
            for k in range(KD):
                residual(1, 1, k, lambda k, b: acc[:, k, b * T:(b + 1) * T])
            norm_a(2 * DEPTH)

        @block.tensor
        def _(pe):
            mm = nc.tensor.matmul

            def arrived(kind, l, j):
                n = ITEM[kind, l, j]
                pe.wait_ge(in_slot[n % SLOTS], ARRIVED[n])
                return n

            def piece(q, k):
                pe.wait_ge(low_ready, q + 1)
                return tuple(t[:, q % PIECES, :].rearrange("p (k n) -> p k n", k=k) for t in (high, low))

            pe.wait_ge(small_in, 16 * 10)
            for a, r in ((0, 128), (1, V_B_ROWS)):
                last = nc.tensor.transpose(ps[:, 0, 128 * a:128 * a + r], vrow[0:r, a, :], ident[0:r, 0:r])
            last.then_inc(vecT_done, 1)
            pe.wait_ge(x_in, 32)
            for b in range(2):
                for k in range(KD):
                    last = nc.tensor.transpose(ps[:, 1 + 2 * b + k // 4, (k % 4) * 128:(k % 4 + 1) * 128], xin[:, b, k * 128:(k + 1) * 128], ident)
            last.then_inc(xT_done, 1)
            pe.wait_ge(ones_set, 1)

            def norm(t):
                pe.wait_ge(sq_ready, t + 1)
                if t == 0:
                    pe.wait_ge(vecT_ready, 1)
                for k in range(KD):
                    last = mm(ps[:, 0, 0:N2], ones[:, :], sq[:, k, :], start=k == 0, stop=k == KD - 1)
                last.then_inc(ss_done, 1)

            norm(0)
            pe.wait_ge(silul_ready, 1)

            def mod_rows(l, j):
                m = l * ADA_ITEMS + j
                if m >= 2 - l:
                    pe.wait_ge(mrow_ready, m - 1 + l)
                for q in range(4):
                    hi, lo = piece(first("ada", l, 2 * j) + q, 2)
                    for i in range(2):
                        for w in (hi, lo):
                            k = 2 * q + i
                            last = mm(ps[0:4, rows_bank(l, j), :], silu_c[:, k, :], w[:, i, :], start=q == 0 and i == 0 and w is hi, stop=q == 3 and i == 1 and w is lo)
                    last.then_inc(pieces_used, 1)

            def turn_mod(l, j):
                m = l * ADA_ITEMS + j
                pe.wait_ge(mrow_ready, m + 1)
                if m:
                    pe.wait_ge(mod_ready, m)
                for q in range(4):
                    last = mm(ps[:, turned_bank(l), 2 * q:2 * q + 2], mrow[:, q * 128:(q + 1) * 128], cst[0:4, C_SEL:C_SEL + 2], start=True, stop=True)
                last.then_inc(modT_done, 1)

            for j in range(ADA_ITEMS):
                mod_rows(0, j)
                if j:
                    turn_mod(0, j - 1)
            turn_mod(0, ADA_ITEMS - 1)

            def project(out, q, x, waits=None):
                hi, lo = piece(q, KD)
                for k in range(KD):
                    if waits and k % 4 == 0:
                        pe.wait_ge(hx_ready, waits + k // 4)
                    xh, xl = hx[:, k, 0, :], hx[:, k, 1, :]
                    mm(out, hi[:, k, :], xh, start=k == 0, stop=False)
                    mm(out, hi[:, k, :], xl, start=False, stop=False)
                    last = mm(out, lo[:, k, :], xh, start=False, stop=k == KD - 1)
                last.then_inc(pieces_used, 1)

            def half_bank(bank, half):
                return ps[:, bank, half * N2:(half + 1) * N2]

            def direct(out, ws, x):
                for k, w in enumerate(ws):
                    last = mm(out, w, x[:, k, :], start=k == 0, stop=k == len(ws) - 1)
                return last

            def mixer(l):
                cache = slot(arrived("cache", l, 0), 3, 128)
                if l == 0:
                    pe.wait_ge(x_ready, 1)
                else:
                    pe.wait_ge(x_ready, 2 * l + 1)
                for m in range(3):
                    last = nc.tensor.transpose(ps[:, 3, m * 128:(m + 1) * 128], cache[:, m, :], ident)
                last.then_inc(direct_used, 1)
                if l:
                    norm(2 * l)
                for i, (bank, half) in enumerate(((1, 0), (1, 1), (2, 0), (3, 0), (3, 1), (2, 1), (4, 0), (4, 1), (5, 0), (5, 1))):
                    if i == 3:
                        pe.wait_ge(cacheT_ready, l + 1)
                    project(half_bank(bank, half), first("in", l, 0) + i, None, (4 * l + 1) if i == 0 else None)
                pe.wait_ge(sqqk_ready, l + 1)
                for m in range(KQ):
                    mm(ps[:, 1, 0:N2], ones[:, :], sqqk[:, m, :], start=m == 0, stop=m == KQ - 1)
                for m in range(KK):
                    last = mm(ps[:, 1, N2:2 * N2], ones[:, :], sqqk[:, KQ + m, :], start=m == 0, stop=m == KK - 1)
                last.then_inc(ssqk_done, 1)
                rot = cst[:, C_ROT:C_ROT + 128]
                mm(ps[:, 2, 0:T], rot, kpe_raw[:, T:], start=True, stop=True).then_inc(kpe_rot_done, 1)
                pe.wait_ge(qkvn_ready, l + 1)
                pe.wait_ge(u_ready, l + 1)
                w0 = slot(arrived("uq", l, 0), 2, NH * (NOPE + ROPE))
                w1 = slot(arrived("uq", l, 1), 1, NH * (NOPE + ROPE))
                wq = [w0[:, 0, :], w0[:, 1, :], w1[:, 0, :]]
                for h in range(NH):
                    a = h * (NOPE + ROPE)
                    direct(half_bank(4 + h // 2, h % 2), [w[:, a:a + NOPE] for w in wq], cqT)
                for h in range(NH):
                    a, pp = h * (NOPE + ROPE) + NOPE, slice(64 * (h % 2), 64 * (h % 2) + 64)
                    last = direct(ps[pp, 3, h // 2 * N2:(h // 2 + 1) * N2], [w[:, a:a + ROPE] for w in wq], cqT)
                last.then_inc(direct_used, 1)
                pe.wait_ge(qraw_ready, l + 1)
                pe.wait_ge(kpe_ready, l + 1)
                q2 = qpe
                mm(ps[:, 2, 0:N2], rot, q2[:, :, T:], start=True, stop=True).then_inc(qpe_rot_done, 1)
                w = slot(arrived("ukv", l, 0), KK, NH * (NOPE + VD))
                for h, b in enumerate((4, 5, 3, 1)):
                    direct(ps[:, b, 0:3 * 128], [w[:, k, h * 256:h * 256 + NOPE] for k in range(KK)], ckvT)
                wv = w.rearrange("p k (h n) -> p k h n", h=NH)
                for i, b in enumerate((0, 6, 7)):
                    for k in range(KK):
                        last = mm(ps[:, b, :], ckvT[:, k, i * 128:(i + 1) * 128], wv[:, k, :, NOPE:], start=k == 0, stop=k == KK - 1)
                last.then_inc(direct_used, 1)
                pe.wait_ge(k_ready, l + 1)
                pe.wait_ge(v_ready, l + 1)
                pe.wait_ge(qpe_ready, l + 1)
                for h in range(NH):
                    pp = slice(64 * (h % 2), 64 * (h % 2) + 64)
                    for b, (a, z) in enumerate(((0, T), (T, 3 * T))):
                        mm(ps[:, 4 + h, a:z], qT[:, h, b * T:(b + 1) * T], kT[:, h, a:z], start=True, stop=False)
                        last = mm(ps[:, 4 + h, a:z], q2[pp, h // 2, b * T:(b + 1) * T], kpeT[pp, a:z], start=False, stop=True)
                last.then_inc(s_done, 1)
                pe.wait_ge(pn_ready, l + 1)
                for h, b in enumerate((1, 2, 3, 0)):
                    for i in range(3):
                        last = nc.tensor.transpose(ps[:, b, i * 128:(i + 1) * 128], p[:, h, i * 128:(i + 1) * 128], ident)
                last.then_inc(pT_done, 1)
                pe.wait_ge(pool_ready, l + 1)
                wp = slot(arrived("pool", l, 0), NG, 128)
                for g in range(NG):
                    last = mm(half_bank(6 + g // 2, g % 2), wp[:, g, :], poolT[:, g, :], start=True, stop=True)
                last.then_inc(direct_used, 1)
                pe.wait_ge(pT_low_ready, l + 1)
                pe.wait_ge(pT_high_ready, l + 1)
                for h in range(NH):
                    o = half_bank(4 + h // 2, h % 2)
                    vh = slice(h * VD, (h + 1) * VD)
                    mm(o[:, 0:T], v[:, 0, vh], pT[:, h, 0:128], start=True, stop=True)
                    mm(o[:, T:], v[:, 1, vh], pT[:, h, 128:256], start=True, stop=False)
                    last = mm(o[:, T:], v[:, 2, vh], pT[:, h, 256:384], start=False, stop=True)
                last.then_inc(o_done, 1)
                pe.wait_ge(pooledl_ready, l + 1)
                pe.wait_ge(ol_ready, l + 1)
                for m in range(KD):
                    project(half_bank(m // 2, m % 2), first("out", l, 0) + m, None)
                for m in range(KK):
                    nc.tensor.transpose(ps[:, 4, m * 128:(m + 1) * 128], ckvT[:, m, 0:T], ident)
                nc.tensor.transpose(ps[:, 4, KL:KL + ROPE], kpe_raw[0:ROPE, 0:T], ident[0:ROPE, 0:ROPE]).then_inc(kv_outT_done, 1)
                pe.wait_ge(x_ready, 2 * l + 2)
                norm(2 * l + 1)

            mixer(0)
            pe.wait_ge(kv_out_ready, 1)

            def ffn_down(c):
                pe.wait_ge(fx_ready, c + 1)
                for k in range(FC // 128):
                    hi, lo = piece(first("down", 0, c) + k, 1)
                    xh, xl = fx[:, c % 2, k, 0, :], fx[:, c % 2, k, 1, :]
                    for m in range(KD):
                        o = half_bank(2 + m // 2, m % 2)
                        a, z = c == 0 and k == 0 and m % 2 == 0, c == FSTEPS - 1 and k == FC // 128 - 1
                        mc = slice(m * 128, (m + 1) * 128)
                        mm(o, hi[:, 0, mc], xh, start=a, stop=False, skip_group_check=True)
                        mm(o, hi[:, 0, mc], xl, start=False, stop=False, skip_group_check=True)
                        last = mm(o, lo[:, 0, mc], xh, start=False, stop=z, skip_group_check=True)
                    last.then_inc(pieces_used, 1)

            for c in range(FSTEPS):
                for w, kind in enumerate(("gate", "up")):
                    if c:
                        pe.wait_ge((fsg_ready, fh_ready)[w], c)
                    for m in range(2):
                        project(half_bank(w, m), first(kind, 0, c) + m, None, 3 if c == 0 and w == 0 and m == 0 else None)
                if c:
                    ffn_down(c - 1)
                    turn_mod(1, c - 1)
                mod_rows(1, c)
            ffn_down(FSTEPS - 1)
            turn_mod(1, FSTEPS - 1)
            mod_rows(1, FSTEPS)
            turn_mod(1, FSTEPS)
            mixer(1)
            pe.wait_ge(h_ready, 2 * 3 + 2)
            pe.wait_ge(router_in, 16)

            for b in range(2):
                for k in range(KD):
                    last = nc.tensor.transpose(ps[:, 2 * b + k // 4, (k % 4) * 128:(k % 4 + 1) * 128], hT[:, k, b * T:(b + 1) * T], ident)
            last.then_inc(h2T_done, 1)
            pe.wait_ge(kv_out_ready, 2)
            for b in range(2):
                for k in range(KD):
                    last = mm(ps[:, 4, b * NE:(b + 1) * NE], hT[:, k, b * T:(b + 1) * T], wr[:, k, :], start=k == 0, stop=k == KD - 1)
            last.then_inc(logits_done, 1)
            pe.wait_ge(sel_ready, 1)
            tri = cst[:, C_TRI:C_TRI + 128]
            mm(ps[:, 5, 0:NE], tri, oh[:, 2, 0, :], start=True, stop=True)
            mm(ps[:, 5, NE:2 * NE], tri, oh[:, 2, 1, :], start=True, stop=False)
            mm(ps[:, 5, NE:2 * NE], ones[:, :], oh[:, 2, 0, :], start=False, stop=True)
            for b in range(2):
                last = mm(ps[:, 5, 2 * NE:3 * NE], ones[:, :], oh[:, 2, b, :], start=b == 0, stop=b == 1)
            last.then_inc(rank_done, 1)


            def gather(e):
                for m in range(KD):
                    for b in range(2):
                        rhs = P[:, e, b, :] if isinstance(e, int) else P[:, bass.ds(e, 1), b, :].rearrange("p o t -> p (o t)")
                        last = mm(ps[:, 6 + m // 4, (m % 4) * 128:(m % 4 + 1) * 128], h2[:, b, m * 128:(m + 1) * 128], rhs, start=b == 0, stop=b == 1)
                last.then_inc(gat_done, 1)

            def combine(e):
                for r, bank in enumerate(COMBINE_BANKS):
                    for q in range(2):
                        m = 2 * r + q
                        rhs = PgT[:, e, :, :] if isinstance(e, int) else PgT[:, bass.ds(e, 1), :, :].rearrange("p o b t -> p (o b) t")
                        last = mm(half_bank(bank, q), Y[:, m * 128:(m + 1) * 128], rhs, start=True, stop=True)
                    last.then_inc(cmb_done, 1)

            def experts(rnd):
                for e in range(NE):
                    pe.wait_ge(Pg_ready, e + 1 + NE * rnd)
                    for b in range(2):
                        last = nc.tensor.transpose(ps[:, 6, b * 128:(b + 1) * 128], Pg[:, b, :], ident)
                    last.then_inc(PgT_done, 1)
                pe.wait_ge(PgT_ready, rnd + 1)
                pe.wait_ge(h2_ready, 1)
                pe.wait_ge(moe_zero, 1)
                gather(0)
                with pe.Fori(0, NE) as e:
                    k = e + NE * rnd

                    def piece_e(i, kk):
                        pe.wait_ge(low_ready, k * E_PIECES + (MP0 + i + 1))
                        return tuple(t[:, (MP0 + i) % PIECES, :].rearrange("p (k n) -> p k n", k=kk) for t in (high, low))

                    def into_hidden(bank, i):
                        for q in range(4):
                            hi, lo = piece_e(i + q, 2)
                            for j in range(2):
                                kk = 2 * q + j
                                xh, xl = xg[:, 0, kk, :], xg[:, 1, kk, :]
                                mm(ps[:, bank, :], xh, hi[:, j, :], start=kk == 0, stop=False)
                                mm(ps[:, bank, :], xh, lo[:, j, :], start=False, stop=False)
                                last = mm(ps[:, bank, :], xl, hi[:, j, :], start=False, stop=kk == KD - 1)
                            last.then_inc(pieces_used, 1)

                    def turn(c):
                        pe.wait_ge(eh_ready, k * ESTEPS + (c + 3))
                        pe.wait_ge(ehT_ready, k * ESTEPS + (c + 1))
                        for r in range(EC // 128):
                            last = nc.tensor.transpose(ps[:, 2, r * 128:(r + 1) * 128], hm[:, c % 2, r:EC:EC // 128], ident)
                        last.then_inc(ehT_done, 1)

                    def down(c):
                        pe.wait_ge(ehT_ready, k * ESTEPS + (c + 2))
                        for r in range(EC // 128):
                            hi, lo = piece_e(piece_d(c) + r, 1)
                            xh, xl = hTm[:, 0, r, :], hTm[:, 1, r, :]
                            a, z = c == 0 and r == 0, c == ESTEPS - 1 and r == EC // 128 - 1
                            for half in range(2):
                                o, n = ps[:, 4 + half, :], slice(half * 512, (half + 1) * 512)
                                mm(o, xh, hi[:, 0, n], start=a, stop=False)
                                mm(o, xh, lo[:, 0, n], start=False, stop=False)
                                last = mm(o, xl, hi[:, 0, n], start=False, stop=z)
                            last.then_inc(pieces_used, 1)

                    pe.wait_ge(xg_ready, k + (rnd + 1))
                    for c in range(ESTEPS):
                        pe.wait_ge(esg_ready, k * ESTEPS + (c + 1))
                        into_hidden(0, piece_g(c))
                        if c == 1:
                            pe.wait_ge(acc_ready, k * 4 + (4 * rnd + 4))
                        if c:
                            turn(c - 1)
                        pe.wait_ge(eh_ready, k * ESTEPS + (c + 2))
                        into_hidden(1, piece_u(c))
                        if c:
                            down(c - 1)
                        else:
                            pe.wait_ge(Y_ready, k + (rnd + 1))
                            combine(e)
                    turn(ESTEPS - 1)
                    pe.wait_ge(acc_ready, k * 4 + (4 * rnd + 4))
                    gather(e + 1)
                    down(ESTEPS - 1)
                pe.wait_ge(Y_ready, 9 * (rnd + 1))
                pe.wait_ge(xg_ready, 9 * (rnd + 1))
                combine(NE)

            experts(0)
            pe.wait_ge(over_ready, 1)
            more = pe.value_load(over[0:1, 0:1])
            with pe.If(more > 0):
                experts(1)
            norm(2 * DEPTH)
            pe.wait_ge(h_ready, 2 * 2 * DEPTH + 1)
            for b in range(2):
                for k in range(KD):
                    last = nc.tensor.transpose(ps[:, 1 + 2 * b + k // 4, (k % 4) * 128:(k % 4 + 1) * 128], hT[:, k, b * T:(b + 1) * T], ident)
            last.then_inc(outT_done, 1)


OVER_LIMIT = 128.0
_INS = ["x_prompt", "x_sample", "c", "cache_ckv", "cache_kpe", "c_ctx", "norm1_g", "norm2_g", "w_ada", "b_ada", "w_in",
        "q_norm_g", "kv_norm_g", "w_uq", "w_ukv", "w_pool", "pool_scale", "w_out", "ffn_w_gate", "ffn_w_up", "ffn_w_down",
        "moe_w_router", "moe_w_gate", "moe_w_up", "moe_w_down", "final_norm_g"]
_OUTS = [(1, T, D), (1, T, D), (1, DEPTH, T, KL), (1, DEPTH, T, ROPE)]


def kernel(**inputs):
    import concourse.bacc as _bacc
    from concourse.bass_utils import run_bass_kernel_spmd as _run

    nc = _bacc.Bacc("TRN2", target_bir_lowering=False, num_devices=1)
    f32 = mybir.dt.float32
    arrays, aps = {}, {}
    for name in _INS:
        a = np.ascontiguousarray(inputs[name])
        arrays[f"in_{name}"] = a
        aps[name] = nc.dram_tensor(f"in_{name}", a.shape, f32, kind="ExternalInput").ap()
    arrays["in_constants"] = constants()
    consts = nc.dram_tensor("in_constants", (128, C_COLS), f32, kind="ExternalInput").ap()
    outs = [nc.dram_tensor(f"out_{i}", s, f32, kind="ExternalOutput").ap() for i, s in enumerate(_OUTS)]
    program(nc, aps, consts, outs[0].rearrange("b t d -> (b t) d"), outs[1].rearrange("b t d -> (b t) d"), outs[2], outs[3])
    r = _run(nc, [arrays], core_ids=[0])
    return tuple(r.results[0][f"out_{i}"] for i in range(len(_OUTS)))
```

```python
import numpy as np
import concourse.bass as bass
from concourse import mybir
from contextlib import ExitStack

D = 1024
T = 128
DEPTH = 2
PAST = 128
GRID_W = 64
NH = 4
NOPE = 128
ROPE = 64
VD = 128
QL = 384
KL = 256
POOL_WINDOWS = (2, 4, 8, 16)
NG = len(POOL_WINDOWS)
POOL_W = 512
FF = 2816
NE = 8
FE = 3584
EPS = 1e-6
ROPE_BASE = 10000.0

KD = D // 128
KQ = QL // 128
KK = KL // 128
N2 = 2 * T
ADA = 6 * D
ADA_COLS = 512
ADA_ITEMS = ADA // ADA_COLS
FC = 256
FSTEPS = FF // FC
EC = 512
ESTEPS = FE // EC
SLOTS = 7
SLOT = 2048
PIECE = 1024
PIECES = 7
E_ITEMS = 6 * ESTEPS
E_PIECES = 2 * E_ITEMS
assert E_PIECES % PIECES == 0
COMBINE_BANKS = (6, 7, 3, 2)
PAD = 8
TP = T + 2 * PAD

C_ID, C_ROT, C_COS, C_SIN, C_TRI, C_IOTA, C_CNT = (128 * i for i in range(7))
C_SEL = C_CNT + NG * 128
C_COLS = C_SEL + 2

V_BADA, V_N1, V_N2 = 0, 96, 112
V_FIN, V_PS, V_QG, V_KG, V_CC, V_C = (128 + i for i in (0, 8, 16, 22, 26, 34))
V_B_ROWS = 42


def constants():
    out = np.zeros((128, C_COLS), np.float32)
    out[:, C_ID:C_ID + 128] = np.eye(128)
    rot = np.zeros((128, 128), np.float32)
    q = ROPE // 4
    for base in range(0, 128, 2 * q):
        for i in range(q):
            rot[base + i, base + q + i] = -1.0
            rot[base + q + i, base + i] = 1.0
    out[:, C_ROT:C_ROT + 128] = rot.T
    t = np.arange(T)
    half = ROPE // 2
    freqs = (ROPE_BASE ** (-np.arange(0, half, 2, dtype=np.float32) / half)).astype(np.float32)
    ar = (t // GRID_W).astype(np.float32)[:, None] * freqs
    ac = (t % GRID_W).astype(np.float32)[:, None] * freqs
    ang = np.concatenate([ar, ar, ac, ac], axis=-1).T
    out[:, C_COS:C_COS + 128] = np.tile(np.cos(ang), (2, 1))
    out[:, C_SIN:C_SIN + 128] = np.tile(np.sin(ang), (2, 1))
    out[:, C_TRI:C_TRI + 128] = np.triu(np.ones((128, 128)), 1)
    out[:, C_IOTA:C_IOTA + 128] = np.arange(128)
    for g, w in enumerate(POOL_WINDOWS):
        cnt = np.minimum(t + w // 2, T) - np.maximum(t - w // 2, 0)
        out[:, C_CNT + g * 128:C_CNT + (g + 1) * 128] = (1.0 / cnt).astype(np.float32)
    out[0:4, C_SEL:C_SEL + 2] = np.tile(np.eye(2), (2, 1))
    return out


DIRECT = ("cache", "uq", "ukv", "pool")
IN_COLS = ((0, 256), (256, 512), (512, QL + KL + ROPE), (704, 960), (960, 1216))

ADA_PLACES = {
    ("start", 0): ((0, 1, 2, 3), (6, 7), 5),
    ("latents", 0): ((4, 5, 6), (6, 7), 0),
    ("softmax", 0): ((7,), (0, 1), 2),
    ("out", 0): ((8, 9), (6, 7), 5),
    ("norm2", 0): ((10, 11), (6, 7), 5),
    ("ffn", 1): ((12,), (6, 6), 7),
    ("ffn", 3): ((13,), (6, 6), 7),
    ("ffn", 5): ((14,), (6, 6), 7),
    ("norm1", 1): ((15, 16), (6, 1), 7),
    ("latents", 1): ((17, 18), (6, 7), 0),
    ("softmax", 1): ((19,), (0, 1), 2),
    ("out", 1): ((20, 21), (6, 7), 5),
    ("norm2", 1): ((22, 23), (6, 7), 5),
}
ADA_PLACE = {m: place for place, (blocks, _, _) in ADA_PLACES.items() for m in blocks}
assert sorted(ADA_PLACE) == list(range(DEPTH * ADA_ITEMS))


def blocks_at(*place):
    return ADA_PLACES[place][0] if place in ADA_PLACES else ()


def stream():
    def ada(*place):
        return [("ada",) + divmod(2 * m + i, 2 * ADA_ITEMS) for m in blocks_at(*place) for i in range(2)]

    out = ada("start", 0)
    for l in range(DEPTH):
        out += [("cache", l, 0)] + ada("norm1", l) + [("in", l, j) for j in range(5)]
        latents = ada("latents", l)
        out += latents[:-2] + [("uq", l, 0), ("uq", l, 1)] + latents[-2:] + [("ukv", l, 0)]
        out += ada("softmax", l) + [("pool", l, 0)]
        out += [("out", l, 0), ("out", l, 1)] + ada("out", l) + [("out", l, 2), ("out", l, 3)] + ada("norm2", l)
        if l == 0:
            for c in range(FSTEPS):
                out += [("gate", l, c), ("up", l, c)]
                if c:
                    out += [("down", l, c - 1)]
                out += ada("ffn", c)
            out += [("down", l, FSTEPS - 1)]
    return out


STREAM = stream()
ITEM = {x: n for n, x in enumerate(STREAM)}
N0 = len(STREAM)
MOE0 = -(-N0 // SLOTS) * SLOTS
PIECE0 = [2 * sum(x[0] not in DIRECT for x in STREAM[:n]) for n in range(N0 + 1)]
MP0 = PIECE0[N0]


def first(kind, l, j):
    return PIECE0[ITEM[kind, l, j]]


def end(kind, l, j):
    return PIECE0[ITEM[kind, l, j] + 1]


def ada_first(m):
    return first("ada", *divmod(2 * m, 2 * ADA_ITEMS))


def ada_end(m):
    return ada_first(m) + 4


TRANSFERS = {"cache": 3}
_count = [0] * SLOTS
ARRIVED = []
for _n, _x in enumerate(STREAM):
    _count[_n % SLOTS] += 16 * TRANSFERS.get(_x[0], 1)
    ARRIVED.append(_count[_n % SLOTS])
MOE_ARRIVED = list(_count)
PER_EXPERT = [len(range(s, E_ITEMS, SLOTS)) for s in range(SLOTS)]
DIRECT_USED = {("cache", 0): 1, ("uq", 0): 2, ("uq", 1): 2, ("ukv", 0): 3, ("pool", 0): 4}


def piece_g(c):
    return 0 if c == 0 else 12 * c - 4


def piece_u(c):
    return piece_g(c) + 4


def piece_d(c):
    return 12 * c + 16 if c < ESTEPS - 1 else E_PIECES - 4


def expert_item(i):
    for c in range(ESTEPS):
        for what, at in (("g", piece_g(c)), ("u", piece_u(c)), ("d", piece_d(c))):
            if 0 <= 2 * i - at < 4:
                return what, c, (2 * i - at) // 2


def program(nc, ins, consts, y_prompt, y_sample, new_ckv, new_kpe):
    f32 = mybir.dt.float32
    f32r = mybir.dt.float32r
    i32 = mybir.dt.int32
    u32 = mybir.dt.uint32
    ALU = mybir.AluOpType
    ACT = mybir.ActivationFunctionType
    AX = mybir.AxisListType
    SCALE = float(NOPE + ROPE) ** -0.5

    ctx = ExitStack()
    with ctx:
        place_at = [-(-nc.sbuf_base // 32) * 32]

        def sb(name, *shape, dt=f32):
            t = nc.alloc_sbuf_tensor_at(name, list(shape), dt, offset=place_at[0])
            place_at[0] += -(-4 * int(np.prod(shape[1:])) // 32) * 32
            return t

        def sem(name):
            return ctx.enter_context(nc.semaphore(name))

        ring = sb("ring", 128, SLOTS, SLOT)
        high = sb("high", 128, PIECES, PIECE, dt=f32r)
        low = sb("low", 128, PIECES, PIECE, dt=f32r)
        cst = sb("cst", 128, C_COLS)
        xT = sb("xT", 128, KD, N2)
        sq = sb("sq", 128, KD, N2)
        ones = sb("ones", 128, 128)
        vecT = sb("vecT", 128, 128 + V_B_ROWS)
        silu_f = sb("silu_f", 128, KD, 2)
        silu_c = sb("silu_c", 128, KD, 4, dt=f32r)
        mod = sb("mod", 128, DEPTH, 48, 2)
        amod = sb("amod", 128, DEPTH, 2, KD, 2)
        mrow = sb("mrow", 4, 2, ADA_COLS)
        rs = sb("rs", 128, N2)
        wr = sb("wr", 128, KD, NE)
        kv_out = sb("kv_out", 128, DEPTH, KL + ROPE)
        stat = sb("stat", 128, 64)
        rt8 = sb("rt8", 128, 2, 8)
        rti = sb("rti", 128, 2, 8, dt=u32)
        oh = sb("oh", 128, 4, 2, NE)
        over = sb("over", 128, 1, dt=i32)
        shared = place_at[0]
        hT = sq

        def words(*shape):
            return int(np.prod(shape))

        def view(t, at, *shape):
            a = t[:, at:at + words(*shape)]
            if len(shape) == 1:
                return a
            names = "abcd"[:len(shape)]
            return a.rearrange(f"p ({' '.join(names)}) -> p {' '.join(names)}", **dict(zip(names, shape)))

        hx = sb("hx", 128, KD, 2, N2, dt=f32r)
        hid = sb("hid", 128, 2 * NH * 3 * 128)
        arena_at = place_at[0]
        arena = sb("arena", 128, 9216)
        assert place_at[0] <= nc.sbuf_usable_end, (place_at[0], nc.sbuf_usable_end)
        at = [0]

        def cut(*shape):
            at[0] += words(*shape)
            assert at[0] <= 9216, at[0]
            return view(arena, at[0] - words(*shape), *shape)

        xin = view(arena, 0, 2, D)
        vrow = view(arena, 2 * D, 2, 128)
        cqT = cut(KQ, N2)
        ckvT = cut(KK, T + T + PAST)
        kpe_raw = cut(N2)
        kpeT = cut(T + T + PAST)
        sqqk = cut(KQ + KK, N2)
        rqk = cut(2, N2)
        qT = cut(NH, N2)
        qpe = cut(2, N2)
        qq = arena[:, at[0] - (NH + 2) * N2:at[0]]
        rope_t = cut(2, T)
        kT = view(hid, 0, NH, 3 * 128)
        v = view(hid, NH * 3 * 128, 3, NH * VD)
        p = qq.rearrange("p (h t) -> p h t", h=NH)
        pT = kT
        up = cut(NG, 2, TP)
        win = cut(2, NG * 2 * TP)
        poolT = sq[:, 0:NG, :]
        fsg, fh = view(hid, 0, 2, FC * 2), view(hid, 2 * FC * 2, 2, FC * 2)
        place_at[0] = arena_at
        fx = sb("fx", 128, 2, FC // 128, 2, N2, dt=f32r)
        place_at[0] = shared
        hTm = sb("hTm", 128, 2, EC // 128, 128, dt=f32r)
        xg = sb("xg", 128, 2, KD, 128, dt=f32r)
        ehid = sb("ehid", 128, 2, 2, EC)
        sg, hm = ehid[:, 0], ehid[:, 1]
        h2 = sb("h2", 128, 2, D)
        P = sb("P", 128, NE + 1, 2, 128)
        PgT = sb("PgT", 128, NE + 1, 2, 128)
        Y = sb("Y", 128, D)
        Pg = sb("Pg", 128, NE, 2, 128)
        yout = h2[:, :, :].rearrange("p b d -> p (b d)")
        acc = sq

        ps = ctx.enter_context(nc.psum_tensor("ps", [128, 8, 512], f32))

        in_slot = [sem(f"in_slot{i}") for i in range(SLOTS)]
        high_ready, low_ready, pieces_used, direct_used = (sem(x) for x in ("high_ready", "low_ready", "pieces_used", "direct_used"))
        small_in, x_in, router_in = sem("small_in"), sem("x_in"), sem("router_in")
        ones_set, pads_set = sem("ones_set"), sem("pads_set")
        vecT_done, vecT_ready = sem("vecT_done"), sem("vecT_ready")
        xT_done, x_ready = sem("xT_done"), sem("x_ready")
        silu_ready, siluh_ready, silul_ready = sem("silu_ready"), sem("siluh_ready"), sem("silul_ready")
        mrow_ready, modT_done, mod_ready, amod_ready = (sem(x) for x in ("mrow_ready", "modT_done", "mod_ready", "amod_ready"))
        sq_ready, ss_done, ms_ready, rt_ready = (sem(x) for x in ("sq_ready", "ss_done", "ms_ready", "rt_ready"))
        normed, h_ready, h_last_ready = sem("normed"), sem("h_ready"), sem("h_last_ready")
        hxh_ready, hx_ready = sem("hxh_ready"), sem("hx_ready")
        cacheT_ready, kv_done = sem("cacheT_ready"), sem("kv_done")
        u_ready, sqqk_ready, ssqk_done, kpe_rot_done = (sem(x) for x in ("u_ready", "sqqk_ready", "ssqk_done", "kpe_rot_done"))
        msqk_ready, rtqk_ready, qkvn_ready, kpe_ready = (sem(x) for x in ("msqk_ready", "rtqk_ready", "qkvn_ready", "kpe_ready"))
        qraw_ready, qpe_rot_done, qpe_ready = (sem(x) for x in ("qraw_ready", "qpe_rot_done", "qpe_ready"))
        k_ready, v_ready, s_done, nmx_ready, p_ready, pn_ready = (sem(x) for x in ("k_ready", "v_ready", "s_done", "nmx_ready", "p_ready", "pn_ready"))
        pT_done, pT_low_ready, pT_high_ready, o_done, oh_ready, ol_ready = (sem(x) for x in ("pT_done", "pT_low_ready", "pT_high_ready", "o_done", "oh_ready", "ol_ready"))
        pool_ready, pooledh_ready, pooledl_ready = (sem(x) for x in ("pool_ready", "pooledh_ready", "pooledl_ready"))
        kv_outT_done, kv_out_ready, stored = (sem(x) for x in ("kv_outT_done", "kv_out_ready", "stored"))
        fsg_ready, fh_ready, fxh_ready, fx_ready = (sem(x) for x in ("fsg_ready", "fh_ready", "fxh_ready", "fx_ready"))
        h2T_done, h2_ready, logits_done, sel_ready, rank_done = (sem(x) for x in ("h2T_done", "h2_ready", "logits_done", "sel_ready", "rank_done"))
        e1_ready, top2_ready = sem("e1_ready"), sem("top2_ready")
        P_ready, Pg_ready, PgT_done, PgT_first_ready, PgT_last_ready = (sem(x) for x in ("P_ready", "Pg_ready", "PgT_done", "PgT_first_ready", "PgT_last_ready"))
        moe_zero, over_ready, shift_ready = sem("moe_zero"), sem("over_ready"), sem("shift_ready")
        esg_ready, eh_ready, ehT_done, ehTh_ready, ehT_ready = (sem(x) for x in ("esg_ready", "eh_ready", "ehT_done", "ehTh_ready", "ehT_ready"))
        Y_ready, cmb_done, acc_ready = sem("Y_ready"), sem("cmb_done"), sem("acc_ready")
        gat_done, xgh_ready, xg_ready = sem("gat_done"), sem("xgh_ready"), sem("xg_ready")
        outT_done, y_first_ready, y_second_ready = (sem(x) for x in ("outT_done", "y_first_ready", "y_second_ready"))
        dve_step, act_step, pool_step = sem("dve_step"), sem("act_step"), sem("pool_step")

        ident = cst[:, C_ID:C_ID + 128]

        class Steps:

            def __init__(self, eng, semaphore):
                self.eng, self.sem, self.n = eng, semaphore, 0

            def __call__(self, instruction):
                self.n += 1
                instruction.then_inc(self.sem, 1)
                self.eng.wait_ge(self.sem, self.n)

        def slot(n, k, width):
            return ring[:, n % SLOTS, 0:k * width].rearrange("p (k n) -> p k n", k=k)

        def shape_of(kind, j):
            if kind == "in":
                return KD, IN_COLS[j][1] - IN_COLS[j][0]
            return {"ada": (KD // 2, ADA_COLS), "out": (KD, 256), "gate": (KD, FC), "up": (KD, FC), "down": (FC // 128, D)}[kind]

        def raw_piece(n, half):
            kind, _, j = STREAM[n]
            k, width = shape_of(kind, j)
            a = slot(n, k, width)
            if kind in ("ada", "down"):
                return a[:, half * k // 2:(half + 1) * k // 2, :]
            if kind == "in" and j == 2 and half:
                return a[:, :, 128:].rearrange("p k (o n) -> p k o n", o=1).to_broadcast([128, KD, 2, ROPE])
            return a[:, :, half * 128:(half + 1) * 128]

        def halves(q, like):
            for t in (high, low):
                a = t[:, q % PIECES, :]
                if len(like.shape) == 4:
                    yield a.rearrange("p (k o n) -> p k o n", k=KD, o=2)
                else:
                    yield a.rearrange("p (k n) -> p k n", k=like.shape[1])

        def free(eng, n):
            kind, l, j = STREAM[n]
            if kind in DIRECT:
                eng.wait_ge(direct_used, 4 * l + DIRECT_USED[kind, j])
            else:
                eng.wait_ge(low_ready, PIECE0[n + 1])

        def mod_rows_of(m):
            return ps[0:4, ADA_PLACES[ADA_PLACE[m]][1][m % 2], :]

        def mod_turned(m):
            return ps[:, ADA_PLACES[ADA_PLACE[m]][2], 0:8]

        TURNED_BANKS = (4, 5, 2, 3)

        block = ctx.enter_context(nc.Block())

        @block.sync
        def _(sp):
            def by_rows(name):
                return ins[name].rearrange("l (k p) n -> l p k n", p=128)

            w = {x: by_rows(y) for x, y in (("ada", "w_ada"), ("in", "w_in"), ("uq", "w_uq"), ("ukv", "w_ukv"), ("out", "w_out"),
                                            ("gate", "ffn_w_gate"), ("up", "ffn_w_up"), ("down", "ffn_w_down"))}
            e_gate = ins["moe_w_gate"].rearrange("l e (k p) n -> (l e) p k n", p=128)
            e_up = ins["moe_w_up"].rearrange("l e (k p) n -> (l e) p k n", p=128)
            e_down = ins["moe_w_down"].rearrange("l e (c p r) n -> (l e) c p r n", p=128, r=EC // 128)

            def rows(r, a):
                src = a.rearrange("(r p) -> r p", p=128) if len(a.shape) == 1 else a.rearrange("l (r p) -> (l r) p", p=128)
                sp.dma_start(vrow[r % 128:r % 128 + src.shape[0], r // 128, :], src).then_inc(small_in, 16)

            sp.dma_start(cst[:, :], consts).then_inc(small_in, 16)
            for r, name in ((V_CC, "c_ctx"), (V_C, "c"), (V_BADA, "b_ada"), (V_N1, "norm1_g"), (V_N2, "norm2_g"),
                            (V_FIN, "final_norm_g"), (V_PS, "pool_scale"), (V_QG, "q_norm_g"), (V_KG, "kv_norm_g")):
                rows(r, ins[name])

            for n, (kind, l, j) in enumerate(STREAM):
                if n >= SLOTS:
                    free(sp, n - SLOTS)
                s = in_slot[n % SLOTS]
                if kind == "cache":
                    sp.dma_start(ring[:, n % SLOTS, 0:KL], ins["cache_ckv"][0, l]).then_inc(s, 16)
                    for i in range(2):
                        sp.dma_start(ring[:, n % SLOTS, KL + i * ROPE:KL + (i + 1) * ROPE], ins["cache_kpe"][0, l]).then_inc(s, 16)
                elif kind == "pool":
                    sp.dma_start(slot(n, NG, 128), ins["w_pool"][l].rearrange("g c d -> c g d")).then_inc(s, 16)
                elif kind == "uq":
                    a, b = ((0, 2), (2, KQ))[j]
                    sp.dma_start(slot(n, b - a, NH * (NOPE + ROPE)), w["uq"][l][:, a:b, :]).then_inc(s, 16)
                elif kind == "ukv":
                    sp.dma_start(slot(n, KK, NH * (NOPE + VD)), w["ukv"][l]).then_inc(s, 16)
                elif kind == "ada":
                    b, half = divmod(j, 2)
                    sp.dma_start(slot(n, KD // 2, ADA_COLS), w["ada"][l][:, half * (KD // 2):(half + 1) * (KD // 2), b * ADA_COLS:(b + 1) * ADA_COLS]).then_inc(s, 16)
                elif kind == "down":
                    k = FC // 128
                    sp.dma_start(slot(n, k, D), w["down"][l // 2][:, j * k:(j + 1) * k, :]).then_inc(s, 16)
                else:
                    a, b = IN_COLS[j] if kind == "in" else (j * 256, (j + 1) * 256)
                    sp.dma_start(slot(n, KD, b - a), w[kind][l if kind in ("in", "out") else l // 2][:, :, a:b]).then_inc(s, 16)

            def load(e, i):
                what, c, half = expert_item(i)
                s = in_slot[i % SLOTS]
                one = slice(e, e + 1) if isinstance(e, int) else bass.ds(e, 1)
                if what == "d":
                    r = EC // 128 // 2
                    src = e_down[one, c, :, half * r:(half + 1) * r, :].rearrange("o p r n -> (o p) r n")
                    sp.dma_start(slot(i, r, D), src).then_inc(s, 16)
                else:
                    k = KD // 2
                    src = (e_gate if what == "g" else e_up)[one, :, half * k:(half + 1) * k, c * EC:(c + 1) * EC].rearrange("o p k n -> (o p) k n")
                    sp.dma_start(slot(i, k, EC), src).then_inc(s, 16)

            def rest(e, rnd):
                for i in range(SLOTS, E_ITEMS):
                    if i != SLOTS + 1:
                        sp.wait_ge(low_ready, (e + NE * rnd) * E_PIECES + (MP0 + 2 * (max(i, SLOTS + 1) - SLOTS + 1)))
                    load(e, i)

            def first_of_next(e, k):
                for i in range(SLOTS):
                    before = i + SLOTS * (PER_EXPERT[i] - 1)
                    sp.wait_ge(low_ready, k * E_PIECES + (MP0 + 2 * (before + 1)))
                    load(e, i)

            def experts(rnd):
                with sp.Fori(0, NE - 1) as e:
                    rest(e, rnd)
                    first_of_next(e + 1, e + NE * rnd)
                rest(NE - 1, rnd)

            for i in range(SLOTS):
                n = MOE0 + i - SLOTS
                if n >= N0:
                    n -= SLOTS
                free(sp, n)
                load(0, i)
            experts(0)
            sp.wait_ge(over_ready, 1)
            more = sp.value_load(over[0:1, 0:1])
            with sp.If(more > 0):
                first_of_next(0, NE - 1)
                experts(1)
            sp.wait_ge(y_first_ready, 1)
            sp.wait_ge(y_second_ready, 1)
            sp.dma_start(y_prompt, yout[:, 0:D]).then_inc(stored, 16)
            sp.wait_ge(y_first_ready, 2)
            sp.wait_ge(y_second_ready, 2)
            sp.dma_start(y_sample, yout[:, D:2 * D]).then_inc(stored, 16)
            sp.wait_ge(stored, 16 * (2 + 2 * DEPTH))

        @block.gpsimd
        def _(pool):
            step = Steps(pool, pool_step)
            nc.gpsimd.memset(ones[:, :], 1.0).then_inc(ones_set, 1)
            pool.wait_ge(xT_done, 1)
            nc.gpsimd.memset(up, 0.0).then_inc(pads_set, 1)
            wa = win[:, 0, :].rearrange("p (g b t) -> p g b t", g=NG, b=2)
            wb = win[:, 1, :].rearrange("p (g b t) -> p g b t", g=NG, b=2)
            for l in range(DEPTH):
                pool.wait_ge(u_ready, l + 1)
                src = up
                for g, w in enumerate(POOL_WINDOWS):
                    dst = (wa, wb)[g % 2]
                    n = TP - w + 1
                    for gg in range(g, NG):
                        last = nc.gpsimd.tensor_tensor(dst[:, gg, :, 0:n], src[:, gg, :, 0:n], src[:, gg, :, w // 2:w // 2 + n], ALU.add)
                    step(last)
                    cnt = cst[:, C_CNT + g * 128:C_CNT + (g + 1) * 128]
                    for b in range(2):
                        last = nc.gpsimd.tensor_tensor(poolT[:, g, b * T:(b + 1) * T], dst[:, g, b, PAD - w // 2:PAD - w // 2 + T], cnt, ALU.mult)
                    step(last)
                    for b in range(2):
                        last = nc.gpsimd.tensor_tensor(poolT[:, g, b * T:(b + 1) * T], poolT[:, g, b * T:(b + 1) * T], up[:, g, b, PAD:PAD + T], ALU.subtract)
                    if g == NG - 1:
                        last.then_inc(pool_ready, 1)
                    else:
                        step(last)
                    src = dst
            pool.wait_ge(h2T_done, 1)
            nc.gpsimd.memset(P[:, NE, :, :], 0.0)
            nc.gpsimd.memset(PgT[:, 0, :, :], 0.0)
            nc.gpsimd.memset(acc[:, :, :], 0.0).then_inc(moe_zero, 1)

        @block.scalar
        def _(act):
            step = Steps(act, act_step)
            A = nc.scalar.activation
            act.dma_start(xin[:, 0, :], ins["x_prompt"].rearrange("b t d -> (b t) d")).then_inc(x_in, 16)
            act.dma_start(xin[:, 1, :], ins["x_sample"].rearrange("b t d -> (b t) d")).then_inc(x_in, 16)
            act.dma_start(wr[:, :, :], ins["moe_w_router"].rearrange("l (k p) n -> p (l k) n", p=128)).then_inc(router_in, 16)

            split = [0]

            def upto(q_end):
                for q in range(split[0], min(q_end, MP0)):
                    n = next(n for n in range(N0) if PIECE0[n + 1] > q)
                    half = q - PIECE0[n]
                    if half == 0:
                        act.wait_ge(in_slot[n % SLOTS], ARRIVED[n])
                    if q >= PIECES:
                        act.wait_ge(pieces_used, q - PIECES + 1)
                    raw = raw_piece(n, half)
                    A(next(halves(q, raw)), raw, ACT.Copy).then_inc(high_ready, 1)
                    split[0] = q + 1

            AHEAD = PIECES - 1

            act.wait_ge(vecT_ready, 1)
            A(silu_f[:, :, :].rearrange("p k c -> p c k"), vecT[:, V_CC:V_CC + 2 * KD].rearrange("p (c k) -> p c k", c=2), ACT.Silu).then_inc(silu_ready, 1)
            act.wait_ge(silu_ready, 1)
            A(silu_c[:, :, 0:2], silu_f[:, :, :], ACT.Copy).then_inc(siluh_ready, 1)

            squared = [0]

            def squares(t, pairs):
                for r in pairs:
                    act.wait_ge(x_ready, 4 * t + r + 1)
                    A(sq[:, 2 * r:2 * r + 2, :], xT[:, 2 * r:2 * r + 2, :], ACT.Square).then_inc(sq_ready, 1)
                    squared[0] += 1

            def norm_a(t):
                squares(t, range(squared[0] - 4 * t, 4))
                act.wait_ge(ms_ready, t + 1)
                A(rs[:, :], rs[:, :], ACT.Sqrt).then_inc(rt_ready, 1)

            def norm_b(t, halves_too=True):
                l, i = divmod(t, 2)
                act.wait_ge(normed, 2 * t + 1)
                act.wait_ge(amod_ready, t + 1)
                for k in range(KD // 2, KD):
                    for b in range(2):
                        x = hT[:, k, b * T:(b + 1) * T]
                        last = A(x, x, ACT.Identity, bias=mod[:, l, 24 * i + k, b:b + 1], scale=amod[:, l, i, k, b:b + 1])
                last.then_inc(h_last_ready, 1)
                for q in range(2 if halves_too else 0):
                    act.wait_ge((h_ready, h_last_ready)[q], t + 1)
                    A(hx[:, 4 * q:4 * q + 4, 0, :], hT[:, 4 * q:4 * q + 4, :], ACT.Copy).then_inc(hxh_ready, 1)

            def take_rows(m):
                act.wait_ge(pieces_used, ada_end(m))
                if m >= 2:
                    act.wait_ge(modT_done, m - 1)
                A(mrow[:, m % 2, :], mod_rows_of(m), ACT.Copy).then_inc(mrow_ready, 1)

            for m in blocks_at("start", 0):
                if m == 2:
                    norm_a(0)
                upto(ada_end(m) + 2)
                if m == 0:
                    squares(0, range(4))
                take_rows(m)

            def mixer(l):
                if l:
                    upto(PIECE0[ITEM["cache", l, 0]] + AHEAD)
                    norm_a(2 * l)
                    take_rows(blocks_at("norm1", l)[0])
                    upto(ada_end(blocks_at("norm1", l)[1]))
                    norm_b(2 * l)
                    take_rows(blocks_at("norm1", l)[1])
                else:
                    norm_b(2 * l)
                upto(end("in", l, 2) + AHEAD)
                act.wait_ge(pieces_used, end("in", l, 2))
                A(cqT[:, 0:2, :], ps[:, 1, :], ACT.Copy)
                A(cqT[:, 2, :], ps[:, 2, 0:N2], ACT.Copy)
                A(kpe_raw, ps[:, 2, N2:2 * N2], ACT.Copy)
                step(A(rqk, ps[:, 3, :], ACT.Copy))
                A(sqqk[:, 0:KQ, :], cqT, ACT.Square)
                A(sqqk[:, KQ:, :], rqk, ACT.Square).then_inc(sqqk_ready, 1)
                upto(end("in", l, 4) + AHEAD)
                act.wait_ge(msqk_ready, l + 1)
                A(sqqk[:, 0:2, :], sqqk[:, 2:4, :], ACT.Sqrt).then_inc(rtqk_ready, 1)
                for m in blocks_at("latents", l)[:-1]:
                    upto(ada_end(m))
                    take_rows(m)
                upto(ada_end(blocks_at("latents", l)[-1]))
                act.wait_ge(direct_used, 4 * l + DIRECT_USED["uq", 0])
                A(qT[:, 0:2, :], ps[:, 4, :], ACT.Copy)
                A(qT[:, 2:4, :], ps[:, 5, :], ACT.Copy)
                A(qpe, ps[:, 3, :], ACT.Copy).then_inc(qraw_ready, 1)
                take_rows(blocks_at("latents", l)[-1])
                act.wait_ge(kv_done, 3 * l + 1)
                for h, b in enumerate((4, 5, 3, 1)):
                    last = A(kT[:, h, :], ps[:, b, 0:3 * 128], ACT.Copy)
                last.then_inc(k_ready, 1)
                upto(PIECE0[ITEM["ukv", l, 0]] + PIECES)
                act.wait_ge(nmx_ready, l + 1)
                for h in range(NH):
                    for b, (a, z) in enumerate(((0, T), (T, 3 * T))):
                        last = A(p[:, h, a:z], ps[:, 4 + h, a:z], ACT.Exp, bias=stat[:, 8 + 2 * h + b:9 + 2 * h + b],
                                 scale=SCALE, accum_out=stat[:, 16 + 2 * h + b:17 + 2 * h + b])
                last.then_inc(p_ready, 1)
                for m in blocks_at("softmax", l):
                    take_rows(m)
                act.wait_ge(pT_done, l + 1)
                A(pT[:, 0, :], ps[:, 1, 0:3 * 128], ACT.Copy)
                A(pT[:, 1, :], ps[:, 2, 0:3 * 128], ACT.Copy).then_inc(pT_low_ready, 1)
                act.wait_ge(direct_used, 4 * l + DIRECT_USED["pool", 0])
                for g in range(NG):
                    last = A(hx[:, NH + g, 0, :], ps[:, 6 + g // 2, (g % 2) * N2:(g % 2 + 1) * N2], ACT.Copy, scale=vecT[:, V_PS + NG * l + g:V_PS + NG * l + g + 1])
                last.then_inc(pooledh_ready, 1)
                act.wait_ge(o_done, l + 1)
                A(hx[:, 0:2, 0, :], ps[:, 4, :].rearrange("p (h t) -> p h t", h=2), ACT.Copy)
                A(hx[:, 2:4, 0, :], ps[:, 5, :].rearrange("p (h t) -> p h t", h=2), ACT.Copy).then_inc(oh_ready, 1)
                for m in blocks_at("out", l):
                    upto(ada_end(m) + AHEAD)
                    take_rows(m)
                for j in range(4):
                    upto(end("out", l, j) + AHEAD)
                    squares(2 * l + 1, (j,))
                act.wait_ge(kv_outT_done, l + 1)
                A(kv_out[:, l, :], ps[:, 4, 0:KL + ROPE], ACT.Copy).then_inc(kv_out_ready, 1)
                act.wait_ge(kv_out_ready, l + 1)
                act.dma_start(new_ckv[0, l], kv_out[:, l, 0:KL]).then_inc(stored, 16)
                act.dma_start(new_kpe[0, l], kv_out[:, l, KL:KL + ROPE]).then_inc(stored, 16)
                upto(end("out", l, 3) + PIECES)
                norm_a(2 * l + 1)
                upto(ada_end(blocks_at("norm2", l)[-1]))
                norm_b(2 * l + 1, l == 0)
                for m in blocks_at("norm2", l):
                    take_rows(m)

            mixer(0)
            for c in range(FSTEPS):
                upto(end("gate", 0, c) + AHEAD)
                act.wait_ge(pieces_used, end("gate", 0, c))
                if c >= 2:
                    act.wait_ge(fh_ready, c - 1)
                A(fsg[:, c % 2, :], ps[:, 0, :], ACT.Silu).then_inc(fsg_ready, 1)
                upto(end("up", 0, c) + AHEAD)
                act.wait_ge(fh_ready, c + 1)
                if c >= 2:
                    act.wait_ge(pieces_used, end("down", 0, c - 2))
                A(fx[:, c % 2, :, 0, :], fh[:, c % 2, :].rearrange("p (k t) -> p k t", t=N2), ACT.Copy).then_inc(fxh_ready, 1)
                for m in blocks_at("ffn", c):
                    upto(ada_end(m) + AHEAD)
                    take_rows(m)
            mixer(1)

            def split_e(k, a, z):
                for i in range(a, z):
                    n, half = divmod(i, 2)
                    s = n % SLOTS
                    if half == 0:
                        act.wait_ge(in_slot[s], k * (16 * PER_EXPERT[s]) + (MOE_ARRIVED[s] + 16 * (n // SLOTS + 1)))
                    act.wait_ge(pieces_used, k * E_PIECES + (MP0 + i - PIECES + 1))
                    A(high[:, (MP0 + i) % PIECES, :], ring[:, s, half * PIECE:(half + 1) * PIECE], ACT.Copy).then_inc(high_ready, 1)

            split_e(0, 0, AHEAD)
            act.wait_ge(top2_ready, 1)
            A(stat[:, 26:28], stat[:, 24:26], ACT.Exp).then_inc(e1_ready, 1)
            act.wait_ge(e1_ready, 1)
            A(stat[:, 28:29], stat[:, 24:25], ACT.Silu).then_inc(esg_ready, 1)
            act.wait_ge(h2T_done, 1)
            A(h2[:, 0, 0:512], ps[:, 0, :], ACT.Copy)
            A(h2[:, 0, 512:1024], ps[:, 1, :], ACT.Copy)
            A(h2[:, 1, 0:512], ps[:, 2, :], ACT.Copy)
            A(h2[:, 1, 512:1024], ps[:, 3, :], ACT.Copy).then_inc(h2_ready, 1)

            def take_xg(n):
                act.wait_ge(gat_done, n)
                for q in range(2):
                    last = A(xg[:, 0, 4 * q:4 * q + 4, :], ps[:, 6 + q, :].rearrange("p (k t) -> p k t", k=4), ACT.Copy)
                last.then_inc(xgh_ready, 1)

            def take_Y():
                A(Y[:, 0:512], ps[:, 4, :], ACT.Copy)
                A(Y[:, 512:1024], ps[:, 5, :], ACT.Copy).then_inc(Y_ready, 1)

            def experts(rnd):
                if rnd:
                    split_e(NE * rnd, 0, AHEAD)
                take_xg(9 * rnd + 1)
                act.wait_ge(PgT_done, rnd + 1)
                for i in (0, 1):
                    last = A(PgT[:, 2 * i + 1:2 * i + 3, :, :], ps[:, TURNED_BANKS[i], :].rearrange("p (e b t) -> p e b t", e=2, b=2), ACT.Copy)
                last.then_inc(PgT_first_ready, 1)
                def expert(e):
                    k = e + NE * rnd
                    done = [AHEAD]
                    more = AHEAD if not isinstance(e, int) else 0

                    def upto_e(z):
                        z = max(done[0], min(z, E_PIECES + more))
                        split_e(k, done[0], z)
                        done[0] = z

                    act.wait_ge(pieces_used, k * E_PIECES + MP0)
                    take_Y()
                    for c in range(ESTEPS + 1):
                        upto_e((piece_g(c) if c < ESTEPS else piece_d(c - 2)) + 4 + AHEAD)
                        if c:
                            act.wait_ge(ehT_done, k * ESTEPS + c)
                            A(hTm[:, 0, :, :], ps[:, 2, :].rearrange("p (r t) -> p r t", t=128), ACT.Copy).then_inc(ehTh_ready, 1)
                        if c < ESTEPS:
                            act.wait_ge(pieces_used, k * E_PIECES + (MP0 + piece_g(c) + 4))
                            act.wait_ge(eh_ready, k * ESTEPS + (c + 1))
                            A(sg[:, c % 2, :], ps[:, 0, :], ACT.Silu).then_inc(esg_ready, 1)
                    upto_e(E_PIECES)
                    take_xg(k + (rnd + 2))
                    upto_e(E_PIECES + AHEAD)

                with act.Fori(0, NE - 1) as e:
                    expert(e)
                expert(NE - 1)
                act.wait_ge(pieces_used, NE * (rnd + 1) * E_PIECES + MP0)
                take_Y()

            experts(0)
            act.wait_ge(over_ready, 1)
            more = act.value_load(over[0:1, 0:1])
            with act.If(more > 0):
                experts(1)
            norm_a(2 * DEPTH)
            act.wait_ge(outT_done, 1)
            for b in range(2):
                A(yout[:, b * D:b * D + 512], ps[:, 1 + 2 * b, :], ACT.Copy).then_inc(y_first_ready, 1)

        @block.vector
        def _(dve):
            step = Steps(dve, dve_step)
            V = nc.vector
            split = [0]
            AHEAD = PIECES - 1

            def upto(q_end):
                for q in range(split[0], min(q_end, MP0)):
                    n = next(n for n in range(N0) if PIECE0[n + 1] > q)
                    raw = raw_piece(n, q - PIECE0[n])
                    hi, lo = halves(q, raw)
                    dve.wait_ge(high_ready, q + 1)
                    V.tensor_tensor(lo, raw, hi, ALU.subtract).then_inc(low_ready, 1)
                    split[0] = q + 1

            dve.wait_ge(vecT_done, 1)
            V.tensor_copy(vecT[:, :], ps[:, 0, 0:128 + V_B_ROWS]).then_inc(vecT_ready, 1)
            dve.wait_ge(xT_done, 1)
            for q in range(2):
                for b in range(2):
                    last = V.tensor_copy(xT[:, 4 * q:4 * q + 4, b * T:(b + 1) * T], ps[:, 1 + 2 * b + q, :].rearrange("p (k t) -> p k t", k=4))
            last.then_inc(x_ready, 4)
            dve.wait_ge(siluh_ready, 1)
            V.tensor_tensor(silu_c[:, :, 2:4], silu_f[:, :, :], silu_c[:, :, 0:2], ALU.subtract).then_inc(silul_ready, 1)
            dve.wait_ge(vecT_ready, 1)

            def norm_a(t):
                dve.wait_ge(ss_done, t + 1)
                V.tensor_scalar(rs[:, :], ps[:, 0, 0:N2], 1.0 / D, EPS, ALU.mult, ALU.add).then_inc(ms_ready, 1)
                dve.wait_ge(rt_ready, t + 1)
                step(V.reciprocal(rs[:, :], rs[:, :]))
                if t == 2 * DEPTH:
                    for k in range(KD):
                        V.scalar_tensor_tensor(hT[:, k, :], xT[:, k, :], vecT[:, V_FIN + k:V_FIN + k + 1], rs[:, :], ALU.mult, ALU.mult).then_inc(h_ready, 1)
                else:
                    for q in (1, 0):
                        x = slice(4 * q, 4 * q + 4)
                        V.tensor_tensor(hT[:, x, :], xT[:, x, :], rs[:, :].rearrange("p (o t) -> p o t", o=1).to_broadcast([128, 4, N2]), ALU.mult).then_inc(normed, 1)
                    dve.wait_ge(normed, 2 * t + 2)

            def norm_b(t, blocks, halves_too=True):
                l, i = divmod(t, 2)
                for k in range(KD // 2):
                    for b in range(2):
                        x = hT[:, k, b * T:(b + 1) * T]
                        last = V.tensor_scalar(x, x, amod[:, l, i, k, b:b + 1], mod[:, l, 24 * i + k, b:b + 1], ALU.mult, ALU.add)
                last.then_inc(h_ready, 1)
                if blocks:
                    upto(ada_end(blocks[-1]))
                if halves_too:
                    for q in range(2):
                        dve.wait_ge(hxh_ready, 2 * t + q + 1)
                        x = slice(4 * q, 4 * q + 4)
                        V.tensor_tensor(hx[:, x, 1, :], hT[:, x, :], hx[:, x, 0, :], ALU.subtract).then_inc(hx_ready, 1)

            def take_mod(m):
                l, j = divmod(m, ADA_ITEMS)
                dve.wait_ge(modT_done, m + 1)
                bias = vecT[:, V_BADA + 48 * l + 4 * j:V_BADA + 48 * l + 4 * j + 4].rearrange("p (m o) -> p m o", o=1).to_broadcast([128, 4, 2])
                V.tensor_tensor(mod[:, l, 4 * j:4 * j + 4, :], mod_turned(m).rearrange("p (m c) -> p m c", c=2), bias, ALU.add).then_inc(mod_ready, 1)

            def take_amod(l, i):
                dve.wait_ge(mod_ready, l * ADA_ITEMS + 6 * i + 4)
                sc, vg = ((8, V_N1), (32, V_N2))[i]
                g = vecT[:, vg + KD * l:vg + KD * (l + 1)].rearrange("p (m o) -> p m o", o=1).to_broadcast([128, KD, 2])
                V.scalar_tensor_tensor(amod[:, l, i, :, :], mod[:, l, sc:sc + KD, :], 1.0, g, ALU.add, ALU.mult).then_inc(amod_ready, 1)
                dve.wait_ge(amod_ready, 2 * l + i + 1)

            for m in blocks_at("start", 0):
                if m == 2:
                    norm_a(0)
                upto(ada_end(m) + 2)
                if m:
                    take_mod(m - 1)
            take_mod(blocks_at("start", 0)[-1])
            take_amod(0, 0)

            def residual(l, i, k, src):
                for b in range(2):
                    x = xT[:, k, b * T:(b + 1) * T]
                    last = V.scalar_tensor_tensor(x, src(k, b), mod[:, l, 24 * i + 16 + k, b:b + 1], x, ALU.mult, ALU.add)
                if k % 2:
                    last.then_inc(x_ready, 1)
                if k == KD - 1:
                    dve.wait_ge(x_ready, 4 * (2 * l + i + 2))

            def mixer(l):
                if l:
                    upto(PIECE0[ITEM["cache", l, 0]] + AHEAD)
                    norm_a(2 * l)
                    take_mod(blocks_at("norm1", l)[0])
                    take_amod(l, 0)
                norm_b(2 * l, blocks_at("norm1", l))
                dve.wait_ge(direct_used, 4 * l + DIRECT_USED["cache", 0])
                if l:
                    dve.wait_ge(pieces_used, end("down", 0, FSTEPS - 1))
                V.tensor_copy(ckvT[:, :, 2 * T:], ps[:, 3, 0:2 * PAST].rearrange("p (k t) -> p k t", k=KK))
                V.tensor_copy(kpeT[:, 2 * T:], ps[:, 3, 2 * PAST:3 * PAST]).then_inc(cacheT_ready, 1)
                if l:
                    upto(end("in", l, 0) + 3)
                    take_mod(blocks_at("norm1", l)[1])
                upto(end("in", l, 4) + AHEAD)
                dve.wait_ge(pieces_used, end("in", l, 4))
                dve.wait_ge(pads_set, 1)
                if l:
                    dve.wait_ge(pool_ready, l)
                for i in range(2):
                    last = V.tensor_copy(up[:, 2 * i:2 * i + 2, :, PAD:PAD + T], ps[:, 4 + i, :].rearrange("p (g b t) -> p g b t", g=2, b=2))
                last.then_inc(u_ready, 1)
                dve.wait_ge(ssqk_done, l + 1)
                V.tensor_scalar(sqqk[:, 2, :], ps[:, 1, 0:N2], 1.0 / QL, EPS, ALU.mult, ALU.add)
                V.tensor_scalar(sqqk[:, 3, :], ps[:, 1, N2:2 * N2], 1.0 / KL, EPS, ALU.mult, ALU.add).then_inc(msqk_ready, 1)
                dve.wait_ge(kpe_rot_done, l + 1)
                V.tensor_copy(kpeT[:, 0:T], kpe_raw[:, 0:T])
                V.tensor_tensor(kpeT[:, T:2 * T], kpe_raw[:, T:2 * T], cst[:, C_COS:C_COS + T], ALU.mult)
                step(V.tensor_tensor(rope_t[:, 0, :], ps[:, 2, 0:T], cst[:, C_SIN:C_SIN + T], ALU.mult))
                V.tensor_tensor(kpeT[:, T:2 * T], kpeT[:, T:2 * T], rope_t[:, 0, :], ALU.add).then_inc(kpe_ready, 1)
                dve.wait_ge(rtqk_ready, l + 1)
                step(V.reciprocal(sqqk[:, 0:2, :], sqqk[:, 0:2, :]))
                for m in range(KQ):
                    V.scalar_tensor_tensor(cqT[:, m, :], cqT[:, m, :], vecT[:, V_QG + KQ * l + m:V_QG + KQ * l + m + 1], sqqk[:, 0, :], ALU.mult, ALU.mult)
                for m in range(KK):
                    last = V.scalar_tensor_tensor(ckvT[:, m, 0:N2], rqk[:, m, :], vecT[:, V_KG + KK * l + m:V_KG + KK * l + m + 1], sqqk[:, 1, :], ALU.mult, ALU.mult)
                last.then_inc(qkvn_ready, 1)
                for m in blocks_at("latents", l)[:-1]:
                    upto(ada_end(m + 1))
                    take_mod(m)
                dve.wait_ge(qpe_rot_done, l + 1)
                cos, sin = (cst[:, a:a + T].rearrange("p (o t) -> p o t", o=1).to_broadcast([128, 2, T]) for a in (C_COS, C_SIN))
                q2 = qpe
                V.tensor_tensor(q2[:, :, T:], q2[:, :, T:], cos, ALU.mult)
                step(V.tensor_tensor(rope_t, ps[:, 2, 0:N2].rearrange("p (j t) -> p j t", j=2), sin, ALU.mult))
                V.tensor_tensor(q2[:, :, T:], q2[:, :, T:], rope_t, ALU.add).then_inc(qpe_ready, 1)
                take_mod(blocks_at("latents", l)[-1])
                for i, b in enumerate((0, 6, 7)):
                    if i < 2:
                        dve.wait_ge(kv_done, 3 * l + 2 + i)
                    else:
                        dve.wait_ge(direct_used, 4 * l + DIRECT_USED["ukv", 0])
                    last = V.tensor_copy(v[:, i, :], ps[:, b, :])
                last.then_inc(v_ready, 1)
                upto(PIECE0[ITEM["ukv", l, 0]] + 4)
                dve.wait_ge(s_done, l + 1)
                mx = stat[:, 0:8].rearrange("p (h b) -> p h b", b=2)
                V.reduce_max(mx[:, :, 0], ps[:, 4:8, 0:T], AX.X)
                step(V.reduce_max(mx[:, :, 1], ps[:, 4:8, T:3 * T], AX.X))
                V.tensor_scalar(stat[:, 8:16], stat[:, 0:8], -SCALE, None, ALU.mult).then_inc(nmx_ready, 1)
                dve.wait_ge(p_ready, l + 1)
                step(V.reciprocal(stat[:, 16:24], stat[:, 16:24]))
                ri = stat[:, 16:24].rearrange("p (h b) -> p h b", b=2)
                V.tensor_tensor(p[:, :, 0:T], p[:, :, 0:T], ri[:, :, 0:1].to_broadcast([128, NH, T]), ALU.mult)
                V.tensor_tensor(p[:, :, T:], p[:, :, T:], ri[:, :, 1:2].to_broadcast([128, NH, 2 * T]), ALU.mult).then_inc(pn_ready, 1)
                for m in blocks_at("softmax", l):
                    take_mod(m)
                upto(PIECE0[ITEM["ukv", l, 0]] + PIECES)
                dve.wait_ge(pT_done, l + 1)
                V.tensor_copy(pT[:, 2, :], ps[:, 3, 0:3 * 128])
                V.tensor_copy(pT[:, 3, :], ps[:, 0, 0:3 * 128]).then_inc(pT_high_ready, 1)
                dve.wait_ge(pooledh_ready, l + 1)
                for g in range(NG):
                    last = V.scalar_tensor_tensor(hx[:, NH + g, 1, :], ps[:, 6 + g // 2, (g % 2) * N2:(g % 2 + 1) * N2],
                                                  vecT[:, V_PS + NG * l + g:V_PS + NG * l + g + 1], hx[:, NH + g, 0, :], ALU.mult, ALU.subtract)
                last.then_inc(pooledl_ready, 1)
                dve.wait_ge(oh_ready, l + 1)
                for i in range(2):
                    last = V.tensor_tensor(hx[:, 2 * i:2 * i + 2, 1, :], ps[:, 4 + i, :].rearrange("p (h t) -> p h t", h=2), hx[:, 2 * i:2 * i + 2, 0, :], ALU.subtract)
                last.then_inc(ol_ready, 1)
                for j in range(4):
                    upto(end("out", l, j) + AHEAD)
                    if j == 2:
                        for m in blocks_at("out", l)[:-1]:
                            take_mod(m)
                    dve.wait_ge(pieces_used, end("out", l, j))
                    for m in (2 * j, 2 * j + 1):
                        residual(l, 0, m, lambda k, b: ps[:, k // 2, (k % 2) * N2 + b * T:(k % 2) * N2 + (b + 1) * T])
                for m in blocks_at("out", l)[-1:]:
                    take_mod(m)
                take_amod(l, 1)
                upto(end("out", l, 3) + PIECES)
                norm_a(2 * l + 1)
                norm_b(2 * l + 1, blocks_at("norm2", l), l == 0)
                if l == 0:
                    upto(end("gate", 0, 0))
                for m in blocks_at("norm2", l):
                    take_mod(m)

            mixer(0)
            for c in range(FSTEPS):
                upto(end("up", 0, c) + AHEAD)
                dve.wait_ge(pieces_used, end("up", 0, c))
                dve.wait_ge(fsg_ready, c + 1)
                V.tensor_tensor(fh[:, c % 2, :], fsg[:, c % 2, :], ps[:, 1, :], ALU.mult).then_inc(fh_ready, 1)
                dve.wait_ge(fxh_ready, c + 1)
                dve.wait_ge(fh_ready, c + 1)
                V.tensor_tensor(fx[:, c % 2, :, 1, :], fh[:, c % 2, :].rearrange("p (k t) -> p k t", t=N2), fx[:, c % 2, :, 0, :], ALU.subtract).then_inc(fx_ready, 1)
                if c:
                    upto(end("down", 0, c - 1) + AHEAD)
                    for m in blocks_at("ffn", c - 1):
                        take_mod(m)
                for m in blocks_at("ffn", c):
                    upto(ada_end(m) + AHEAD)
            upto(end("down", 0, FSTEPS - 1) + AHEAD)
            dve.wait_ge(pieces_used, end("down", 0, FSTEPS - 1))
            for k in range(KD):
                residual(0, 1, k, lambda k, b: ps[:, 2 + k // 2, (k % 2) * N2 + b * T:(k % 2) * N2 + (b + 1) * T])
            mixer(1)

            def split_e(k, a, z):
                for i in range(a, z):
                    n, half = divmod(i, 2)
                    q = (MP0 + i) % PIECES
                    dve.wait_ge(high_ready, k * E_PIECES + (MP0 + i + 1))
                    V.tensor_tensor(low[:, q, :], ring[:, n % SLOTS, half * PIECE:(half + 1) * PIECE], high[:, q, :], ALU.subtract).then_inc(low_ready, 1)

            split_e(0, 0, AHEAD)
            dve.wait_ge(logits_done, 1)
            lg = stat[:, 32:48].rearrange("p (b e) -> p b e", b=2)
            step(V.tensor_copy(lg, ps[:, 4, 0:16].rearrange("p (b e) -> p b e", b=2)))
            for b in range(2):
                last = V.max(rt8[:, b, :], lg[:, b, :])
            step(last)
            for b in range(2):
                V.max_index(rti[:, b, :], rt8[:, b, :], lg[:, b, :])
            last = V.tensor_tensor(stat[:, 24:26], rt8[:, :, 1], rt8[:, :, 0], ALU.subtract)
            last.then_inc(top2_ready, 1)
            dve.wait_ge(top2_ready, 1)
            step(V.tensor_copy(stat[:, 48:52].rearrange("p (b j) -> p b j", b=2), rti[:, :, 0:2]))
            iota8 = cst[:, C_IOTA:C_IOTA + NE]
            for b in range(2):
                for j in range(2):
                    last = V.tensor_scalar(oh[:, j, b, :], iota8, stat[:, 48 + 2 * b + j:49 + 2 * b + j], None, ALU.is_equal)
            step(last)
            V.tensor_tensor(oh[:, 2, :, :], oh[:, 0, :, :], oh[:, 1, :, :], ALU.add).then_inc(sel_ready, 1)
            dve.wait_ge(e1_ready, 1)
            step(V.tensor_scalar(stat[:, 52:54], stat[:, 26:28], 1.0, None, ALU.add))
            step(V.reciprocal(stat[:, 52:54], stat[:, 52:54]))
            step(V.tensor_tensor(stat[:, 54:56], stat[:, 52:54], stat[:, 26:28], ALU.mult))
            for b in range(2):
                last = V.tensor_scalar(oh[:, 0, b, :], oh[:, 0, b, :], stat[:, 52 + b:53 + b], None, ALU.mult)
            step(last)
            for b in range(2):
                last = V.scalar_tensor_tensor(oh[:, 3, b, :], oh[:, 1, b, :], stat[:, 54 + b:55 + b], oh[:, 0, b, :], ALU.mult, ALU.add)
            step(last)
            dve.wait_ge(rank_done, 1)
            step(V.scalar_tensor_tensor(oh[:, 0, :, :], ps[:, 5, 0:16].rearrange("p (b e) -> p b e", b=2), 1.0, oh[:, 2, :, :], ALU.add, ALU.mult))
            step(V.tensor_scalar(oh[:, 0, :, :], oh[:, 0, :, :], -1.0, None, ALU.add))
            V.memset(stat[:, 58:59], 0.0).then_inc(eh_ready, 1)
            V.memset(stat[:, 59:60], 0.0).then_inc(eh_ready, 1)
            V.memset(stat[:, 62:63], 0.0).then_inc(ehT_ready, 1)
            dve.wait_ge(moe_zero, 1)

            def place(rnd):
                if rnd:
                    V.tensor_scalar(oh[:, 0, :, :], oh[:, 0, :, :], -128.0, None, ALU.add).then_inc(shift_ready, 1)
                    dve.wait_ge(shift_ready, rnd)
                iota = cst[:, C_IOTA:C_IOTA + 128]
                for e in range(NE):
                    for b in range(2):
                        last = V.tensor_scalar(P[:, e, b, :], iota, oh[:, 0, b, e:e + 1], None, ALU.is_equal)
                    last.then_inc(P_ready, 1)
                for e in range(NE):
                    for b in range(2):
                        last = V.tensor_scalar(Pg[:, e, b, :], iota, oh[:, 0, b, e:e + 1], oh[:, 3, b, e:e + 1], ALU.is_equal, ALU.mult)
                    last.then_inc(Pg_ready, 1)

            def take_PgT(rnd):
                dve.wait_ge(PgT_done, rnd + 1)
                for i in (2, 3):
                    last = V.tensor_copy(PgT[:, 2 * i + 1:2 * i + 3, :, :], ps[:, TURNED_BANKS[i], :].rearrange("p (e b t) -> p e b t", e=2, b=2))
                last.then_inc(PgT_last_ready, 1)

            def count_over():
                step(V.reduce_max(stat[:, 56:57], ps[:, 5, 16:16 + NE], AX.X))
                step(V.tensor_scalar(stat[:, 57:58], stat[:, 56:57], OVER_LIMIT, None, ALU.is_gt))
                V.tensor_copy(over[:, :], stat[:, 57:58]).then_inc(over_ready, 1)

            def take_xg(n):
                dve.wait_ge(xgh_ready, n)
                for q in range(2):
                    x = slice(4 * q, 4 * q + 4)
                    last = V.tensor_tensor(xg[:, 1, x, :], ps[:, 6 + q, :].rearrange("p (k t) -> p k t", k=4), xg[:, 0, x, :], ALU.subtract)
                last.then_inc(xg_ready, 1)

            def add_up(done):
                for r, bank in enumerate(COMBINE_BANKS):
                    dve.wait_ge(cmb_done, done + (r + 1))
                    a = acc[:, 2 * r:2 * r + 2, :]
                    V.tensor_tensor(a, a, ps[:, bank, :].rearrange("p (k t) -> p k t", k=2), ALU.add).then_inc(acc_ready, 1)

            def experts(rnd):
                if rnd:
                    split_e(NE * rnd, 0, AHEAD)
                place(rnd)
                if rnd == 0:
                    count_over()
                take_xg(9 * rnd + 1)
                take_PgT(rnd)
                def expert(e):
                    k = e + NE * rnd
                    done = [AHEAD]
                    more = AHEAD if not isinstance(e, int) else 0

                    def upto_e(z):
                        z = max(done[0], min(z, E_PIECES + more))
                        split_e(k, done[0], z)
                        done[0] = z

                    def take_hT(c):
                        dve.wait_ge(ehTh_ready, k * ESTEPS + (c + 1))
                        V.tensor_tensor(hTm[:, 1, :, :], ps[:, 2, :].rearrange("p (r t) -> p r t", t=128), hTm[:, 0, :, :], ALU.subtract).then_inc(ehT_ready, 1)

                    for c in range(ESTEPS):
                        if c:
                            upto_e(piece_g(c) + 4 + AHEAD)
                            take_hT(c - 1)
                        upto_e(piece_u(c) + 4 + AHEAD)
                        dve.wait_ge(pieces_used, k * E_PIECES + (MP0 + piece_u(c) + 4))
                        dve.wait_ge(esg_ready, k * ESTEPS + (c + 2))
                        V.tensor_tensor(hm[:, c % 2, :], sg[:, c % 2, :], ps[:, 1, :], ALU.mult).then_inc(eh_ready, 1)
                        if c == 0:
                            add_up(k * 4 + 4 * rnd)
                    upto_e(piece_d(ESTEPS - 2) + 4 + AHEAD)
                    take_hT(ESTEPS - 1)
                    upto_e(E_PIECES)
                    take_xg(k + (rnd + 2))
                    upto_e(E_PIECES + AHEAD)

                with dve.Fori(0, NE - 1) as e:
                    expert(e)
                expert(NE - 1)
                add_up(36 * rnd + 32)
                dve.wait_ge(acc_ready, 36 * (rnd + 1))

            experts(0)
            more = dve.value_load(over[0:1, 0:1])
            with dve.If(more > 0):
                experts(1)
            for k in range(KD):
                residual(1, 1, k, lambda k, b: acc[:, k, b * T:(b + 1) * T])
            norm_a(2 * DEPTH)
            dve.wait_ge(outT_done, 1)
            for b in range(2):
                V.tensor_copy(yout[:, b * D + 512:(b + 1) * D], ps[:, 2 + 2 * b, :]).then_inc(y_second_ready, 1)

        @block.tensor
        def _(pe):
            mm = nc.tensor.matmul

            def arrived(kind, l, j):
                n = ITEM[kind, l, j]
                pe.wait_ge(in_slot[n % SLOTS], ARRIVED[n])
                return n

            def piece(q, k):
                pe.wait_ge(low_ready, q + 1)
                return tuple(t[:, q % PIECES, :].rearrange("p (k n) -> p k n", k=k) for t in (high, low))

            pe.wait_ge(small_in, 16 * 10)
            for a, r in ((0, 128), (1, V_B_ROWS)):
                last = nc.tensor.transpose(ps[:, 0, 128 * a:128 * a + r], vrow[0:r, a, :], ident[0:r, 0:r])
            last.then_inc(vecT_done, 1)
            pe.wait_ge(x_in, 32)
            for b in range(2):
                for k in range(KD):
                    last = nc.tensor.transpose(ps[:, 1 + 2 * b + k // 4, (k % 4) * 128:(k % 4 + 1) * 128], xin[:, b, k * 128:(k + 1) * 128], ident)
            last.then_inc(xT_done, 1)
            pe.wait_ge(ones_set, 1)

            def norm(t):
                if t == 0:
                    pe.wait_ge(vecT_ready, 1)
                for k in range(KD):
                    if k % 2 == 0:
                        pe.wait_ge(sq_ready, 4 * t + k // 2 + 1)
                    last = mm(ps[:, 0, 0:N2], ones[:, :], sq[:, k, :], start=k == 0, stop=k == KD - 1)
                last.then_inc(ss_done, 1)

            pe.wait_ge(silul_ready, 1)

            def mod_rows(m):
                if m >= 2:
                    pe.wait_ge(mrow_ready, m if len(set(ADA_PLACES[ADA_PLACE[m]][1])) == 1 else m - 1)
                for q in range(4):
                    hi, lo = piece(ada_first(m) + q, 2)
                    for i in range(2):
                        for w in (hi, lo):
                            k = 2 * q + i
                            last = mm(mod_rows_of(m), silu_c[:, k, :], w[:, i, :], start=q == 0 and i == 0 and w is hi, stop=q == 3 and i == 1 and w is lo)
                    last.then_inc(pieces_used, 1)

            def turn_mod(m):
                pe.wait_ge(mrow_ready, m + 1)
                if m:
                    pe.wait_ge(mod_ready, m)
                for q in range(4):
                    last = mm(mod_turned(m)[:, 2 * q:2 * q + 2], mrow[:, m % 2, q * 128:(q + 1) * 128], cst[0:4, C_SEL:C_SEL + 2], start=True, stop=True)
                last.then_inc(modT_done, 1)

            def modulation(blocks):
                for m in blocks:
                    if m == 1:
                        norm(0)
                    mod_rows(m)
                    if m != blocks[0]:
                        turn_mod(m - 1)

            modulation(blocks_at("start", 0))
            turn_mod(blocks_at("start", 0)[-1])

            def project(out, q, x, waits=None):
                hi, lo = piece(q, KD)
                for k in range(KD):
                    if waits and k % 4 == 0:
                        pe.wait_ge(hx_ready, waits + k // 4)
                    xh, xl = hx[:, k, 0, :], hx[:, k, 1, :]
                    mm(out, hi[:, k, :], xh, start=k == 0, stop=False)
                    mm(out, hi[:, k, :], xl, start=False, stop=False)
                    last = mm(out, lo[:, k, :], xh, start=False, stop=k == KD - 1)
                last.then_inc(pieces_used, 1)

            def half_bank(bank, half):
                return ps[:, bank, half * N2:(half + 1) * N2]

            def direct(out, ws, x):
                for k, w in enumerate(ws):
                    last = mm(out, w, x[:, k, :], start=k == 0, stop=k == len(ws) - 1)
                return last

            def mixer(l):
                if l:
                    norm(2 * l)
                    mod_rows(blocks_at("norm1", l)[0])
                    pe.wait_ge(x_ready, 4 * (2 * l + 1))
                else:
                    pe.wait_ge(x_ready, 4)
                cache = slot(arrived("cache", l, 0), 3, 128)
                for m in range(3):
                    last = nc.tensor.transpose(ps[:, 3, m * 128:(m + 1) * 128], cache[:, m, :], ident)
                last.then_inc(direct_used, 1)
                if l:
                    turn_mod(blocks_at("norm1", l)[0])
                    mod_rows(blocks_at("norm1", l)[1])
                for i, (bank, half) in enumerate(((1, 0), (1, 1), (2, 0), (3, 0), (3, 1), (2, 1), (4, 0), (4, 1), (5, 0), (5, 1))):
                    if i == 3:
                        pe.wait_ge(cacheT_ready, l + 1)
                    project(half_bank(bank, half), first("in", l, 0) + i, None, (4 * l + 1) if i == 0 else None)
                    if l and i == 1:
                        turn_mod(blocks_at("norm1", l)[1])
                pe.wait_ge(sqqk_ready, l + 1)
                for m in range(KQ):
                    mm(ps[:, 1, 0:N2], ones[:, :], sqqk[:, m, :], start=m == 0, stop=m == KQ - 1)
                for m in range(KK):
                    last = mm(ps[:, 1, N2:2 * N2], ones[:, :], sqqk[:, KQ + m, :], start=m == 0, stop=m == KK - 1)
                last.then_inc(ssqk_done, 1)
                rot = cst[:, C_ROT:C_ROT + 128]
                mm(ps[:, 2, 0:T], rot, kpe_raw[:, T:], start=True, stop=True).then_inc(kpe_rot_done, 1)
                pe.wait_ge(mod_ready, blocks_at("latents", l)[0])
                modulation(blocks_at("latents", l)[:-1])
                pe.wait_ge(qkvn_ready, l + 1)
                pe.wait_ge(u_ready, l + 1)
                w0 = slot(arrived("uq", l, 0), 2, NH * (NOPE + ROPE))
                w1 = slot(arrived("uq", l, 1), 1, NH * (NOPE + ROPE))
                wq = [w0[:, 0, :], w0[:, 1, :], w1[:, 0, :]]
                for h in range(NH):
                    a = h * (NOPE + ROPE)
                    direct(half_bank(4 + h // 2, h % 2), [w[:, a:a + NOPE] for w in wq], cqT)
                for h in range(NH):
                    a, pp = h * (NOPE + ROPE) + NOPE, slice(64 * (h % 2), 64 * (h % 2) + 64)
                    last = direct(ps[pp, 3, h // 2 * N2:(h // 2 + 1) * N2], [w[:, a:a + ROPE] for w in wq], cqT)
                last.then_inc(direct_used, 1)
                turn_mod(blocks_at("latents", l)[-2])
                mod_rows(blocks_at("latents", l)[-1])
                pe.wait_ge(qraw_ready, l + 1)
                pe.wait_ge(kpe_ready, l + 1)
                q2 = qpe
                mm(ps[:, 2, 0:N2], rot, q2[:, :, T:], start=True, stop=True).then_inc(qpe_rot_done, 1)
                turn_mod(blocks_at("latents", l)[-1])
                w = slot(arrived("ukv", l, 0), KK, NH * (NOPE + VD))
                for h, b in enumerate((4, 5, 3, 1)):
                    last = direct(ps[:, b, 0:3 * 128], [w[:, k, h * 256:h * 256 + NOPE] for k in range(KK)], ckvT)
                last.then_inc(kv_done, 1)
                wv = w.rearrange("p k (h n) -> p k h n", h=NH)
                pe.wait_ge(mod_ready, blocks_at("latents", l)[-1] + 1)
                for i, b in enumerate((0, 6, 7)):
                    for k in range(KK):
                        last = mm(ps[:, b, :], ckvT[:, k, i * 128:(i + 1) * 128], wv[:, k, :, NOPE:], start=k == 0, stop=k == KK - 1)
                    last.then_inc(kv_done if i < 2 else direct_used, 1)
                pe.wait_ge(k_ready, l + 1)
                pe.wait_ge(v_ready, l + 1)
                pe.wait_ge(qpe_ready, l + 1)
                for h in range(NH):
                    pp = slice(64 * (h % 2), 64 * (h % 2) + 64)
                    for b, (a, z) in enumerate(((0, T), (T, 3 * T))):
                        mm(ps[:, 4 + h, a:z], qT[:, h, b * T:(b + 1) * T], kT[:, h, a:z], start=True, stop=False)
                        last = mm(ps[:, 4 + h, a:z], q2[pp, h // 2, b * T:(b + 1) * T], kpeT[pp, a:z], start=False, stop=True)
                last.then_inc(s_done, 1)
                modulation(blocks_at("softmax", l))
                turn_mod(blocks_at("softmax", l)[-1])
                pe.wait_ge(p_ready, l + 1)
                pe.wait_ge(pool_ready, l + 1)
                wp = slot(arrived("pool", l, 0), NG, 128)
                for g in range(NG):
                    last = mm(half_bank(6 + g // 2, g % 2), wp[:, g, :], poolT[:, g, :], start=True, stop=True)
                last.then_inc(direct_used, 1)
                pe.wait_ge(pn_ready, l + 1)
                pe.wait_ge(mod_ready, blocks_at("softmax", l)[-1] + 1)
                for h, b in enumerate((1, 2, 3, 0)):
                    for i in range(3):
                        last = nc.tensor.transpose(ps[:, b, i * 128:(i + 1) * 128], p[:, h, i * 128:(i + 1) * 128], ident)
                last.then_inc(pT_done, 1)
                pe.wait_ge(pT_low_ready, l + 1)
                pe.wait_ge(pT_high_ready, l + 1)
                for h in range(NH):
                    o = half_bank(4 + h // 2, h % 2)
                    vh = slice(h * VD, (h + 1) * VD)
                    mm(o[:, 0:T], v[:, 0, vh], pT[:, h, 0:128], start=True, stop=True)
                    mm(o[:, T:], v[:, 1, vh], pT[:, h, 128:256], start=True, stop=False)
                    last = mm(o[:, T:], v[:, 2, vh], pT[:, h, 256:384], start=False, stop=True)
                last.then_inc(o_done, 1)
                pe.wait_ge(pooledl_ready, l + 1)
                pe.wait_ge(ol_ready, l + 1)
                for m in range(KD):
                    if m == 4:
                        modulation(blocks_at("out", l))
                    project(half_bank(m // 2, m % 2), first("out", l, m // 2) + m % 2, None)
                turn_mod(blocks_at("out", l)[-1])
                for m in range(KK):
                    nc.tensor.transpose(ps[:, 4, m * 128:(m + 1) * 128], ckvT[:, m, 0:T], ident)
                nc.tensor.transpose(ps[:, 4, KL:KL + ROPE], kpe_raw[0:ROPE, 0:T], ident[0:ROPE, 0:ROPE]).then_inc(kv_outT_done, 1)
                norm(2 * l + 1)
                mod_rows(blocks_at("norm2", l)[0])
                mod_rows(blocks_at("norm2", l)[1])
                turn_mod(blocks_at("norm2", l)[0])
                if l:
                    turn_mod(blocks_at("norm2", l)[-1])

            mixer(0)
            pe.wait_ge(kv_out_ready, 1)

            def ffn_down(c):
                pe.wait_ge(fx_ready, c + 1)
                for k in range(FC // 128):
                    hi, lo = piece(first("down", 0, c) + k, 1)
                    xh, xl = fx[:, c % 2, k, 0, :], fx[:, c % 2, k, 1, :]
                    for m in range(KD):
                        o = half_bank(2 + m // 2, m % 2)
                        a, z = c == 0 and k == 0 and m % 2 == 0, c == FSTEPS - 1 and k == FC // 128 - 1
                        mc = slice(m * 128, (m + 1) * 128)
                        mm(o, hi[:, 0, mc], xh, start=a, stop=False, skip_group_check=True)
                        mm(o, hi[:, 0, mc], xl, start=False, stop=False, skip_group_check=True)
                        last = mm(o, lo[:, 0, mc], xh, start=False, stop=z, skip_group_check=True)
                    last.then_inc(pieces_used, 1)

            for c in range(FSTEPS):
                for w, kind in enumerate(("gate", "up")):
                    if c:
                        pe.wait_ge((fsg_ready, fh_ready)[w], c)
                    for m in range(2):
                        project(half_bank(w, m), first(kind, 0, c) + m, None, 3 if c == 0 and w == 0 and m == 0 else None)
                    if c == 0 and w == 0:
                        turn_mod(blocks_at("norm2", 0)[-1])
                if c == 1:
                    pe.wait_ge(mod_ready, blocks_at("norm2", 0)[-1] + 1)
                if c:
                    ffn_down(c - 1)
                    for m in blocks_at("ffn", c - 1):
                        turn_mod(m)
                modulation(blocks_at("ffn", c))
            ffn_down(FSTEPS - 1)
            mixer(1)
            pe.wait_ge(h_ready, 4)
            pe.wait_ge(h_last_ready, 4)
            pe.wait_ge(router_in, 16)

            pe.wait_ge(kv_out_ready, 2)
            for b in range(2):
                for k in range(KD):
                    last = mm(ps[:, 4, b * NE:(b + 1) * NE], hT[:, k, b * T:(b + 1) * T], wr[:, k, :], start=k == 0, stop=k == KD - 1)
            last.then_inc(logits_done, 1)
            for b in range(2):
                for k in range(KD):
                    last = nc.tensor.transpose(ps[:, 2 * b + k // 4, (k % 4) * 128:(k % 4 + 1) * 128], hT[:, k, b * T:(b + 1) * T], ident)
            last.then_inc(h2T_done, 1)
            pe.wait_ge(sel_ready, 1)
            tri = cst[:, C_TRI:C_TRI + 128]
            mm(ps[:, 5, 0:NE], tri, oh[:, 2, 0, :], start=True, stop=True)
            mm(ps[:, 5, NE:2 * NE], tri, oh[:, 2, 1, :], start=True, stop=False)
            mm(ps[:, 5, NE:2 * NE], ones[:, :], oh[:, 2, 0, :], start=False, stop=True)
            for b in range(2):
                last = mm(ps[:, 5, 2 * NE:3 * NE], ones[:, :], oh[:, 2, b, :], start=b == 0, stop=b == 1)
            last.then_inc(rank_done, 1)


            def gather(e):
                for m in range(KD):
                    for b in range(2):
                        rhs = P[:, e, b, :] if isinstance(e, int) else P[:, bass.ds(e, 1), b, :].rearrange("p o t -> p (o t)")
                        last = mm(ps[:, 6 + m // 4, (m % 4) * 128:(m % 4 + 1) * 128], h2[:, b, m * 128:(m + 1) * 128], rhs, start=b == 0, stop=b == 1)
                last.then_inc(gat_done, 1)

            def combine(e):
                for r, bank in enumerate(COMBINE_BANKS):
                    for q in range(2):
                        m = 2 * r + q
                        rhs = PgT[:, e, :, :] if isinstance(e, int) else PgT[:, bass.ds(e, 1), :, :].rearrange("p o b t -> p (o b) t")
                        last = mm(half_bank(bank, q), Y[:, m * 128:(m + 1) * 128], rhs, start=True, stop=True)
                    last.then_inc(cmb_done, 1)

            def experts(rnd):
                pe.wait_ge(h2_ready, 1)
                pe.wait_ge(moe_zero, 1)
                if rnd:
                    pe.wait_ge(acc_ready, 36 * rnd)
                pe.wait_ge(P_ready, NE * rnd + 1)
                gather(0)
                pe.wait_ge(over_ready, 1)
                for e in range(NE):
                    pe.wait_ge(Pg_ready, NE * rnd + e + 1)
                    for b in range(2):
                        c = (2 * (e % 2) + b) * 128
                        last = nc.tensor.transpose(ps[:, TURNED_BANKS[e // 2], c:c + 128], Pg[:, e, b, :], ident)
                last.then_inc(PgT_done, 1)
                with pe.Fori(0, NE) as e:
                    k = e + NE * rnd

                    def piece_e(i, kk):
                        pe.wait_ge(low_ready, k * E_PIECES + (MP0 + i + 1))
                        return tuple(t[:, (MP0 + i) % PIECES, :].rearrange("p (k n) -> p k n", k=kk) for t in (high, low))

                    def into_hidden(bank, i):
                        for q in range(4):
                            hi, lo = piece_e(i + q, 2)
                            for j in range(2):
                                kk = 2 * q + j
                                xh, xl = xg[:, 0, kk, :], xg[:, 1, kk, :]
                                mm(ps[:, bank, :], xh, hi[:, j, :], start=kk == 0, stop=False)
                                mm(ps[:, bank, :], xh, lo[:, j, :], start=False, stop=False)
                                last = mm(ps[:, bank, :], xl, hi[:, j, :], start=False, stop=kk == KD - 1)
                            last.then_inc(pieces_used, 1)

                    def turn(c):
                        pe.wait_ge(eh_ready, k * ESTEPS + (c + 3))
                        pe.wait_ge(ehT_ready, k * ESTEPS + (c + 1))
                        for r in range(EC // 128):
                            last = nc.tensor.transpose(ps[:, 2, r * 128:(r + 1) * 128], hm[:, c % 2, r:EC:EC // 128], ident)
                        last.then_inc(ehT_done, 1)

                    def down(c):
                        pe.wait_ge(ehT_ready, k * ESTEPS + (c + 2))
                        for r in range(EC // 128):
                            hi, lo = piece_e(piece_d(c) + r, 1)
                            xh, xl = hTm[:, 0, r, :], hTm[:, 1, r, :]
                            a, z = c == 0 and r == 0, c == ESTEPS - 1 and r == EC // 128 - 1
                            for half in range(2):
                                o, n = ps[:, 4 + half, :], slice(half * 512, (half + 1) * 512)
                                mm(o, xh, hi[:, 0, n], start=a, stop=False)
                                mm(o, xh, lo[:, 0, n], start=False, stop=False)
                                last = mm(o, xl, hi[:, 0, n], start=False, stop=z)
                            last.then_inc(pieces_used, 1)

                    pe.wait_ge(xg_ready, k + (rnd + 1))
                    for c in range(ESTEPS):
                        pe.wait_ge(esg_ready, k * ESTEPS + (c + 1))
                        into_hidden(0, piece_g(c))
                        if c == 1:
                            pe.wait_ge(acc_ready, k * 4 + (4 * rnd + 4))
                        if c:
                            turn(c - 1)
                        pe.wait_ge(eh_ready, k * ESTEPS + (c + 2))
                        into_hidden(1, piece_u(c))
                        if c:
                            down(c - 1)
                        else:
                            pe.wait_ge(Y_ready, k + (rnd + 1))
                            pe.wait_ge(PgT_first_ready, rnd + 1)
                            pe.wait_ge(PgT_last_ready, rnd + 1)
                            combine(e)
                    turn(ESTEPS - 1)
                    pe.wait_ge(acc_ready, k * 4 + (4 * rnd + 4))
                    gather(e + 1)
                    down(ESTEPS - 1)
                pe.wait_ge(Y_ready, 9 * (rnd + 1))
                pe.wait_ge(xg_ready, 9 * (rnd + 1))
                combine(NE)

            experts(0)
            pe.wait_ge(over_ready, 1)
            more = pe.value_load(over[0:1, 0:1])
            with pe.If(more > 0):
                experts(1)
            norm(2 * DEPTH)
            for k in range(KD):
                pe.wait_ge(h_ready, 2 * DEPTH + k + 1)
                for b in range(2):
                    last = nc.tensor.transpose(ps[:, 1 + 2 * b + k // 4, (k % 4) * 128:(k % 4 + 1) * 128], hT[:, k, b * T:(b + 1) * T], ident)
            last.then_inc(outT_done, 1)


OVER_LIMIT = 128.0
_INS = ["x_prompt", "x_sample", "c", "cache_ckv", "cache_kpe", "c_ctx", "norm1_g", "norm2_g", "w_ada", "b_ada", "w_in",
        "q_norm_g", "kv_norm_g", "w_uq", "w_ukv", "w_pool", "pool_scale", "w_out", "ffn_w_gate", "ffn_w_up", "ffn_w_down",
        "moe_w_router", "moe_w_gate", "moe_w_up", "moe_w_down", "final_norm_g"]
_OUTS = [(1, T, D), (1, T, D), (1, DEPTH, T, KL), (1, DEPTH, T, ROPE)]


def kernel(**inputs):
    import concourse.bacc as _bacc
    from concourse.bass_utils import run_bass_kernel_spmd as _run

    nc = _bacc.Bacc("TRN2", target_bir_lowering=False, num_devices=1)
    f32 = mybir.dt.float32
    arrays, aps = {}, {}
    for name in _INS:
        a = np.ascontiguousarray(inputs[name])
        arrays[f"in_{name}"] = a
        aps[name] = nc.dram_tensor(f"in_{name}", a.shape, f32, kind="ExternalInput").ap()
    arrays["in_constants"] = constants()
    consts = nc.dram_tensor("in_constants", (128, C_COLS), f32, kind="ExternalInput").ap()
    outs = [nc.dram_tensor(f"out_{i}", s, f32, kind="ExternalOutput").ap() for i, s in enumerate(_OUTS)]
    program(nc, aps, consts, outs[0].rearrange("b t d -> (b t) d"), outs[1].rearrange("b t d -> (b t) d"), outs[2], outs[3])
    r = _run(nc, [arrays], core_ids=[0])
    return tuple(r.results[0][f"out_{i}"] for i in range(len(_OUTS)))
```
